# Optimizing a Trainium2 kernel written in Bass

```python
import math
import jax, jax.numpy as jnp
from jax import lax
import numpy as np

D_MODEL = 1024
BATCH = 1
SEQ = 1024
DEPTH = 1
DEC_BATCH = 8
DEC_SEQ = 4
PAST_LEN = 256
PAGE_SIZE = 128

N_META = 16
ATT_WIDTH = D_MODEL // 2
POOL_WIDTH = D_MODEL - ATT_WIDTH
N_ATT_HEADS = 4
HEAD_DIM = ATT_WIDTH // N_ATT_HEADS
QK_DIM = HEAD_DIM // 2
ROPE_DIM = QK_DIM // 4
ROPE_THETA = 500000.0
POOL_WINDOWS = (2, 4, 8, 16)
N_POOL_GROUPS = len(POOL_WINDOWS)
POOL_GROUP_DIM = POOL_WIDTH // N_POOL_GROUPS
POOL_STATE = max(POOL_WINDOWS) - 1
IN_WIDTH = 3 * ATT_WIDTH + POOL_WIDTH
N_KEYS = 128
N_EXPERTS = N_KEYS * N_KEYS
PEER_HEADS = 8
PEER_QDIM = 256
PEER_HALF = PEER_QDIM // 2
PEER_TOPK = 16
PEER_BLOCK = 128
Q_BLOCK = 128
EPS = 1e-6
NEG = -1e30

kernel_name = 'hymba_diffattn_pool_peer_step'

def rmsnorm(x, g):
    xf = x.astype(jnp.float32)
    y = xf * lax.rsqrt(jnp.mean(xf * xf, axis=-1, keepdims=True) + EPS)
    return (y * g.astype(jnp.float32)).astype(x.dtype)

def rope(x, pos):
    inv = ROPE_THETA ** (-jnp.arange(0, ROPE_DIM, 2, dtype=jnp.float32) / ROPE_DIM)
    ang = pos.astype(jnp.float32)[:, None] * inv[None, :]
    cos = jnp.cos(ang)[:, None, None, :]
    sin = jnp.sin(ang)[:, None, None, :]
    xr = x[..., :ROPE_DIM].astype(jnp.float32)
    x1, x2 = xr[..., :ROPE_DIM // 2], xr[..., ROPE_DIM // 2:]
    rot = jnp.concatenate([x1 * cos - x2 * sin, x2 * cos + x1 * sin], axis=-1)
    return jnp.concatenate([rot.astype(x.dtype), x[..., ROPE_DIM:]], axis=-1)

def diff_attn(q, k, v, q_pos, k_pos, lam):
    s = jnp.einsum('bqhcd,bkhcd->bchqk', q, k).astype(jnp.float32) * (QK_DIM ** -0.5)
    mask = k_pos[None, :] <= q_pos[:, None]
    s = jnp.where(mask, s, NEG)
    p = jax.nn.softmax(s, axis=-1)
    a = p[:, 0] - lam * p[:, 1]
    return jnp.einsum('bhqk,bkhd->bqhd', a.astype(v.dtype), v)

def attn_blocks(q, k, v, pos, lam):
    B, T = q.shape[0], q.shape[1]
    nb = -(-T // Q_BLOCK)
    tp = nb * Q_BLOCK
    qp = jnp.pad(q, ((0, 0), (0, tp - T), (0, 0), (0, 0), (0, 0)))
    qpos = jnp.arange(tp)

    def blk(i):
        st = i * Q_BLOCK
        qb = lax.dynamic_slice_in_dim(qp, st, Q_BLOCK, axis=1)
        pb = lax.dynamic_slice_in_dim(qpos, st, Q_BLOCK)
        return diff_attn(qb, k, v, pb, pos, lam)

    o = lax.map(blk, jnp.arange(nb))
    o = jnp.moveaxis(o, 0, 1).reshape(B, tp, N_ATT_HEADS, HEAD_DIM)
    return o[:, :T]

def pool_mix(p, prev, pos, w_pool, b_pool, pool_scale):
    B, T, _ = p.shape
    ext = jnp.concatenate([prev.astype(p.dtype), p], axis=1)
    cz = jnp.pad(jnp.cumsum(ext.astype(jnp.float32), axis=1), ((0, 0), (1, 0), (0, 0)))
    means = []
    for g, w in enumerate(POOL_WINDOWS):
        c0, c1 = g * POOL_GROUP_DIM, (g + 1) * POOL_GROUP_DIM
        tot = cz[:, POOL_STATE + 1:POOL_STATE + 1 + T, c0:c1] - cz[:, POOL_STATE + 1 - w:POOL_STATE + 1 - w + T, c0:c1]
        cnt = jnp.minimum(pos + 1, w).astype(jnp.float32)[None, :, None]
        means.append(tot / cnt)
    d = (jnp.concatenate(means, axis=-1) - p.astype(jnp.float32)).astype(p.dtype)
    d = d.reshape(B, T, N_POOL_GROUPS, POOL_GROUP_DIM)
    y = jnp.einsum('btgc,gcd->btgd', d, w_pool) + b_pool
    y = y.reshape(B, T, POOL_WIDTH) * pool_scale
    return y, ext[:, -POOL_STATE:]

def peer(x, w_query, sub_keys, w_u, w_v):
    B, T, D = x.shape
    n = B * T
    nb = -(-n // PEER_BLOCK)
    xf = jnp.pad(x.reshape(n, D), ((0, nb * PEER_BLOCK - n), (0, 0))).reshape(nb, PEER_BLOCK, D)

    def blk(xb):
        q = (xb @ w_query).reshape(PEER_BLOCK, PEER_HEADS, 2, PEER_HALF)
        s = jnp.einsum('thcd,hcnd->thcn', q, sub_keys).astype(jnp.float32)
        sv, si = lax.top_k(s, PEER_TOPK)
        cand = (sv[:, :, 0, :, None] + sv[:, :, 1, None, :]).reshape(PEER_BLOCK, PEER_HEADS, PEER_TOPK * PEER_TOPK)
        cidx = (si[:, :, 0, :, None] * N_KEYS + si[:, :, 1, None, :]).reshape(PEER_BLOCK, PEER_HEADS, PEER_TOPK * PEER_TOPK)
        top, sel = lax.top_k(cand, PEER_TOPK)
        eidx = jnp.take_along_axis(cidx, sel, axis=-1)
        gate = jax.nn.softmax(top, axis=-1)
        a = jnp.einsum('td,thkd->thk', xb, w_u[eidx])
        a = jax.nn.gelu(a.astype(jnp.float32), approximate=False) * gate
        return jnp.einsum('thk,thkd->td', a.astype(xb.dtype), w_v[eidx])

    y = lax.map(blk, xf).reshape(nb * PEER_BLOCK, D)[:n]
    return y.reshape(B, T, D)

def hybrid_layer(x, pos, pool_prev, past_k, past_v, lam, lam_init, norm1_g, w_in, q_norm_g, k_norm_g,
                 subln_g, w_pool, b_pool, pool_scale, w_out, norm2_g, w_query, sub_keys, w_u, w_v):
    B, T, _ = x.shape
    h = rmsnorm(x, norm1_g)
    z = h @ w_in
    q, k, v, p = jnp.split(z, [ATT_WIDTH, 2 * ATT_WIDTH, 3 * ATT_WIDTH], axis=-1)
    q = rope(rmsnorm(q.reshape(B, T, N_ATT_HEADS, 2, QK_DIM), q_norm_g), pos)
    k = rope(rmsnorm(k.reshape(B, T, N_ATT_HEADS, 2, QK_DIM), k_norm_g), pos)
    v = v.reshape(B, T, N_ATT_HEADS, HEAD_DIM)
    if past_k is None:
        att = attn_blocks(q, k, v, pos, lam)
    else:
        n_past = past_k.shape[1]
        k_all = jnp.concatenate([past_k.astype(k.dtype), k], axis=1)
        v_all = jnp.concatenate([past_v.astype(v.dtype), v], axis=1)
        att = diff_attn(q, k_all, v_all, pos, jnp.arange(n_past + T), lam)
    att = rmsnorm(att, subln_g) * (1.0 - lam_init)
    pool_y, pool_new = pool_mix(p, pool_prev, pos, w_pool, b_pool, pool_scale)
    x = x + jnp.concatenate([att.reshape(B, T, ATT_WIDTH), pool_y], axis=-1) @ w_out
    x = x + peer(rmsnorm(x, norm2_g), w_query, sub_keys, w_u, w_v)
    return x, k.reshape(B, T, N_ATT_HEADS, 2 * QK_DIM), v, pool_new

def setup_inputs(seed: int = 0) -> dict:
    key = jax.random.key(seed)
    ks = jax.random.split(key, 26)
    f32 = jnp.float32
    n_pages = PAST_LEN // PAGE_SIZE
    n_pool = (DEC_BATCH * n_pages * 5) // 4
    nrm = lambda k, s, sc: jax.random.normal(k, s, f32) * sc
    gain = lambda k, s: 1.0 + 0.05 * jax.random.normal(k, s, f32)
    perm = jax.random.permutation(ks[5], n_pool)[:DEC_BATCH * n_pages]
    return {
        'x_prompt': nrm(ks[0], (BATCH, SEQ, D_MODEL), 1.0),
        'x_sample': nrm(ks[1], (DEC_BATCH, DEC_SEQ, D_MODEL), 1.0),
        'cache_k': nrm(ks[2], (DEPTH, n_pool, PAGE_SIZE, N_ATT_HEADS, 2 * QK_DIM), 1.0),
        'cache_v': nrm(ks[3], (DEPTH, n_pool, PAGE_SIZE, N_ATT_HEADS, HEAD_DIM), 1.0),
        'state_pool': nrm(ks[4], (DEPTH, DEC_BATCH, POOL_STATE, POOL_WIDTH), 1.0),
        'page_table': perm.reshape(DEC_BATCH, n_pages).astype(jnp.int32),
        'meta_tokens': nrm(ks[6], (N_META, D_MODEL), 1.0),
        'norm1_g': gain(ks[7], (DEPTH, D_MODEL)),
        'w_in': nrm(ks[8], (DEPTH, D_MODEL, IN_WIDTH), D_MODEL ** -0.5),
        'q_norm_g': gain(ks[9], (DEPTH, QK_DIM)),
        'k_norm_g': gain(ks[10], (DEPTH, QK_DIM)),
        'lambda_q1': nrm(ks[11], (DEPTH, QK_DIM), 0.1),
        'lambda_k1': nrm(ks[12], (DEPTH, QK_DIM), 0.1),
        'lambda_q2': nrm(ks[13], (DEPTH, QK_DIM), 0.1),
        'lambda_k2': nrm(ks[14], (DEPTH, QK_DIM), 0.1),
        'subln_g': gain(ks[15], (DEPTH, HEAD_DIM)),
        'w_pool': nrm(ks[16], (DEPTH, N_POOL_GROUPS, POOL_GROUP_DIM, POOL_GROUP_DIM), POOL_GROUP_DIM ** -0.5),
        'b_pool': nrm(ks[17], (DEPTH, N_POOL_GROUPS, POOL_GROUP_DIM), 0.02),
        'pool_scale': gain(ks[18], (DEPTH, POOL_WIDTH)),
        'w_out': nrm(ks[19], (DEPTH, D_MODEL, D_MODEL), D_MODEL ** -0.5),
        'norm2_g': gain(ks[20], (DEPTH, D_MODEL)),
        'w_query': nrm(ks[21], (DEPTH, D_MODEL, PEER_HEADS * PEER_QDIM), D_MODEL ** -0.5),
        'sub_keys': nrm(ks[22], (DEPTH, PEER_HEADS, 2, N_KEYS, PEER_HALF), PEER_HALF ** -0.5),
        'w_u': nrm(ks[23], (DEPTH, N_EXPERTS, D_MODEL), D_MODEL ** -0.5),
        'w_v': nrm(ks[24], (DEPTH, N_EXPERTS, D_MODEL), 0.3),
    }

def reference(x_prompt, x_sample, cache_k, cache_v, state_pool, page_table, meta_tokens, norm1_g, w_in,
              q_norm_g, k_norm_g, lambda_q1, lambda_k1, lambda_q2, lambda_k2, subln_g, w_pool, b_pool,
              pool_scale, w_out, norm2_g, w_query, sub_keys, w_u, w_v):
    B = x_prompt.shape[0]
    DB, S = x_sample.shape[0], x_sample.shape[1]
    n_past = page_table.shape[1] * PAGE_SIZE
    xp = jnp.concatenate([jnp.broadcast_to(meta_tokens[None].astype(x_prompt.dtype), (B, N_META, D_MODEL)), x_prompt], axis=1)
    xs = x_sample
    pos_p = jnp.arange(xp.shape[1])
    pos_s = n_past + jnp.arange(S)
    pk, pv, pp, sk, sv, sp = [], [], [], [], [], []
    for l in range(DEPTH):
        lam_init = 0.8 - 0.6 * math.exp(-0.3 * l)
        lam = (jnp.exp(jnp.sum(lambda_q1[l].astype(jnp.float32) * lambda_k1[l].astype(jnp.float32)))
               - jnp.exp(jnp.sum(lambda_q2[l].astype(jnp.float32) * lambda_k2[l].astype(jnp.float32))) + lam_init)
        w = (norm1_g[l], w_in[l], q_norm_g[l], k_norm_g[l], subln_g[l], w_pool[l], b_pool[l], pool_scale[l],
             w_out[l], norm2_g[l], w_query[l], sub_keys[l], w_u[l], w_v[l])
        zero_prev = jnp.zeros((B, POOL_STATE, POOL_WIDTH), xp.dtype)
        xp, k_new, v_new, pool_new = hybrid_layer(xp, pos_p, zero_prev, None, None, lam, lam_init, *w)
        pk.append(k_new); pv.append(v_new); pp.append(pool_new)
        past_k = cache_k[l][page_table].reshape(DB, n_past, N_ATT_HEADS, 2, QK_DIM)
        past_v = cache_v[l][page_table].reshape(DB, n_past, N_ATT_HEADS, HEAD_DIM)
        xs, k_new, v_new, pool_new = hybrid_layer(xs, pos_s, state_pool[l], past_k, past_v, lam, lam_init, *w)
        sk.append(k_new); sv.append(v_new); sp.append(pool_new)
    y_prompt = xp[:, N_META:]
    y_sample = xs
    return (y_prompt, y_sample, jnp.stack(pk, 0), jnp.stack(pv, 0), jnp.stack(pp, 0),
            jnp.stack(sk, 0), jnp.stack(sv, 0), jnp.stack(sp, 0))


_drawn_inputs = setup_inputs


def setup_inputs(seed=0):
    import zlib

    import numpy as np

    out = dict(_drawn_inputs(seed))
    spreads = {}
    factors = {'b_pool': 3.407}
    for name, (base, spread) in spreads.items():
        noise = np.random.default_rng([zlib.crc32(name.encode()), seed]).standard_normal(out[name].shape)
        drawn = base * np.exp(spread * noise) if base else spread * noise
        out[name] = __import__('jax').numpy.asarray(drawn.astype(out[name].dtype))
    for name, factor in factors.items():
        out[name] = (out[name] * factor).astype(out[name].dtype)
    return out
```

```python
import math
from contextlib import ExitStack

import concourse.bass as bass
from concourse import mybir
import numpy as np

F32 = mybir.dt.float32
BF16 = mybir.dt.bfloat16
I32 = mybir.dt.int32
U32 = mybir.dt.uint32
ALU = mybir.AluOpType
ACT = mybir.ActivationFunctionType
AX = mybir.AxisListType

P = 128
D = 1024
DC = D // P
ATT = 512
HEADS = 4
QK = 64
ROPE = QK // 4
HALF = ROPE // 2
INW = 3 * ATT + 512
META = 16
SEQ = 1024
SEQS = 8
NEW = 4
PAST = 256
PAGE = 128
PAGES = PAST // PAGE
TILES = 9
LAST = TILES - 1
TAIL = META + SEQ - LAST * P
ROWS8 = TAIL + SEQS * NEW
KEYS = LAST * P
KTW = KEYS + ROWS8
WINDOWS = (2, 4, 8, 16)
STATE = 15
PH = 8
NK = 128
TOPK = 16
GROUPS = 2 * PH
PICKS = PH * TOPK
NEXP = NK * NK
EPS = 1e-6
NEG = -1e30
LAM_INIT = 0.8 - 0.6 * math.exp(-0.3 * 0)
SLOTS = 4
GRP = 4
SW = PAST + ROWS8

HEAD0, HEADW = 1, 6
SAMP0, SAMPW = 27, 20


def after_attention(last):
    return SAMP0 + 2 * SAMPW if last else HEAD0 + HEADW * HEADS + 1


class Counter:

    def __init__(self, eng):
        self.eng, self.count = eng, {}

    def __call__(self, sem, more=1):
        self.count[sem] = self.count.get(sem, 0) + more
        return self.count[sem]

    def settle(self):
        for sem, n in self.count.items():
            self.eng.sem_inc(sem, -n)
        self.count = {}


def build(nc, x, xT, g1T, w_in, gqk, cs, mt, mst, state, w_pool, b_poolT, scaleT, wqT, skT, g2T, g2b, lams,
          rows01, w_out, subT, mask, mext, msam, ktc, vc, pages, wuv, iota,
          y_all, k_all, v_all, p_last, state_old):
    with ExitStack() as ctx:
        def sb(name, n, dt=F32):
            return ctx.enter_context(nc.sbuf_tensor(name, [P, n], dt))

        def pb(name, n):
            return ctx.enter_context(nc.psum_tensor(name, [P, n], F32))

        def sem(name):
            return ctx.enter_context(nc.semaphore(name))

        qp_dram = nc.dram_tensor("qp_dram", [TILES, P, 1024], F32).ap()

        big1 = sb("big1", 16384)
        big2 = sb("big2", 16384)
        KT = sb("KT", HEADS * KTW)
        V = sb("V", TILES * ATT)
        work = sb("work", 4096)
        x1c = sb("x1c", D)
        h2c = sb("h2c", D)
        g2w = sb("g2w", D)
        maskw = sb("maskw", 512)
        qpw = sb("qpw", 1024)
        att = sb("att", ATT)
        ext = sb("ext", 2 * ROWS8 + P)
        emask = sb("emask", ROWS8)
        ident = sb("ident", P)
        diag = sb("diag", SLOTS * P)
        idx_n = sb("idx_n", PICKS, I32)
        idx_c = sb("idx_c", PICKS, I32)
        gate_n = sb("gate_n", PICKS)
        gate_c = sb("gate_c", PICKS)
        dots = sb("dots", SLOTS)
        gel = sb("gel", SLOTS)
        amp = sb("amp", SLOTS)
        iota16 = sb("iota16", TOPK)
        sm = sb("sm", P)
        pt = sb("pt", SEQS * PAGES, I32)

        w_in_sb = big1[:, :].rearrange("p (c n) -> p c n", c=DC)
        wqT_sb = big1[:, :].rearrange("p (j n) -> p j n", j=GROUPS)
        w_out_sb = big1[:, 0:8192].rearrange("p (c n) -> p c n", c=DC)
        ring = big1[:, 8192:16384].rearrange("p (s n) -> p s n", s=SLOTS)
        w_route = big2[:, :].rearrange("p (c n) -> p c n", c=DC)
        KT3 = KT[:, :].rearrange("p (h n) -> p h n", h=HEADS)
        V3 = V[:, :].rearrange("p (t n) -> p t n", t=TILES)

        def part(lo, n):
            return big2[:, lo:lo + n]
        hxT = [part(0, 1024), part(1024, 1024)]
        hx = [part(2048, 1024), part(3072, 1024)]
        hqk = [part(4096, 1024), part(5120, 1024)]
        hsq = part(6144, 1024)
        hgqk = part(7168, 1024)
        hp = [part(8192, 512), part(8704, 512)]
        hdT = part(9216, 512)
        hqp = [part(9728, 1024), part(10752, 1024)]
        hmt = [part(11776, 1024), part(12800, 1024)]
        hcs = [part(13824, ROPE), part(13840, ROPE)]
        hwp = part(13856, 512)
        hst = part(14368, 512)
        hmst = part(14880, 512)
        hrope = part(15392, 512)
        hg1 = part(15904, DC)

        e0, e1, aT, x1n = (work[:, a:a + 1024] for a in (0, 1024, 2048, 3072))
        scores = work[:, 0:2048].rearrange("p (g n) -> p g n", g=GROUPS)
        cand = work[:, 0:2048].rearrange("p (h n) -> p h n", h=PH)
        onehot = work[:, 0:2048].rearrange("p (h k j) -> p h k j", h=PH, k=TOPK)
        skT_sb = work[:, 0:2048].rearrange("p (j n) -> p j n", j=GROUPS)
        qT = qpw[:, 0:512].rearrange("p (h n) -> p h n", h=HEADS)
        pyT = qpw[:, 512:1024].rearrange("p (g n) -> p g n", g=HEADS)
        sv = qpw[:, 0:256].rearrange("p (g k) -> p g k", g=GROUPS)
        si = qpw[:, 256:512].bitcast(U32).rearrange("p (g k) -> p g k", g=GROUPS)
        sif = qpw[:, 512:768].rearrange("p (g k) -> p g k", g=GROUPS)
        tv = qpw[:, 768:896].rearrange("p (h k) -> p h k", h=PH)
        tpos = qpw[:, 896:1024].bitcast(U32).rearrange("p (h k) -> p h k", h=PH)
        mask_sb = maskw[:, :].bitcast(BF16)
        posa, posb, pick1, pick2 = (maskw[:, a:a + PICKS] for a in (0, 128, 256, 384))
        ex0, ex1, exT = ext[:, 0:ROWS8], ext[:, ROWS8:2 * ROWS8], ext[:, 2 * ROWS8:]
        Kb = work[:, 0:1024].rearrange("p (g h n) -> p g h n", g=PAGES, h=HEADS)
        Vb = work[:, 0:1024].rearrange("p (g n) -> p g n", g=PAGES)
        Ps = work[:, 1024:1024 + SW]
        PT = work[:, 1536:1536 + 3 * P].rearrange("p (k n) -> p k n", k=3)
        QZ = work[:, 2048:2048 + P * (1 + HEADS)]
        AZ = work[:, 2048:2048 + P * (1 + 3 * HEADS)]
        msam_sb = maskw[:, 0:SW]

        def col(i, n=1):
            return sm[:, i:i + n]
        ss1, rs1, ss16, rs16 = col(0), col(1), col(4, 16), col(20, 16)
        eps = col(36)
        coef = col(38, 4)
        nmx = col(42, 4)
        sums = col(46, 4)
        rc = col(50, 2)
        ss4, rs4 = col(52, 4), col(56, 4)
        ss2, rs2, r2 = col(60), col(61), col(62)
        gsum, grec = col(64, 8), col(72, 8)
        snm, ssum, src, scoef = col(80), col(81), col(82), col(83)
        lamt = col(84, 4)
        bpT, scT, g2c, subc, r01 = col(88, 4), col(92, 4), col(96, 8), col(104), col(106, 3)
        nm = col(110, 2)

        Y = pb("Y", 1024)
        S0 = pb("S0", 1024)
        S1 = pb("S1", 1024)
        T = pb("T", 512)
        O = pb("O", 512)
        S = [S0, S1]
        zbank = [Y[:, 0:512], Y[:, 512:1024], S0[:, 0:512], S0[:, 512:1024]]
        qTp, kTp = S1[:, 0:512], S1[:, 512:1024]
        dTp, pyp = T[:, :], O[:, :]
        route_bank = [S0[:, 0:512], S0[:, 512:1024], S1[:, 0:512], S1[:, 512:1024]]

        pe_own, act_own, dve_own, pool_own = sem("pe_own"), sem("act_own"), sem("dve_own"), sem("pool_own")
        c_w_in = [sem(f"c_w_in{c}") for c in range(DC)]
        c_act = sem("c_act")
        c_dve = sem("c_dve")
        c_pool = sem("c_pool")
        c_pe = sem("c_pe")
        c_sp = sem("c_sp")
        ident_pe, ident_act = sem("ident_pe"), sem("ident_act")
        eps_ready = sem("eps_ready")
        p0_ready = sem("p0_ready")
        x_in = [sem("x_in0"), sem("x_in1")]
        xT_in = [sem("xT_in0"), sem("xT_in1")]
        mt_in = [sem("mt_in0"), sem("mt_in1")]
        cs_in = [sem("cs_in0"), sem("cs_in1")]
        in_free = sem("in_free")
        xg_ready = sem("xg_ready")
        z_ready = sem("z_ready")
        z_free = sem("z_free")
        sq_ready = sem("sq_ready")
        r1_ready = sem("r1_ready")
        qk_raw = sem("qk_raw")
        ss16_ready, rs16_ready = sem("ss16_ready"), sem("rs16_ready")
        qk_ready = sem("qk_ready")
        k_store = sem("k_store")
        v_store = sem("v_store")
        qp_store = sem("qp_store")
        stored = sem("stored")
        qk_free = sem("qk_free")
        p_ready = sem("p_ready")
        qTp_ready, qTp_free = sem("qTp_ready"), sem("qTp_free")
        kTp_ready, kTp_free = sem("kTp_ready"), sem("kTp_free")
        dTp_ready, dT_ready = sem("dTp_ready"), sem("dT_ready")
        py_ready, py_free = sem("py_ready"), sem("py_free")
        pe_done = sem("pe_done")
        head_pe = sem("head_pe")
        head_over = sem("head_over")
        wq_in = [sem(f"wq_in{i}") for i in range(4)]
        fold_ready, fold_free = sem("fold_ready"), sem("fold_free")
        folded = sem("folded")
        route_w = sem("route_w")
        wo_in, wo_ready = sem("wo_in"), sem("wo_ready")
        lam_ready, lam_done = sem("lam_ready"), sem("lam_done")
        a_over = sem("a_over")
        x1n_free = sem("x1n_free")
        mask_in = sem("mask_in")
        qp_in = sem("qp_in")
        x1_in = sem("x1_in")
        s_free = sem("s_free")
        s_ready = sem("s_ready")
        nm_ready, exp_ready = sem("nm_ready"), sem("exp_ready")
        a_ready, a_used = sem("a_ready"), sem("a_used")
        t_free, t_ready = sem("t_free"), sem("t_ready")
        t_evac = sem("t_evac")
        o_ready, o_free = sem("o_ready"), sem("o_free")
        att_raw = sem("att_raw")
        ss4_ready, rs4_ready = sem("ss4_ready"), sem("rs4_ready")
        att_ready = sem("att_ready")
        proj_ready = sem("proj_ready")
        x1_ready, x1_sq = sem("x1_ready"), sem("x1_sq")
        rs2_ready, r2_ready = sem("rs2_ready"), sem("r2_ready")
        route_ready, sc_ready = sem("route_ready"), sem("sc_ready")
        gexp_in, gexp_out = sem("gexp_in"), sem("gexp_out")
        e_free = sem("e_free")
        kv_in = sem("kv_in")
        msam_in, msam_free = sem("msam_in"), sem("msam_free")
        qz_ready, qz_free = sem("qz_ready"), sem("qz_free")
        pt_ready = sem("pt_ready")
        idx_lo, idx_hi = sem("idx_lo"), sem("idx_hi")
        slot_free = sem("slot_free")
        landed = [sem(f"landed{s}") for s in range(SLOTS)]
        dot_ready = sem("dot_ready")
        diag_ready = sem("diag_ready")
        y_ready = sem("y_ready")
        y_free = sem("y_free")
        y_store = sem("y_store")
        x1c_free = sem("x1c_free")

        block = ctx.enter_context(nc.Block())

        def tile_rows(t):
            return P if not isinstance(t, int) or t < LAST else ROWS8

        @block.sync
        def _(sp):
            n = Counter(sp)

            def head_load(t, par):
                sp.wait_ge(in_free, n(in_free))
                sp.dma_start(hxT[par], xT[t]).then_inc(xT_in[par], 16)
                sp.dma_start(hx[par], x[t]).then_inc(x_in[par], 16)
                sp.dma_start(hcs[par], cs[t]).then_inc(cs_in[par], 16)
                sp.dma_start(hmt[par], mt[t]).then_inc(mt_in[par], 16)

            def head_store(t, par):
                r = tile_rows(t)
                sp.wait_ge(k_store, n(k_store))
                sp.dma_start(k_all[t][0:r, :], hqk[par][0:r, 512:1024]).then_inc(stored, 16)
                sp.wait_ge(v_store, n(v_store))
                sp.dma_start(v_all[t][0:r, :], V3[0:r, t, :]).then_inc(stored, 16)
                if r < P:
                    sp.dma_start(p_last, hp[par][0:r, :]).then_inc(stored, 16)
                sp.wait_ge(qp_store, n(qp_store, 2))
                sp.dma_start(qp_dram[t], hqp[par]).then_inc(stored, 16)
                sp.wait_ge(stored, n(stored, 64 if r < P else 48))
                sp.sem_inc(qk_free, 1)

            sp.dma_start(hg1, g1T).then_inc(c_pool, 16)
            head_load(0, 0)
            for c in range(DC):
                sp.dma_start(w_in_sb[:, c, :], w_in[c]).then_inc(c_w_in[c], 16)
                if c == 1:
                    sp.dma_start(hgqk, gqk).then_inc(c_dve, 16)
                    sp.dma_start(bpT, b_poolT).then_inc(c_dve, 16)
                    sp.dma_start(scT, scaleT).then_inc(c_dve, 16)
                    sp.dma_start(g2c, g2T).then_inc(c_dve, 16)
                    sp.dma_start(subc, subT).then_inc(c_dve, 16)
                    sp.dma_start(r01, rows01).then_inc(c_dve, 16)
                    sp.dma_start(att[:, 0:256], lams).then_inc(c_dve, 16)
                    sp.dma_start(g2w[:, :], g2b).then_inc(c_dve, 16)
                    sp.dma_start(iota16[:, :], iota).then_inc(c_dve, 16)
                    sp.dma_start(hwp, w_pool).then_inc(c_pe, 16)
                    sp.dma_start(hst[0:SEQS * STATE, :], state).then_inc(c_pe, 16)
                    sp.dma_start(hmst[0:SEQS * STATE, :], mst).then_inc(c_pe, 16)
                    sp.dma_start(skT_sb, skT).then_inc(c_pe, 16)
                    sp.dma_start(pt[0:1, :], pages).then_inc(c_sp, 16)
            sp.dma_start(state_old, state.rearrange("(b j) n -> b j n", b=SEQS)[:, NEW:STATE, :]).then_inc(stored, 16)
            sp.wait_ge(stored, n(stored, 16))
            sp.wait_ge(c_sp, n(c_sp, 16))
            n.settle()
            with sp.Fori(0, LAST // 2) as j:
                head_load(2 * j + 1, 1)
                head_store(2 * j, 0)
                head_load(2 * j + 2, 0)
                head_store(2 * j + 1, 1)
                n.settle()
            head_store(LAST, 0)
            sp.sem_inc(head_over, 1)
            sp.wait_ge(head_pe, n(head_pe))
            for j in range(0, GROUPS, 4):
                sp.dma_start(wqT_sb[:, j:j + 4, :], wqT[j:j + 4].rearrange("j p n -> p j n")).then_inc(wq_in[j // 4], 16)
            sp.wait_ge(folded, n(folded))
            sp.dma_start(w_out_sb, w_out.rearrange("(c p) n -> p c n", p=P)).then_inc(wo_in, 16)

            def a_load(t):
                sp.wait_ge(a_over, n(a_over))
                sp.dma_start(mask_sb, mask[t]).then_inc(mask_in, 16)
                sp.dma_start(qpw[:, :], qp_dram[t]).then_inc(qp_in, 16)
                if isinstance(t, int) and t == LAST:
                    sp.dma_start(emask[:, :], mext).then_inc(mask_in, 16)
                    sample_load()
                sp.wait_ge(x1n_free, n(x1n_free))
                sp.dma_start(x1n, x[t]).then_inc(x1_in, 16)

            def sample_load():
                for g in range(SEQS // GRP):
                    sp.wait_ge(msam_free, n(msam_free))
                    sp.dma_start(msam_sb, msam[g]).then_inc(msam_in, 16)
                    for what in (ktc, vc):
                        for b in range(GRP * g, GRP * g + GRP):
                            sp.wait_ge(e_free, n(e_free))
                            for i in range(PAGES):
                                page = sp.value_load(pt[0:1, b * PAGES + i:b * PAGES + i + 1],
                                                     min_val=0, max_val=ktc.shape[0] - 1)
                                dst = Kb[:, i, :, :].rearrange("p h n -> p (h n)") if what is ktc else Vb[:, i, :]
                                sp.dma_start(dst, what[page]).then_inc(kv_in, 16)

            def y_out(t):
                r = tile_rows(t)
                sp.wait_ge(y_store, n(y_store))
                sp.dma_start(y_all[t][0:r, :], x1c[0:r, :]).then_inc(stored, 16)
                sp.wait_ge(stored, n(stored, 16))
                sp.sem_inc(x1c_free, 1)

            a_load(0)
            n.settle()
            with sp.Fori(0, LAST - 1) as t:
                a_load(t + 1)
                y_out(t)
                n.settle()
            a_load(LAST)
            y_out(LAST - 1)
            y_out(LAST)

        @block.gpsimd
        def _(pool):
            n = Counter(pool)
            pool.memset(ident[:, :], 0.0).then_inc(pool_own, 1)
            pool.memset(hp[1], 0.0).then_inc(p0_ready, 1)
            pool.wait_ge(pool_own, n(pool_own))
            pool.affine_select(out=ident[:, :], in_=ident[:, :], compare_op=ALU.not_equal, fill=1.0,
                               base=0, pattern=[[-1, P]], channel_multiplier=1).then_inc(pool_own, 1)
            pool.wait_ge(pool_own, n(pool_own))
            pool.sem_inc(ident_pe, 1)
            pool.sem_inc(ident_act, 1)
            pool.wait_ge(c_pool, n(c_pool, 16))
            n.settle()

            def head(par):
                pool.wait_ge(xT_in[par], n(xT_in[par], 16))
                v = hxT[par].rearrange("p (c n) -> p c n", c=DC)
                pool.tensor_tensor(v, v, hg1.unsqueeze(2).to_broadcast([P, DC, P]), ALU.mult).then_inc(pool_own, 1)
                pool.wait_ge(pool_own, n(pool_own))
                pool.sem_inc(xg_ready, 1)

            with pool.Fori(0, LAST // 2):
                head(0)
                head(1)
                n.settle()
            head(0)
            pool.sem_inc(head_over, 1)
            n.settle()

            def gather(r):
                for k in range(PICKS):
                    if k == 0:
                        pool.wait_ge(idx_lo, n(idx_lo))
                    if k == PICKS // 2:
                        pool.wait_ge(idx_hi, n(idx_hi))
                    pool.wait_ge(slot_free, n(slot_free))
                    pool.indirect_dma_start(ring[0:r, k % SLOTS, :], None, wuv,
                                            bass.IndirectOffsetOnAxis(ap=idx_c[0:r, k:k + 1], axis=0)
                                            ).then_inc(landed[k % SLOTS], 16)
                n.settle()

            with pool.Fori(0, LAST):
                gather(P)
            gather(ROWS8)

        @block.tensor
        def _(pe):
            n = Counter(pe)

            def head(par, first=False, last=False):
                pe.wait_ge(xg_ready, n(xg_ready))
                for q in range(4):
                    pe.wait_ge(z_free, n(z_free))
                    for c in range(DC):
                        if first and q == 0:
                            pe.wait_ge(c_w_in[c], n(c_w_in[c], 16))
                        mm = pe.matmul(zbank[q], hxT[par][:, c * P:(c + 1) * P],
                                       w_in_sb[:, c, q * 512:(q + 1) * 512], start=(c == 0), stop=(c == DC - 1))
                    mm.then_inc(z_ready, 1)
                pe.wait_ge(qk_ready, n(qk_ready))
                pe.wait_ge(qTp_free, n(qTp_free))
                for h in range(HEADS):
                    mm = pe.transpose(qTp[:, h * P:(h + 1) * P], hqk[par][:, h * P:(h + 1) * P], ident[:, :])
                mm.then_inc(qTp_ready, 1)
                pe.wait_ge(kTp_free, n(kTp_free))
                for h in range(HEADS):
                    mm = pe.transpose(kTp[:, h * P:(h + 1) * P], hqk[par][:, 512 + h * P:512 + (h + 1) * P], ident[:, :])
                mm.then_inc(kTp_ready, 1)
                pe.wait_ge(p_ready, n(p_ready))
                pe.wait_ge(mt_in[par], n(mt_in[par], 16))
                for g in range(4):
                    s = slice(g * P, (g + 1) * P)
                    pe.matmul(dTp[:, s], hp[par][:, s], hmt[par][:, s], start=True, stop=False)
                    mm = pe.matmul(dTp[:, s], hp[1 - par][:, s], hmt[par][:, 512 + g * P:512 + (g + 1) * P],
                                   start=False, stop=not last)
                    if last:
                        r = SEQS * STATE
                        mm = pe.matmul(dTp[:, s], hst[0:r, s], hmst[0:r, s], start=False, stop=True)
                mm.then_inc(dTp_ready, 1)
                pe.wait_ge(dT_ready, n(dT_ready))
                pe.wait_ge(py_free, n(py_free))
                for g in range(4):
                    s = slice(g * P, (g + 1) * P)
                    mm = pe.matmul(pyp[:, s], hwp[:, s], hdT[:, s], start=True, stop=True)
                mm.then_inc(py_ready, 1)
                pe.wait_ge(pe_done, n(pe_done))
                pe.sem_inc(in_free, 1)

            pe.wait_ge(ident_pe, n(ident_pe))
            pe.wait_ge(p0_ready, n(p0_ready))
            pe.wait_ge(c_pe, n(c_pe, 64))
            head(0, first=True)
            head(1)
            n.settle()
            with pe.Fori(1, LAST // 2):
                head(0)
                head(1)
                n.settle()
            head(0, last=True)
            pe.sem_inc(head_pe, 1)
            pe.sem_inc(head_over, 1)
            n.settle()

            for j in range(GROUPS):
                if j % 4 == 0:
                    pe.wait_ge(wq_in[j // 4], n(wq_in[j // 4], 16))
                pe.wait_ge(fold_free, n(fold_free))
                bank = S[j % 2]
                for c in range(DC):
                    mm = pe.matmul(bank[:, c * P:(c + 1) * P], wqT_sb[:, j, c * P:(c + 1) * P], skT_sb[:, j, :],
                                   start=True, stop=True)
                mm.then_inc(fold_ready, 1)
            pe.wait_ge(route_w, n(route_w))
            pe.sem_inc(folded, 1)
            pe.wait_ge(wo_ready, n(wo_ready))
            n.settle()

            def scores_of(h, last):
                if h == 0:
                    pe.wait_ge(qp_in, n(qp_in, 16))
                pe.wait_ge(s_free, n(s_free))
                if last:
                    pe.wait_ge(t_free, n(t_free))
                for c in range(2):
                    r = slice(QK * c, QK * c + QK)
                    for m in range(2):
                        mm = pe.matmul(S[c][:, m * 512:(m + 1) * 512], qT[r, h, :], KT3[r, h, m * 512:(m + 1) * 512],
                                       start=True, stop=True)
                    if last:
                        mm = pe.matmul(T[:, c * ROWS8:(c + 1) * ROWS8], qT[r, h, :], KT3[r, h, KEYS:KTW],
                                       start=True, stop=True)
                        if c == 0:
                            mm.then_inc(pe_own, 1)
                            pe.wait_ge(pe_own, n(pe_own))
                mm.then_inc(s_ready, 1)

            def flip(m, last=False):
                if m == 0:
                    pe.wait_ge(a_ready, n(a_ready))
                pe.wait_ge(t_free, n(t_free))
                for i in range(4):
                    b = 4 * m + i
                    mm = pe.transpose(T[:, i * P:(i + 1) * P], e0[:, b * P:(b + 1) * P], ident[:, :])
                mm.then_inc(t_ready, 1)
                if m == 1 and last:
                    pe.wait_ge(t_free, n(t_free))
                    pe.transpose(T[0:ROWS8, 0:P], ex0, ident[:, :]).then_inc(t_ready, 1)

            def values(h, last):
                pe.wait_ge(t_evac, n(t_evac, 3 if last else 2))
                pe.sem_inc(a_used, 1)
                if h == 0:
                    pe.wait_ge(o_free, n(o_free))
                for b in range(LAST):
                    mm = pe.matmul(O[:, h * P:(h + 1) * P], aT[:, b * P:(b + 1) * P], V3[:, b, h * P:(h + 1) * P],
                                   start=(b == 0 and (h == 0 or not last)), stop=(b == LAST - 1) and not last,
                                   skip_group_check=True)
                if last:
                    mm = pe.matmul(O[:, h * P:(h + 1) * P], exT[0:ROWS8, :], V3[0:ROWS8, LAST, h * P:(h + 1) * P],
                                   start=False, stop=False, skip_group_check=True)
                    if h == HEADS - 1:
                        mm.then_inc(qz_free, 1)
                elif h == HEADS - 1:
                    mm.then_inc(o_ready, 1)

            def sample_scores(b):
                bl = b % GRP
                if bl == 0:
                    pe.wait_ge(s_free, n(s_free))
                pe.wait_ge(qz_ready, n(qz_ready))
                pe.wait_ge(kv_in, n(kv_in, 32))
                for h in range(HEADS):
                    lo = P + P * h - (bl * 32 + h * 8)
                    w = QZ[:, lo:lo + P]
                    a, z = (bl == 0 and h == 0), (bl == GRP - 1 and h == HEADS - 1)
                    for i in range(PAGES):
                        pe.matmul(S0[:, i * P:(i + 1) * P], w, Kb[:, i, h, :], start=a and i == 0, stop=z, skip_group_check=True)
                    mm = pe.matmul(S1[:, 0:ROWS8], w, KT3[:, h, KEYS:KTW], start=a, stop=z, skip_group_check=True)
                mm.then_inc(qz_free, 1)

            def sample_flip():
                pe.wait_ge(a_ready, n(a_ready))
                pe.wait_ge(t_free, n(t_free))
                pe.transpose(T[:, 0:P], Ps[:, 0:P], ident[:, :])
                pe.transpose(T[:, P:2 * P], Ps[:, P:2 * P], ident[:, :])
                pe.transpose(T[0:ROWS8, 2 * P:3 * P], Ps[:, 2 * P:SW], ident[:, :]).then_inc(t_ready, 1)

            def sample_values(b):
                pe.wait_ge(qz_ready, n(qz_ready))
                pe.wait_ge(kv_in, n(kv_in, 32))
                for h in range(HEADS):
                    z = b == SEQS - 1
                    for i in range(3):
                        lo = P + P * (HEADS * i + h) - (TAIL + NEW * b)
                        if i < PAGES:
                            w, v = AZ[:, lo:lo + P], Vb[:, i, h * P:(h + 1) * P]
                        else:
                            w, v = AZ[0:ROWS8, lo:lo + P], V3[0:ROWS8, LAST, h * P:(h + 1) * P]
                        mm = pe.matmul(O[:, h * P:(h + 1) * P], w, v, start=False, stop=z and i == 2,
                                       skip_group_check=True)
                mm.then_inc(qz_free, 1)

            def flip_att():
                pe.wait_ge(att_ready, n(att_ready))
                pe.wait_ge(t_free, n(t_free))
                for h in range(HEADS):
                    mm = pe.transpose(T[:, h * P:(h + 1) * P], att[:, h * P:(h + 1) * P], ident[:, :])
                mm.then_inc(t_ready, 1)

            def project():
                pe.wait_ge(t_evac, n(t_evac))
                pe.wait_ge(s_free, n(s_free))
                for c in range(DC):
                    lhs = aT[:, c * P:(c + 1) * P] if c < HEADS else pyT[:, c - HEADS, :]
                    for m in range(2):
                        mm = pe.matmul(S0[:, m * 512:(m + 1) * 512], lhs, w_out_sb[:, c, m * 512:(m + 1) * 512],
                                       start=(c == 0), stop=(c == DC - 1), skip_group_check=True)
                mm.then_inc(proj_ready, 1)

            def flip_x1(m):
                if m == 0:
                    pe.wait_ge(x1_ready, n(x1_ready))
                pe.wait_ge(t_free, n(t_free))
                for i in range(4):
                    b = 4 * m + i
                    mm = pe.transpose(T[:, i * P:(i + 1) * P], x1n[:, b * P:(b + 1) * P], ident[:, :])
                mm.then_inc(t_ready, 1)

            def route(q):
                if q == 0:
                    pe.wait_ge(t_evac, n(t_evac, 2))
                    pe.wait_ge(s_free, n(s_free))
                for c in range(DC):
                    mm = pe.matmul(route_bank[q], aT[:, c * P:(c + 1) * P], w_route[:, c, q * 512:(q + 1) * 512],
                                   start=(c == 0), stop=(c == DC - 1))
                mm.then_inc(route_ready, 1)

            def a_part(k, last):
                for h in range(HEADS):
                    b = HEAD0 + HEADW * h
                    if k == b:
                        scores_of(h, last)
                    if k == b + 4:
                        flip(0)
                    if k == b + 5:
                        flip(1, last)
                    if k == b + 6:
                        values(h, last)
                if last:
                    for g in range(SEQS // GRP):
                        s = SAMP0 + SAMPW * g
                        for i in range(GRP):
                            if k == s + 2 * i + 1:
                                sample_scores(GRP * g + i)
                            if k == s + 12 + 2 * i + 1:
                                sample_values(GRP * g + i)
                        if k == s + 10:
                            sample_flip()
                d = after_attention(last)
                if k == d + 4:
                    flip_att()
                if k == d + 5:
                    project()
                if k == d + 8:
                    flip_x1(0)
                if k == d + 9:
                    flip_x1(1)
                for q in range(4):
                    if k == d + 10 + q:
                        route(q)

            def g_step(k, r):
                if k == 0:
                    pe.wait_ge(y_free, n(y_free))
                pe.wait_ge(diag_ready, n(diag_ready))
                s = k % SLOTS
                for m in range(2):
                    mm = pe.matmul(Y[:, m * 512:(m + 1) * 512], diag[0:r, s * P:(s + 1) * P],
                                   ring[0:r, s, D + m * 512:D + (m + 1) * 512],
                                   start=(k == 0), stop=(k == PICKS - 1), skip_group_check=True)
                mm.then_inc(slot_free if k < PICKS - 1 else y_ready, 1)

            for k in range(PICKS):
                a_part(k, False)
            n.settle()
            with pe.Fori(0, LAST - 1):
                for k in range(PICKS):
                    g_step(k, P)
                    a_part(k, False)
                n.settle()
            for k in range(PICKS):
                g_step(k, P)
                a_part(k, True)
            for k in range(PICKS):
                g_step(k, ROWS8)

        @block.scalar
        def _(act):
            n = Counter(act)
            act.sem_inc(z_free, 4)
            act.sem_inc(qTp_free, 1)
            act.sem_inc(t_free, 1)
            act.sem_inc(o_free, 1)
            act.wait_ge(eps_ready, n(eps_ready))
            n.settle()

            def head(par, t):
                act.wait_ge(x_in[par], n(x_in[par], 16))
                act.activation(hx[par], hx[par], ACT.Square, accum_out=ss1).then_inc(act_own, 1)
                act.wait_ge(act_own, n(act_own))
                act.activation(rs1, ss1, ACT.Sqrt, scale=1.0 / D, bias=eps).then_inc(sq_ready, 1)
                act.wait_ge(r1_ready, n(r1_ready))
                act.wait_ge(qk_free, n(qk_free))
                for q in range(4):
                    act.wait_ge(z_ready, n(z_ready))
                    dst = [hqk[par][:, 0:512], hqk[par][:, 512:1024], V3[:, t, :], hp[par]][q]
                    act.activation(dst, zbank[q], ACT.Copy, scale=rs1).then_inc(act_own, 1)
                    act.wait_ge(act_own, n(act_own))
                    act.sem_inc(z_free, 1)
                    if q == 1:
                        act.sem_inc(qk_raw, 1)
                    if q == 2:
                        act.wait_ge(ss16_ready, n(ss16_ready))
                        act.activation(rs16, ss16, ACT.Sqrt, scale=1.0 / QK, bias=eps).then_inc(rs16_ready, 1)
                act.sem_inc(p_ready, 1)
                act.sem_inc(v_store, 1)
                act.wait_ge(qTp_ready, n(qTp_ready))
                act.activation(hqp[par][:, 0:512], qTp, ACT.Copy).then_inc(act_own, 1)
                act.wait_ge(act_own, n(act_own))
                act.sem_inc(qTp_free, 1)
                act.sem_inc(qp_store, 1)
                act.wait_ge(dTp_ready, n(dTp_ready))
                act.activation(hdT, dTp, ACT.Copy).then_inc(dT_ready, 1)

            with act.Fori(0, LAST // 2) as j:
                head(0, 2 * j)
                head(1, 2 * j + 1)
                n.settle()
            head(0, LAST)
            n.settle()
            act.wait_ge(lam_ready, n(lam_ready))
            act.activation(lamt[:, 2:4], lamt[:, 0:2], ACT.Exp).then_inc(lam_done, 1)
            act.sem_inc(head_over, 1)
            act.wait_ge(ident_act, n(ident_act))
            n.settle()

            def exps(last):
                act.wait_ge(nm_ready, n(nm_ready))
                for c in range(2):
                    act.activation([e0, e1][c], [e0, e1][c], ACT.Exp, scale=-1.0, bias=nm[:, c:c + 1],
                                   accum_out=sums[:, c:c + 1]).then_inc(act_own, 1)
                    if last:
                        act.activation([ex0, ex1][c], [ex0, ex1][c], ACT.Exp, scale=-1.0, bias=nm[:, c:c + 1],
                                       accum_out=sums[:, 2 + c:3 + c]).then_inc(act_own, 1)
                act.wait_ge(act_own, n(act_own, 4 if last else 2))
                act.sem_inc(exp_ready, 1)

            def evac(dst, src):
                act.wait_ge(t_ready, n(t_ready))
                act.activation(dst, src, ACT.Copy).then_inc(act_own, 1)
                act.wait_ge(act_own, n(act_own))
                act.sem_inc(t_free, 1)
                act.sem_inc(t_evac, 1)

            def a_part(k, last):
                for h in range(HEADS):
                    b = HEAD0 + HEADW * h
                    if k == b + 2:
                        exps(last)
                    if k == b + 4:
                        evac(aT[:, 0:512], T[:, :])
                    if k == b + 5:
                        evac(aT[:, 512:1024], T[:, :])
                        if last:
                            evac(exT[0:ROWS8, :], T[0:ROWS8, 0:P])
                if last:
                    for g in range(SEQS // GRP):
                        s = SAMP0 + SAMPW * g
                        if k == s + 9:
                            act.wait_ge(nm_ready, n(nm_ready))
                            act.activation(Ps, Ps, ACT.Exp, scale=-1.0, bias=snm, accum_out=ssum).then_inc(exp_ready, 1)
                        if k == s + 10:
                            act.wait_ge(t_ready, n(t_ready))
                            act.activation(PT[:, 0:2, :], T[:, 0:2 * P].rearrange("p (k n) -> p k n", k=2),
                                           ACT.Copy).then_inc(act_own, 1)
                            act.activation(PT[0:ROWS8, 2, :], T[0:ROWS8, 2 * P:3 * P], ACT.Copy).then_inc(act_own, 1)
                            act.wait_ge(act_own, n(act_own, 2))
                            act.sem_inc(t_free, 1)
                            act.sem_inc(pt_ready, 1)
                d = after_attention(last)
                if k == d:
                    act.wait_ge(o_ready, n(o_ready))
                    act.activation(att[:, :], O[:, :], ACT.Copy).then_inc(act_own, 1)
                    act.wait_ge(act_own, n(act_own))
                    act.sem_inc(o_free, 1)
                    act.sem_inc(att_raw, 1)
                if k == d + 2:
                    act.wait_ge(ss4_ready, n(ss4_ready))
                    act.activation(rs4, ss4, ACT.Sqrt, scale=1.0 / P, bias=eps).then_inc(rs4_ready, 1)
                if k == d + 4:
                    evac(aT[:, 0:512], T[:, :])
                if k == d + 8:
                    act.wait_ge(x1_sq, n(x1_sq))
                    act.activation(e0, x1n, ACT.Square, accum_out=ss2).then_inc(act_own, 1)
                    act.wait_ge(act_own, n(act_own))
                    act.activation(rs2, ss2, ACT.Sqrt, scale=1.0 / D, bias=eps).then_inc(rs2_ready, 1)
                    evac(aT[:, 0:512], T[:, :])
                if k == d + 9:
                    evac(aT[:, 512:1024], T[:, :])
                for q in range(4):
                    if k == d + 11 + q:
                        if q == 0:
                            act.wait_ge(r2_ready, n(r2_ready))
                        act.wait_ge(route_ready, n(route_ready))
                        act.activation(work[:, q * 512:(q + 1) * 512], route_bank[q], ACT.Copy, scale=r2)\
                            .then_inc(act_own, 1)
                        act.wait_ge(act_own, n(act_own))
                        act.sem_inc(sc_ready, 1)
                        if q == 3:
                            act.sem_inc(s_free, 1)
                if k == d + 55:
                    act.wait_ge(gexp_in, n(gexp_in))
                    act.activation(gate_n[:, :], gate_n[:, :], ACT.Exp).then_inc(gexp_out, 1)

            def g_step(k, r):
                s = k % SLOTS
                act.wait_ge(dot_ready, n(dot_ready))
                act.activation(gel[0:r, s:s + 1], dots[0:r, s:s + 1], ACT.Gelu).then_inc(act_own, 1)
                act.wait_ge(act_own, n(act_own))
                act.activation(amp[0:r, s:s + 1], gel[0:r, s:s + 1], ACT.Copy, scale=gate_c[0:r, k:k + 1])\
                    .then_inc(act_own, 1)
                act.wait_ge(act_own, n(act_own))
                act.activation(diag[0:r, s * P:(s + 1) * P], ident[0:r, :], ACT.Copy, scale=amp[0:r, s:s + 1])\
                    .then_inc(diag_ready, 1)

            for k in range(PICKS):
                a_part(k, False)
            n.settle()
            with act.Fori(0, LAST - 1):
                for k in range(PICKS):
                    g_step(k, P)
                    a_part(k, False)
                n.settle()
            for k in range(PICKS):
                g_step(k, P)
                a_part(k, True)
            for k in range(PICKS):
                g_step(k, ROWS8)

        @block.vector
        def _(dve):
            n = Counter(dve)

            dve.memset(eps, EPS).then_inc(dve_own, 1)
            dve.wait_ge(dve_own, n(dve_own))
            dve.sem_inc(eps_ready, 1)
            dve.sem_inc(in_free, 2)
            dve.sem_inc(qk_free, 2)
            dve.sem_inc(kTp_free, 1)
            dve.sem_inc(py_free, 1)
            dve.sem_inc(fold_free, 2)
            dve.sem_inc(s_free, 1)
            dve.sem_inc(y_free, 1)
            dve.sem_inc(slot_free, SLOTS)
            dve.sem_inc(x1c_free, 1)
            dve.sem_inc(x1n_free, 1)
            dve.sem_inc(a_over, 1)
            dve.wait_ge(c_dve, n(c_dve, 9 * 16))
            for i in range(2):
                dve.tensor_tensor_reduce(out=att[:, i * 128:i * 128 + QK], in0=att[:, i * 128:i * 128 + QK],
                                         in1=att[:, i * 128 + QK:(i + 1) * 128], scale=1.0, scalar=0.0,
                                         op0=ALU.mult, op1=ALU.add, accum_out=lamt[:, i:i + 1]).then_inc(dve_own, 1)
                dve.wait_ge(dve_own, n(dve_own))
            dve.sem_inc(lam_ready, 1)
            n.settle()

            def head(par, t):
                dve.wait_ge(sq_ready, n(sq_ready))
                dve.reciprocal(rs1, rs1).then_inc(r1_ready, 1)
                dve.wait_ge(qk_raw, n(qk_raw))
                qk = hqk[par]
                qk3 = qk.rearrange("p (g n) -> p g n", g=16)
                dve.tensor_tensor(hsq, qk, qk, ALU.mult).then_inc(dve_own, 1)
                dve.wait_ge(dve_own, n(dve_own))
                dve.tensor_reduce(ss16, hsq.rearrange("p (g n) -> p g n", g=16), AX.X, ALU.add).then_inc(ss16_ready, 1)
                dve.wait_ge(rs16_ready, n(rs16_ready))
                dve.reciprocal(rs16, rs16).then_inc(dve_own, 1)
                dve.wait_ge(dve_own, n(dve_own))
                dve.tensor_tensor(qk3, qk3, rs16.unsqueeze(2).to_broadcast([P, 16, QK]), ALU.mult)\
                    .then_inc(dve_own, 1)
                dve.wait_ge(dve_own, n(dve_own))
                dve.tensor_tensor(qk, qk, hgqk, ALU.mult).then_inc(dve_own, 1)
                dve.wait_ge(dve_own, n(dve_own))
                dve.wait_ge(cs_in[par], n(cs_in[par], 16))
                a, b = qk3[:, :, 0:HALF], qk3[:, :, HALF:ROPE]
                cos = hcs[par][:, 0:HALF].unsqueeze(1).to_broadcast([P, 16, HALF])
                sin = hcs[par][:, HALF:ROPE].unsqueeze(1).to_broadcast([P, 16, HALF])
                tmp = [hrope[:, i * 128:(i + 1) * 128].rearrange("p (g n) -> p g n", g=16) for i in range(4)]
                for to, u, w in zip(tmp, (a, b, b, a), (cos, sin, cos, sin)):
                    dve.tensor_tensor(to, u, w, ALU.mult).then_inc(dve_own, 1)
                dve.wait_ge(dve_own, n(dve_own, 4))
                dve.tensor_tensor(a, tmp[0], tmp[1], ALU.subtract).then_inc(dve_own, 1)
                dve.tensor_tensor(b, tmp[2], tmp[3], ALU.add).then_inc(dve_own, 1)
                dve.wait_ge(dve_own, n(dve_own, 2))
                dve.sem_inc(qk_ready, 1)
                dve.sem_inc(k_store, 1)
                dve.wait_ge(kTp_ready, n(kTp_ready))
                w = P if not isinstance(t, int) or t < LAST else ROWS8
                dve.tensor_copy(KT3[:, :, bass.ds(t * P, w)],
                                kTp.rearrange("p (h n) -> p h n", h=HEADS)[:, :, 0:w]).then_inc(dve_own, 1)
                dve.wait_ge(dve_own, n(dve_own))
                dve.sem_inc(kTp_free, 1)
                dve.wait_ge(py_ready, n(py_ready))
                for g in range(4):
                    dve.tensor_scalar(hqp[par][:, 512 + g * P:512 + (g + 1) * P], pyp[:, g * P:(g + 1) * P],
                                      bpT[:, g:g + 1], scT[:, g:g + 1], ALU.add, ALU.mult).then_inc(dve_own, 1)
                dve.wait_ge(dve_own, n(dve_own, 4))
                dve.sem_inc(py_free, 1)
                dve.sem_inc(pe_done, 1)
                dve.sem_inc(qp_store, 1)

            with dve.Fori(0, LAST // 2) as j:
                head(0, 2 * j)
                head(1, 2 * j + 1)
                n.settle()
            head(0, LAST)
            dve.wait_ge(head_over, n(head_over, 4))
            for j in range(GROUPS):
                dve.wait_ge(fold_ready, n(fold_ready))
                dve.tensor_tensor(w_route[:, :, j * P:(j + 1) * P],
                                  S[j % 2][:, :].rearrange("p (c n) -> p c n", c=DC),
                                  g2c.unsqueeze(2).to_broadcast([P, DC, P]), ALU.mult).then_inc(dve_own, 1)
                dve.wait_ge(dve_own, n(dve_own))
                dve.sem_inc(fold_free, 1)
            dve.sem_inc(route_w, 1)
            dve.wait_ge(lam_done, n(lam_done))
            dve.tensor_tensor(lamt[:, 0:1], lamt[:, 3:4], lamt[:, 2:3], ALU.subtract).then_inc(dve_own, 1)
            dve.wait_ge(dve_own, n(dve_own))
            dve.tensor_scalar(coef[:, 1:2], lamt[:, 0:1], -LAM_INIT, None, ALU.add).then_inc(dve_own, 1)
            dve.wait_ge(dve_own, n(dve_own))
            dve.memset(coef[:, 0:1], 1.0).then_inc(dve_own, 1)
            dve.tensor_copy(coef[:, 2:3], r01[:, 0:1]).then_inc(dve_own, 1)
            dve.tensor_tensor(coef[:, 3:4], coef[:, 1:2], r01[:, 0:1], ALU.mult).then_inc(dve_own, 1)
            dve.scalar_tensor_tensor(scoef, r01[:, 2:3], coef[:, 1:2], r01[:, 1:2], ALU.mult, ALU.add)\
                .then_inc(dve_own, 1)
            dve.wait_ge(dve_own, n(dve_own, 4))
            dve.wait_ge(wo_in, n(wo_in, 16))
            for c in range(HEADS):
                dve.tensor_scalar(w_out_sb[:, c, :], w_out_sb[:, c, :], subc, 1.0 - LAM_INIT, ALU.mult, ALU.mult)\
                    .then_inc(dve_own, 1)
            dve.wait_ge(dve_own, n(dve_own, HEADS))
            dve.sem_inc(wo_ready, 1)
            n.settle()

            def scale_mask(h, last):
                if h == 0:
                    dve.wait_ge(mask_in, n(mask_in, 32 if last else 16))
                else:
                    dve.wait_ge(a_used, n(a_used))
                dve.wait_ge(s_ready, n(s_ready))
                for c in range(2):
                    dve.tensor_tensor_reduce(out=[e0, e1][c], in0=S[c][:, :], in1=mask_sb, scale=-(QK ** -0.5),
                                             scalar=3e38, op0=ALU.add, op1=ALU.min,
                                             accum_out=nmx[:, c:c + 1]).then_inc(dve_own, 1)
                    if last:
                        dve.tensor_tensor_reduce(out=[ex0, ex1][c], in0=T[:, c * ROWS8:(c + 1) * ROWS8], in1=emask[:, :],
                                                 scale=-(QK ** -0.5), scalar=3e38, op0=ALU.add, op1=ALU.min,
                                                 accum_out=nmx[:, 2 + c:3 + c]).then_inc(dve_own, 1)
                dve.wait_ge(dve_own, n(dve_own, 4 if last else 2))
                if last:
                    dve.tensor_tensor(nm, nmx[:, 0:2], nmx[:, 2:4], ALU.min).then_inc(dve_own, 1)
                    dve.wait_ge(dve_own, n(dve_own))
                    dve.sem_inc(t_free, 1)
                else:
                    dve.tensor_copy(nm, nmx[:, 0:2]).then_inc(dve_own, 1)
                    dve.wait_ge(dve_own, n(dve_own))
                dve.sem_inc(nm_ready, 1)
                dve.sem_inc(s_free, 1)

            def combine(last):
                dve.wait_ge(exp_ready, n(exp_ready))
                cf = coef[:, 2:4] if last else coef[:, 0:2]
                if last:
                    dve.tensor_tensor(sums[:, 0:2], sums[:, 0:2], sums[:, 2:4], ALU.add).then_inc(dve_own, 1)
                    dve.wait_ge(dve_own, n(dve_own))
                dve.reciprocal(rc, sums[:, 0:2]).then_inc(dve_own, 1)
                dve.wait_ge(dve_own, n(dve_own))
                dve.tensor_tensor(rc, rc, cf, ALU.mult).then_inc(dve_own, 1)
                dve.wait_ge(dve_own, n(dve_own))
                dve.tensor_scalar(e1, e1, rc[:, 1:2], None, ALU.mult).then_inc(dve_own, 1)
                dve.wait_ge(dve_own, n(dve_own))
                dve.scalar_tensor_tensor(e0, e0, rc[:, 0:1], e1, ALU.mult, ALU.add).then_inc(dve_own, 1)
                dve.wait_ge(dve_own, n(dve_own))
                if last:
                    dve.tensor_scalar(ex1, ex1, rc[:, 1:2], None, ALU.mult).then_inc(dve_own, 1)
                    dve.wait_ge(dve_own, n(dve_own))
                    dve.scalar_tensor_tensor(ex0, ex0, rc[:, 0:1], ex1, ALU.mult, ALU.add).then_inc(dve_own, 1)
                    dve.wait_ge(dve_own, n(dve_own))
                dve.sem_inc(a_ready, 1)

            def sample(k, g, s):
                for i in range(GRP):
                    b = GRP * g + i
                    if k == s + 2 * i:
                        if i == 0:
                            if g == 0:
                                dve.wait_ge(a_used, n(a_used))
                                dve.wait_ge(qz_free, n(qz_free))
                            dve.memset(QZ, 0.0).then_inc(dve_own, 1)
                            dve.wait_ge(dve_own, n(dve_own))
                            dve.sem_inc(msam_free, 1)
                            dve.sem_inc(e_free, 1)
                        if i > 0:
                            dve.wait_ge(qz_free, n(qz_free))
                            dve.sem_inc(e_free, 1)
                        for c in range(2):
                            r = slice(QK * c, QK * c + QK)
                            dve.tensor_copy(QZ[r, P:].rearrange("p (h n) -> p h n", h=HEADS)[:, :, c * NEW:(c + 1) * NEW],
                                            qT[r, :, TAIL + NEW * b:TAIL + NEW * (b + 1)]).then_inc(dve_own, 1)
                        dve.wait_ge(dve_own, n(dve_own, 2))
                        dve.sem_inc(qz_ready, 1)
                if k == s + 8:
                    dve.wait_ge(qz_free, n(qz_free))
                    dve.wait_ge(msam_in, n(msam_in, 16))
                    dve.tensor_tensor(Ps[:, 0:PAST], S0[:, 0:PAST], msam_sb[:, 0:PAST], ALU.add).then_inc(dve_own, 1)
                    dve.wait_ge(dve_own, n(dve_own))
                    dve.tensor_tensor(Ps[:, PAST:SW], S1[:, 0:ROWS8], msam_sb[:, PAST:SW], ALU.add)\
                        .then_inc(dve_own, 1)
                    dve.wait_ge(dve_own, n(dve_own))
                    dve.sem_inc(s_free, 1)
                    dve.tensor_scalar(Ps, Ps, -(QK ** -0.5), None, ALU.mult).then_inc(dve_own, 1)
                    dve.wait_ge(dve_own, n(dve_own))
                    dve.tensor_reduce(snm, Ps, AX.X, ALU.min).then_inc(dve_own, 1)
                    dve.wait_ge(dve_own, n(dve_own))
                    dve.sem_inc(nm_ready, 1)
                if k == s + 10:
                    dve.wait_ge(exp_ready, n(exp_ready))
                    dve.reciprocal(src, ssum).then_inc(dve_own, 1)
                    dve.wait_ge(dve_own, n(dve_own))
                    dve.tensor_tensor(src, src, scoef, ALU.mult).then_inc(dve_own, 1)
                    dve.wait_ge(dve_own, n(dve_own))
                    dve.tensor_scalar(Ps, Ps, src, None, ALU.mult).then_inc(dve_own, 1)
                    dve.wait_ge(dve_own, n(dve_own))
                    dve.sem_inc(a_ready, 1)
                    dve.memset(AZ, 0.0).then_inc(dve_own, 1)
                    dve.wait_ge(dve_own, n(dve_own))
                for i in range(GRP):
                    b = GRP * g + i
                    if k == s + 12 + 2 * i:
                        if i == 0:
                            dve.wait_ge(pt_ready, n(pt_ready))
                        else:
                            dve.wait_ge(qz_free, n(qz_free))
                        dve.sem_inc(e_free, 1)
                        for kind in range(3):
                            r = slice(0, P if kind < PAGES else ROWS8)
                            src4 = PT[r, kind, i * 32:(i + 1) * 32].rearrange("p (h n) -> p h n", h=HEADS)
                            to = AZ[r, P + P * HEADS * kind:P + P * HEADS * (kind + 1)]\
                                .rearrange("p (h n) -> p h n", h=HEADS)[:, :, 0:NEW]
                            dve.tensor_tensor(to, src4[:, :, 0:NEW], src4[:, :, NEW:2 * NEW], ALU.add)\
                                .then_inc(dve_own, 1)
                        dve.wait_ge(dve_own, n(dve_own, 3))
                        dve.sem_inc(qz_ready, 1)
                if k == s + 19:
                    dve.wait_ge(qz_free, n(qz_free))
                    if g == SEQS // GRP - 1:
                        dve.sem_inc(o_ready, 1)
                        dve.sem_inc(x1n_free, 1)

            def top16(values, indices, source, which):
                m = len(which)
                for lo in (0, 8):
                    for g in which:
                        dve.max(values[:, g, lo:lo + 8], source[:, g, :]).then_inc(dve_own, 1)
                    dve.wait_ge(dve_own, n(dve_own, m))
                    for g in which:
                        dve.max_index(indices[:, g, lo:lo + 8], values[:, g, lo:lo + 8], source[:, g, :])\
                            .then_inc(dve_own, 1)
                    dve.wait_ge(dve_own, n(dve_own, m))
                    if lo == 0:
                        for g in which:
                            dve.match_replace(source[:, g, :], values[:, g, lo:lo + 8], source[:, g, :], -3e38)\
                                .then_inc(dve_own, 1)
                        dve.wait_ge(dve_own, n(dve_own, m))

            def lookup(pick, pos, half):
                dve.tensor_tensor(onehot, pos.rearrange("p (h k) -> p h k", h=PH).unsqueeze(3)
                                  .to_broadcast([P, PH, TOPK, TOPK]),
                                  iota16[:, :].unsqueeze(1).unsqueeze(1).to_broadcast([P, PH, TOPK, TOPK]),
                                  ALU.is_equal).then_inc(dve_own, 1)
                dve.wait_ge(dve_own, n(dve_own))
                keys = sif.rearrange("p (h c) k -> p h c k", c=2)[:, :, half, :]
                dve.tensor_tensor(onehot, onehot, keys.unsqueeze(2).to_broadcast([P, PH, TOPK, TOPK]), ALU.mult)\
                    .then_inc(dve_own, 1)
                dve.wait_ge(dve_own, n(dve_own))
                dve.tensor_reduce(pick, work[:, 0:2048].rearrange("p (m j) -> p m j", j=TOPK), AX.X, ALU.add)\
                    .then_inc(dve_own, 1)
                dve.wait_ge(dve_own, n(dve_own))

            def a_part(k, last):
                for h in range(HEADS):
                    b = HEAD0 + HEADW * h
                    if k == b + 1:
                        scale_mask(h, last)
                    if k == b + 3:
                        combine(last)
                if last:
                    for g in range(SEQS // GRP):
                        sample(k, g, SAMP0 + SAMPW * g)
                d = after_attention(last)
                if k == d + 1:
                    if not last:
                        dve.wait_ge(a_used, n(a_used))
                    dve.wait_ge(att_raw, n(att_raw))
                    dve.tensor_tensor(e1[:, 0:ATT], att[:, :], att[:, :], ALU.mult).then_inc(dve_own, 1)
                    dve.wait_ge(dve_own, n(dve_own))
                    dve.tensor_reduce(ss4, e1[:, 0:ATT].rearrange("p (h n) -> p h n", h=HEADS), AX.X, ALU.add)\
                        .then_inc(ss4_ready, 1)
                if k == d + 3:
                    dve.wait_ge(rs4_ready, n(rs4_ready))
                    dve.reciprocal(rs4, rs4).then_inc(dve_own, 1)
                    dve.wait_ge(dve_own, n(dve_own))
                    a3 = att[:, :].rearrange("p (h n) -> p h n", h=HEADS)
                    dve.tensor_tensor(a3, a3, rs4.unsqueeze(2).to_broadcast([P, HEADS, P]), ALU.mult)\
                        .then_inc(att_ready, 1)
                if k == d + 7:
                    dve.wait_ge(x1_in, n(x1_in, 16))
                    dve.wait_ge(proj_ready, n(proj_ready))
                    dve.tensor_tensor(x1n, x1n, S0[:, :], ALU.add).then_inc(dve_own, 1)
                    dve.wait_ge(dve_own, n(dve_own))
                    dve.sem_inc(s_free, 1)
                    dve.sem_inc(x1_ready, 1)
                    dve.sem_inc(x1_sq, 1)
                if k == d + 9:
                    dve.wait_ge(rs2_ready, n(rs2_ready))
                    dve.reciprocal(r2, rs2).then_inc(dve_own, 1)
                    dve.wait_ge(dve_own, n(dve_own))
                    dve.sem_inc(r2_ready, 1)
                for j in range(8):
                    if k == d + 15 + 2 * j:
                        if j % 2 == 0:
                            dve.wait_ge(sc_ready, n(sc_ready))
                        top16(sv, si, scores, (2 * j, 2 * j + 1))
                if k == d + 31:
                    dve.tensor_copy(sif, si).then_inc(dve_own, 1)
                    dve.wait_ge(dve_own, n(dve_own))
                    sv4 = sv.rearrange("p (h c) k -> p h c k", c=2)
                    dve.tensor_tensor(cand.rearrange("p h (a b) -> p h a b", a=TOPK),
                                      sv4[:, :, 0, :].unsqueeze(3).to_broadcast([P, PH, TOPK, TOPK]),
                                      sv4[:, :, 1, :].unsqueeze(2).to_broadcast([P, PH, TOPK, TOPK]), ALU.add)\
                        .then_inc(dve_own, 1)
                    dve.wait_ge(dve_own, n(dve_own))
                for j in range(4):
                    if k == d + 33 + 4 * j:
                        top16(tv, tpos, cand, (2 * j, 2 * j + 1))
                if k == d + 49:
                    tp = qpw[:, 896:1024].bitcast(U32)
                    dve.tensor_scalar(idx_n[:, :].bitcast(U32), tp, 4, None, ALU.logical_shift_right)\
                        .then_inc(dve_own, 1)
                    dve.wait_ge(dve_own, n(dve_own))
                    dve.tensor_copy(posa, idx_n[:, :].bitcast(U32)).then_inc(dve_own, 1)
                    dve.wait_ge(dve_own, n(dve_own))
                    dve.tensor_scalar(idx_n[:, :].bitcast(U32), tp, TOPK - 1, None, ALU.bitwise_and)\
                        .then_inc(dve_own, 1)
                    dve.wait_ge(dve_own, n(dve_own))
                    dve.tensor_copy(posb, idx_n[:, :].bitcast(U32)).then_inc(dve_own, 1)
                    dve.wait_ge(dve_own, n(dve_own))
                if k == d + 50:
                    lookup(pick1, posa, 0)
                if k == d + 52:
                    lookup(pick2, posb, 1)
                    dve.scalar_tensor_tensor(pick1, pick1, float(NK), pick2, ALU.mult, ALU.add).then_inc(dve_own, 1)
                    dve.wait_ge(dve_own, n(dve_own))
                    dve.tensor_copy(idx_n[:, :], pick1).then_inc(dve_own, 1)
                    dve.wait_ge(dve_own, n(dve_own))
                if k == d + 54:
                    g3 = gate_n[:, :].rearrange("p (h k) -> p h k", h=PH)
                    dve.tensor_tensor(g3, tv, tv[:, :, 0:1].to_broadcast([P, PH, TOPK]), ALU.subtract)\
                        .then_inc(dve_own, 1)
                    dve.wait_ge(dve_own, n(dve_own))
                    dve.sem_inc(gexp_in, 1)
                if k == d + 56:
                    dve.wait_ge(gexp_out, n(gexp_out))
                    g3 = gate_n[:, :].rearrange("p (h k) -> p h k", h=PH)
                    dve.tensor_reduce(gsum, g3, AX.X, ALU.add).then_inc(dve_own, 1)
                    dve.wait_ge(dve_own, n(dve_own))
                    dve.reciprocal(grec, gsum).then_inc(dve_own, 1)
                    dve.wait_ge(dve_own, n(dve_own))
                    dve.tensor_tensor(g3, g3, grec.unsqueeze(2).to_broadcast([P, PH, TOPK]), ALU.mult)\
                        .then_inc(dve_own, 1)
                    dve.wait_ge(dve_own, n(dve_own))
                    dve.sem_inc(a_over, 1)

            def promote_lo():
                dve.tensor_copy(idx_c[:, 0:PICKS // 2], idx_n[:, 0:PICKS // 2]).then_inc(dve_own, 1)
                dve.wait_ge(dve_own, n(dve_own))
                dve.sem_inc(idx_lo, 1)

            def promote():
                dve.tensor_copy(idx_c[:, PICKS // 2:], idx_n[:, PICKS // 2:]).then_inc(dve_own, 1)
                dve.wait_ge(dve_own, n(dve_own))
                dve.sem_inc(idx_hi, 1)
                dve.tensor_copy(gate_c[:, :], gate_n[:, :]).then_inc(dve_own, 1)
                dve.scalar_tensor_tensor(h2c[:, :], x1n, r2, g2w[:, :], ALU.mult, ALU.mult).then_inc(dve_own, 1)
                dve.wait_ge(dve_own, n(dve_own, 2))

            def g_step(t, k, r):
                s = k % SLOTS
                dve.wait_ge(landed[s], t * (16 * PICKS // SLOTS) + 16 * (k // SLOTS + 1))
                dve.tensor_tensor_reduce(out=ring[0:r, s, 0:D], in0=ring[0:r, s, 0:D], in1=h2c[0:r, :], scale=1.0,
                                         scalar=0.0, op0=ALU.mult, op1=ALU.add,
                                         accum_out=dots[0:r, s:s + 1]).then_inc(dot_ready, 1)
                if k == 3:
                    dve.wait_ge(x1c_free, n(x1c_free))
                    dve.tensor_copy(x1c[:, :], x1n).then_inc(dve_own, 1)
                    dve.wait_ge(dve_own, n(dve_own))

            def finish(r):
                dve.wait_ge(y_ready, n(y_ready))
                dve.tensor_tensor(x1c[0:r, :], x1c[0:r, :], Y[0:r, :], ALU.add).then_inc(dve_own, 1)
                dve.wait_ge(dve_own, n(dve_own))
                dve.sem_inc(y_free, 1)
                dve.sem_inc(slot_free, 1)
                dve.sem_inc(y_store, 1)

            for k in range(PICKS):
                a_part(k, False)
            promote_lo()
            n.settle()
            with dve.Fori(0, LAST - 1) as t:
                promote()
                for k in range(PICKS):
                    g_step(t, k, P)
                    if k == 3:
                        dve.sem_inc(x1n_free, 1)
                    a_part(k, False)
                    if k == 100:
                        promote_lo()
                finish(P)
                n.settle()
            promote()
            for k in range(PICKS):
                g_step(LAST - 1, k, P)
                a_part(k, True)
            finish(P)
            promote_lo()
            promote()
            for k in range(PICKS):
                g_step(LAST, k, ROWS8)
            finish(ROWS8)


def rotary_table():
    pos = np.zeros(TILES * P)
    pos[:META + SEQ] = np.arange(META + SEQ)
    pos[META + SEQ:LAST * P + ROWS8] = PAST + np.arange(SEQS * NEW) % NEW
    inv = (np.float32(500000.0) ** (-np.arange(0, ROPE, 2, dtype=np.float32) / ROPE)).astype(np.float32)
    ang = (pos.astype(np.float32)[:, None] * inv[None, :]).astype(np.float64)
    return np.concatenate([np.cos(ang), np.sin(ang)], 1).astype(np.float32).reshape(TILES, P, ROPE)


def pool_tables():
    cur = np.zeros((TILES, P, 2, 4, P), np.float32)
    old = np.zeros((SEQS, STATE, 4, P), np.float32)
    for g, w in enumerate(WINDOWS):
        for t in range(TILES):
            for p in range(P if t < LAST else TAIL):
                pos = t * P + p
                for q in range(max(0, pos - w + 1), pos + 1):
                    cur[t, q % P, 0 if q // P == t else 1, g, p] += np.float32(1.0) / np.float32(min(pos + 1, w))
                cur[t, p, 0, g, p] -= 1
        for b in range(SEQS):
            for s in range(NEW):
                p = TAIL + NEW * b + s
                for q in range(s - w + 1, s + 1):
                    if q >= 0:
                        cur[LAST, TAIL + NEW * b + q, 0, g, p] += 1.0 / w
                    else:
                        old[b, STATE + q, g, p] += 1.0 / w
                cur[LAST, p, 0, g, p] -= 1
    return cur.reshape(TILES, P, 1024), old.reshape(SEQS * STATE, 512)


def masks(bf16):
    full = np.full((TILES, P, KEYS), NEG, np.float32)
    for t in range(TILES):
        for p in range(P):
            full[t, p, :t * P + p + 1] = 0
    extra = np.full((P, ROWS8), NEG, np.float32)
    for p in range(TAIL):
        extra[p, :p + 1] = 0
    sample = np.full((SEQS // GRP, P, SW), NEG, np.float32)
    sample[:, :, :PAST] = 0
    for g in range(SEQS // GRP):
        for r in range(P):
            b, s = GRP * g + r // 32, r % NEW
            lo = PAST + TAIL + NEW * b
            sample[g, r, lo:lo + s + 1] = 0
    return full.astype(bf16), extra, sample


def kernel(x_prompt, x_sample, cache_k, cache_v, state_pool, page_table, meta_tokens, norm1_g, w_in,
           q_norm_g, k_norm_g, lambda_q1, lambda_k1, lambda_q2, lambda_k2, subln_g, w_pool, b_pool,
           pool_scale, w_out, norm2_g, w_query, sub_keys, w_u, w_v):
    import ml_dtypes
    import concourse.bacc as bacc
    from concourse.bass_utils import run_bass_kernel_spmd

    a = {k: np.asarray(v) for k, v in dict(
        x_prompt=x_prompt, x_sample=x_sample, cache_k=cache_k, cache_v=cache_v, state_pool=state_pool,
        page_table=page_table, meta_tokens=meta_tokens, norm1_g=norm1_g, w_in=w_in, q_norm_g=q_norm_g,
        k_norm_g=k_norm_g, lambda_q1=lambda_q1, lambda_k1=lambda_k1, lambda_q2=lambda_q2,
        lambda_k2=lambda_k2, subln_g=subln_g, w_pool=w_pool, b_pool=b_pool, pool_scale=pool_scale,
        w_out=w_out, norm2_g=norm2_g, w_query=w_query, sub_keys=sub_keys, w_u=w_u, w_v=w_v).items()}

    def wide(row):
        return np.broadcast_to(row.reshape(1, -1), (P, row.size))

    x = np.zeros((TILES * P, D), np.float32)
    x[:META] = a["meta_tokens"]
    x[META:META + SEQ] = a["x_prompt"][0]
    x[META + SEQ:LAST * P + ROWS8] = a["x_sample"].reshape(-1, D)
    x = x.reshape(TILES, P, D)
    mt, mst = pool_tables()
    mask, mext, msam = masks(ml_dtypes.bfloat16)
    rows01 = np.zeros((P, 3), np.float32)
    rows01[:TAIL, 0] = 1
    comp = np.arange(P) // NEW % 2
    rows01[:, 1], rows01[:, 2] = comp == 0, comp == 1
    n_pool = a["cache_k"].shape[1]
    ins = dict(
        x=x,
        xT=x.reshape(TILES, P, DC, P).transpose(0, 3, 2, 1).reshape(TILES, P, D),
        g1T=a["norm1_g"].reshape(DC, P).T,
        w_in=a["w_in"][0].reshape(DC, P, INW),
        gqk=np.concatenate([wide(np.tile(a["q_norm_g"], 8)), wide(np.tile(a["k_norm_g"], 8))], 1),
        cs=rotary_table(), mt=mt, mst=mst,
        state=a["state_pool"][0].reshape(SEQS * STATE, 512),
        w_pool=a["w_pool"][0].transpose(1, 0, 2).reshape(P, 512),
        b_poolT=a["b_pool"][0].T, scaleT=a["pool_scale"].reshape(4, P).T,
        wqT=a["w_query"][0].T.reshape(GROUPS, P, D),
        skT=a["sub_keys"][0].reshape(GROUPS, NK, P).transpose(2, 0, 1),
        g2T=a["norm2_g"].reshape(DC, P).T, g2b=wide(a["norm2_g"]),
        lams=np.concatenate([wide(a[k]) for k in ("lambda_q1", "lambda_k1", "lambda_q2", "lambda_k2")], 1),
        rows01=rows01, w_out=a["w_out"][0], subT=a["subln_g"].reshape(P, 1),
        mask=mask, mext=mext, msam=msam,
        ktc=a["cache_k"][0].transpose(0, 3, 2, 1).reshape(n_pool, P, HEADS * PAGE),
        vc=a["cache_v"][0].reshape(n_pool, PAGE, HEADS * P),
        pages=a["page_table"].reshape(1, -1),
        wuv=np.concatenate([a["w_u"][0], a["w_v"][0]], 1),
        iota=wide(np.arange(TOPK, dtype=np.float32)),
    )
    outs = dict(y_all=(TILES, P, D), k_all=(TILES, P, 512), v_all=(TILES, P, 512), p_last=(ROWS8, 512),
                state_old=(SEQS, STATE - NEW, 512))
    nc = bacc.Bacc("TRN2", target_bir_lowering=False, num_devices=1)
    args, arrays = [], {}
    for name, v in ins.items():
        arrays["in_" + name] = v = np.ascontiguousarray(v)
        args.append(nc.dram_tensor("in_" + name, v.shape, mybir.dt.from_np(v.dtype), kind="ExternalInput").ap())
    for name, shape in outs.items():
        args.append(nc.dram_tensor("out_" + name, shape, F32, kind="ExternalOutput").ap())
    build(nc, *args)
    res = run_bass_kernel_spmd(nc, [arrays], core_ids=[0]).results[0]
    y, k, v = (res["out_" + m].reshape(TILES * P, -1) for m in ("y_all", "k_all", "v_all"))
    p_new = res["out_p_last"]
    n_p, n_all = META + SEQ, LAST * P + ROWS8
    return (y[META:n_p].reshape(1, SEQ, D), y[n_p:n_all].reshape(SEQS, NEW, D),
            k[:n_p].reshape(1, 1, n_p, HEADS, P), v[:n_p].reshape(1, 1, n_p, HEADS, P),
            p_new[TAIL - STATE:TAIL].reshape(1, 1, STATE, 512),
            k[n_p:n_all].reshape(1, SEQS, NEW, HEADS, P), v[n_p:n_all].reshape(1, SEQS, NEW, HEADS, P),
            np.concatenate([res["out_state_old"], p_new[TAIL:].reshape(SEQS, NEW, 512)], 1)[None])
```

```python
import math
from contextlib import ExitStack

import concourse.bass as bass
from concourse import mybir
import numpy as np

F32 = mybir.dt.float32
BF16 = mybir.dt.bfloat16
I32 = mybir.dt.int32
U32 = mybir.dt.uint32
ALU = mybir.AluOpType
ACT = mybir.ActivationFunctionType
AX = mybir.AxisListType

P = 128
D = 1024
DC = D // P
ATT = 512
HEADS = 4
QK = 64
ROPE = QK // 4
HALF = ROPE // 2
INW = 3 * ATT + 512
META = 16
SEQ = 1024
SEQS = 8
NEW = 4
PAST = 256
PAGE = 128
PAGES = PAST // PAGE
TILES = 9
LAST = TILES - 1
TAIL = META + SEQ - LAST * P
ROWS8 = TAIL + SEQS * NEW
KEYS = LAST * P
KTW = KEYS + ROWS8
WINDOWS = (2, 4, 8, 16)
STATE = 15
PH = 8
NK = 128
TOPK = 16
GROUPS = 2 * PH
PICKS = PH * TOPK
NEXP = NK * NK
EPS = 1e-6
NEG = -1e30
LAM_INIT = 0.8 - 0.6 * math.exp(-0.3 * 0)
SLOTS = 5
GRP = 4
SW = PAST + ROWS8

FOLD = 64
ROWSF = FOLD + ROWS8


class Plan:

    def __init__(self, last):
        self.head0, self.headw = 1, 6 if last else 9
        self.scores = (0, 0, 1, 1) if last else (0, 1, 2, 3)
        self.scale = (2, 2) if last else (3, 4)
        self.exp = (2, 2) if last else (3, 5)
        self.combine = (3, 3) if last else (6, 7)
        self.flip = (4, 5) if last else (8, 9)
        self.values = (6, 6, 6, 6) if last else (10, 11, 12, 13)
        self.sample0, self.samplew = 27, 20
        self.att = 67 if last else 42
        self.squares, self.norm, self.flip_att = self.att + 1, self.att + 3, self.att + 4
        self.pace = 4 if last else 1
        self.project = self.flip_att + 1
        self.x1 = self.project + 2 * DC // self.pace
        self.flip_x1 = (self.x1 + 1, self.x1 + 2)
        self.r2 = self.x1 + 2
        self.route = self.x1 + 3
        self.take = [self.route + (q + 1) * DC // self.pace for q in range(4)]
        self.top = self.take[0] + 1
        self.top_pace = 2 if last else 1
        self.gate = self.top + 4 * TOPU // self.top_pace

    def head(self, k, at, h):
        return [i for i, a in enumerate(at) if k == self.head0 + self.headw * h + a]

    @staticmethod
    def run(k, start, total, pace):
        return range(max(0, (k - start) * pace), max(0, min(total, (k - start + 1) * pace)))


TOPU = 10
PROMOTE = PICKS - 10
PLANS = {last: Plan(last) for last in (False, True)}


class Counter:

    def __init__(self, eng):
        self.eng, self.count = eng, {}

    def __call__(self, sem, more=1):
        self.count[sem] = self.count.get(sem, 0) + more
        return self.count[sem]

    def settle(self):
        for sem, n in self.count.items():
            self.eng.sem_inc(sem, -n)
        self.count = {}


def build(nc, x, xT, g1T, w_in, gqk, cs, mt, mst, state, w_pool, b_poolT, scaleT, wqT, skT, g2T, g2b, lams,
          rows01, w_out, subT, mask, mext, msam, ktc, vc, pages, wuv, iota,
          y_all, k_all, v_all, p_last, state_old):
    with ExitStack() as ctx:
        def sb(name, n, dt=F32):
            return ctx.enter_context(nc.sbuf_tensor(name, [P, n], dt))

        def pb(name, n):
            return ctx.enter_context(nc.psum_tensor(name, [P, n], F32))

        def sem(name):
            return ctx.enter_context(nc.semaphore(name))

        qp_dram = nc.dram_tensor("qp_dram", [TILES, P, 1024], F32).ap()

        big1 = sb("big1", 16384)
        big2 = sb("big2", 16384)
        KT = sb("KT", HEADS * KTW)
        V = sb("V", TILES * ATT)
        work = sb("work", 4096)
        h2c = sb("h2c", D)
        g2w = sb("g2w", D)
        maskw = sb("maskw", 512)
        qpw = sb("qpw", 1024)
        slot5 = sb("slot5", 2 * D)
        ext = sb("ext", 2 * ROWS8 + P)
        emask = sb("emask", ROWS8)
        ident = sb("ident", P)
        fold_id = sb("fold_id", ROWS8)
        diag = sb("diag", SLOTS * P)
        idx_n = sb("idx_n", PICKS, I32)
        idx_c = sb("idx_c", PICKS, I32)
        gate_n = sb("gate_n", PICKS)
        gate_c = sb("gate_c", PICKS)
        dots = sb("dots", SLOTS)
        gel = sb("gel", SLOTS)
        amp = sb("amp", SLOTS)
        iota16 = sb("iota16", TOPK)
        sm = sb("sm", P)
        pt = sb("pt", SEQS * PAGES, I32)

        w_in_sb = big1[:, :].rearrange("p (c n) -> p c n", c=DC)
        wqT_sb = big1[:, :].rearrange("p (j n) -> p j n", j=GROUPS)
        w_out_sb = big1[:, 0:8192].rearrange("p (c n) -> p c n", c=DC)
        ring = [big1[:, 8192 + 2048 * i:8192 + 2048 * (i + 1)] for i in range(4)] + [slot5[:, :]]
        att = maskw
        w_route = big2[:, :].rearrange("p (c n) -> p c n", c=DC)
        KT3 = KT[:, :].rearrange("p (h n) -> p h n", h=HEADS)
        V3 = V[:, :].rearrange("p (t n) -> p t n", t=TILES)

        def part(lo, n):
            return big2[:, lo:lo + n]
        hxT = [part(0, 1024), part(1024, 1024)]
        hx = [part(2048, 1024), part(3072, 1024)]
        hqk = [part(4096, 1024), part(5120, 1024)]
        hsq = part(6144, 1024)
        hgqk = part(7168, 1024)
        hp = [part(8192, 512), part(8704, 512)]
        hdT = part(9216, 512)
        hqp = [part(9728, 1024), part(10752, 1024)]
        hmt = [part(11776, 1024), part(12800, 1024)]
        hcs = [part(13824, ROPE), part(13840, ROPE)]
        hwp = part(13856, 512)
        hst = part(14368, 512)
        hmst = part(14880, 512)
        hrope = part(15392, 512)
        hg1 = part(15904, DC)

        e0, e1, aT, x1n = (work[:, a:a + 1024] for a in (0, 1024, 2048, 3072))
        scores = work[:, 0:2048].rearrange("p (g n) -> p g n", g=GROUPS)
        cand = work[:, 0:2048].rearrange("p (h n) -> p h n", h=PH)
        onehot = work[:, 0:2048].rearrange("p (h k j) -> p h k j", h=PH, k=TOPK)
        skT_sb = work[:, 0:2048].rearrange("p (j n) -> p j n", j=GROUPS)
        qT = qpw[:, 0:512].rearrange("p (h n) -> p h n", h=HEADS)
        pyT = qpw[:, 512:1024].rearrange("p (g n) -> p g n", g=HEADS)
        sv = qpw[:, 0:256].rearrange("p (g k) -> p g k", g=GROUPS)
        si = qpw[:, 256:512].bitcast(U32).rearrange("p (g k) -> p g k", g=GROUPS)
        sif = qpw[:, 512:768].rearrange("p (g k) -> p g k", g=GROUPS)
        tv = qpw[:, 768:896].rearrange("p (h k) -> p h k", h=PH)
        tpos = qpw[:, 896:1024].bitcast(U32).rearrange("p (h k) -> p h k", h=PH)
        mask_sb = maskw[:, :].bitcast(BF16)
        posa, posb, pick1, pick2 = (maskw[:, a:a + PICKS] for a in (0, 128, 256, 384))
        ex0, ex1, exT = ext[:, 0:ROWS8], ext[:, ROWS8:2 * ROWS8], ext[:, 2 * ROWS8:]
        Kb = work[:, 0:1024].rearrange("p (g h n) -> p g h n", g=PAGES, h=HEADS)
        Vb = work[:, 0:1024].rearrange("p (g n) -> p g n", g=PAGES)
        Ps = work[:, 1024:1024 + SW]
        PT = work[:, 1536:1536 + 3 * P].rearrange("p (k n) -> p k n", k=3)
        QZ = work[:, 2048:2048 + P * (1 + HEADS)]
        AZ = work[:, 2048:2048 + P * (1 + 3 * HEADS)]
        msam_sb = maskw[:, 0:SW]

        def col(i, n=1):
            return sm[:, i:i + n]
        ss1, rs1, ss16, rs16 = col(0), col(1), col(4, 16), col(20, 16)
        eps = col(36)
        coef = col(38, 4)
        nmx = col(42, 4)
        sums = col(46, 4)
        rc = col(50, 2)
        ss4, rs4 = col(52, 4), col(56, 4)
        ss2, rs2, r2 = col(60), col(61), col(62)
        gsum, grec = col(64, 8), col(72, 8)
        snm, ssum, src, scoef = col(80), col(81), col(82), col(83)
        lamt = col(84, 4)
        bpT, scT, g2c, subc, r01 = col(88, 4), col(92, 4), col(96, 8), col(104), col(106, 3)
        nm = col(110, 2)

        Y = pb("Y", 1024)
        S0 = pb("S0", 1024)
        S1 = pb("S1", 1024)
        T = pb("T", 512)
        O = pb("O", 512)
        S = [S0, S1]
        zbank = [Y[:, 0:512], Y[:, 512:1024], S0[:, 0:512], S0[:, 512:1024]]
        qTp, kTp = S1[:, 0:512], S1[:, 512:1024]
        dTp, pyp = T[:, :], O[:, :]
        route_bank = [S0[:, 0:512], S0[:, 512:1024], S1[:, 0:512], S1[:, 512:1024]]

        pe_own, act_own, dve_own, pool_own = sem("pe_own"), sem("act_own"), sem("dve_own"), sem("pool_own")
        c_w_in = [sem(f"c_w_in{c}") for c in range(DC)]
        c_act = sem("c_act")
        c_dve = sem("c_dve")
        c_pool = sem("c_pool")
        c_pe = sem("c_pe")
        c_sp = sem("c_sp")
        ident_pe, ident_act = sem("ident_pe"), sem("ident_act")
        eps_ready = sem("eps_ready")
        p0_ready = sem("p0_ready")
        x_in = [sem("x_in0"), sem("x_in1")]
        xT_in = [sem("xT_in0"), sem("xT_in1")]
        mt_in = [sem("mt_in0"), sem("mt_in1")]
        cs_in = [sem("cs_in0"), sem("cs_in1")]
        in_free = sem("in_free")
        xg_ready = sem("xg_ready")
        z_ready = sem("z_ready")
        z_free = sem("z_free")
        sq_ready = sem("sq_ready")
        r1_ready = sem("r1_ready")
        qk_raw = sem("qk_raw")
        ss16_ready, rs16_ready = sem("ss16_ready"), sem("rs16_ready")
        qk_ready = sem("qk_ready")
        k_store = sem("k_store")
        v_store = sem("v_store")
        qp_store = sem("qp_store")
        stored = sem("stored")
        qk_free = sem("qk_free")
        p_ready = sem("p_ready")
        qTp_ready, qTp_free = sem("qTp_ready"), sem("qTp_free")
        kTp_ready, kTp_free = sem("kTp_ready"), sem("kTp_free")
        dTp_ready, dT_ready = sem("dTp_ready"), sem("dT_ready")
        py_ready, py_free = sem("py_ready"), sem("py_free")
        pe_done = sem("pe_done")
        head_pe = sem("head_pe")
        head_over = sem("head_over")
        wq_in = [sem(f"wq_in{i}") for i in range(4)]
        fold_ready, fold_free = sem("fold_ready"), sem("fold_free")
        folded = sem("folded")
        route_w = sem("route_w")
        wo_in, wo_ready = sem("wo_in"), sem("wo_ready")
        lam_ready, lam_done = sem("lam_ready"), sem("lam_done")
        a_over = sem("a_over")
        x1n_free = sem("x1n_free")
        mask_in = sem("mask_in")
        qp_in = sem("qp_in")
        x1_in = sem("x1_in")
        s_free = sem("s_free")
        s_ready = sem("s_ready")
        nm_ready, exp_ready = sem("nm_ready"), sem("exp_ready")
        a_ready, a_used = sem("a_ready"), sem("a_used")
        t_free, t_ready = sem("t_free"), sem("t_ready")
        t_evac = sem("t_evac")
        o_ready, o_free = sem("o_ready"), sem("o_free")
        att_raw = sem("att_raw")
        ss4_ready, rs4_ready = sem("ss4_ready"), sem("rs4_ready")
        att_ready = sem("att_ready")
        proj_ready = sem("proj_ready")
        x1_ready, x1_sq = sem("x1_ready"), sem("x1_sq")
        rs2_ready, r2_ready = sem("rs2_ready"), sem("r2_ready")
        route_ready, sc_ready = sem("route_ready"), sem("sc_ready")
        gexp_in, gexp_out = sem("gexp_in"), sem("gexp_out")
        e_free = sem("e_free")
        kv_in = sem("kv_in")
        msam_in, msam_free = sem("msam_in"), sem("msam_free")
        qz_ready, qz_free = sem("qz_ready"), sem("qz_free")
        pt_ready = sem("pt_ready")
        idx_lo, idx_hi = sem("idx_lo"), sem("idx_hi")
        slot_free = [sem(f"slot_free{s}") for s in range(SLOTS)]
        landed = [sem(f"landed{s}") for s in range(SLOTS)]
        dot_ready = sem("dot_ready")
        diag_ready = sem("diag_ready")
        y_ready = sem("y_ready")
        y_free = sem("y_free")
        y_store = sem("y_store")
        y_stored = sem("y_stored")
        x1n_read = sem("x1n_read")
        h2_ready = sem("h2_ready")

        block = ctx.enter_context(nc.Block())

        def tile_rows(t):
            return P if not isinstance(t, int) or t < LAST else ROWS8

        @block.sync
        def _(sp):
            n = Counter(sp)

            def head_load(t, par):
                sp.wait_ge(in_free, n(in_free))
                sp.dma_start(hxT[par], xT[t]).then_inc(xT_in[par], 16)
                sp.dma_start(hx[par], x[t]).then_inc(x_in[par], 16)
                sp.dma_start(hcs[par], cs[t]).then_inc(cs_in[par], 16)
                sp.dma_start(hmt[par], mt[t]).then_inc(mt_in[par], 16)

            def head_store(t, par):
                r = tile_rows(t)
                sp.wait_ge(k_store, n(k_store))
                sp.dma_start(k_all[t][0:r, :], hqk[par][0:r, 512:1024]).then_inc(stored, 16)
                sp.wait_ge(v_store, n(v_store))
                sp.dma_start(v_all[t][0:r, :], V3[0:r, t, :]).then_inc(stored, 16)
                if r < P:
                    sp.dma_start(p_last, hp[par][0:r, :]).then_inc(stored, 16)
                sp.wait_ge(qp_store, n(qp_store, 2))
                sp.dma_start(qp_dram[t], hqp[par]).then_inc(stored, 16)
                sp.wait_ge(stored, n(stored, 64 if r < P else 48))
                sp.sem_inc(qk_free, 1)

            sp.dma_start(hg1, g1T).then_inc(c_pool, 16)
            head_load(0, 0)
            for c in range(DC):
                sp.dma_start(w_in_sb[:, c, :], w_in[c]).then_inc(c_w_in[c], 16)
                if c == 1:
                    sp.dma_start(hgqk, gqk).then_inc(c_dve, 16)
                    sp.dma_start(bpT, b_poolT).then_inc(c_dve, 16)
                    sp.dma_start(scT, scaleT).then_inc(c_dve, 16)
                    sp.dma_start(g2c, g2T).then_inc(c_dve, 16)
                    sp.dma_start(subc, subT).then_inc(c_dve, 16)
                    sp.dma_start(r01, rows01).then_inc(c_dve, 16)
                    sp.dma_start(att[:, 0:256], lams).then_inc(c_dve, 16)
                    sp.dma_start(g2w[:, :], g2b).then_inc(c_dve, 16)
                    sp.dma_start(iota16[:, :], iota).then_inc(c_dve, 16)
                    sp.dma_start(hwp, w_pool).then_inc(c_pe, 16)
                    sp.dma_start(hst[0:SEQS * STATE, :], state).then_inc(c_pe, 16)
                    sp.dma_start(hmst[0:SEQS * STATE, :], mst).then_inc(c_pe, 16)
                    sp.dma_start(skT_sb, skT).then_inc(c_pe, 16)
                    sp.dma_start(pt[0:1, :], pages).then_inc(c_sp, 16)
            sp.dma_start(state_old, state.rearrange("(b j) n -> b j n", b=SEQS)[:, NEW:STATE, :]).then_inc(stored, 16)
            sp.wait_ge(stored, n(stored, 16))
            sp.wait_ge(c_sp, n(c_sp, 16))
            n.settle()
            with sp.Fori(0, LAST // 2) as j:
                head_load(2 * j + 1, 1)
                head_store(2 * j, 0)
                head_load(2 * j + 2, 0)
                head_store(2 * j + 1, 1)
                n.settle()
            head_store(LAST, 0)
            sp.sem_inc(head_over, 1)
            sp.wait_ge(head_pe, n(head_pe))
            for j in range(0, GROUPS, 4):
                sp.dma_start(wqT_sb[:, j:j + 4, :], wqT[j:j + 4].rearrange("j p n -> p j n")).then_inc(wq_in[j // 4], 16)
            sp.wait_ge(folded, n(folded))
            sp.dma_start(w_out_sb, w_out.rearrange("(c p) n -> p c n", p=P)).then_inc(wo_in, 16)

            def a_load(t):
                sp.wait_ge(a_over, n(a_over))
                sp.dma_start(mask_sb, mask[t]).then_inc(mask_in, 16)
                sp.dma_start(qpw[:, :], qp_dram[t]).then_inc(qp_in, 16)
                if isinstance(t, int) and t == LAST:
                    sp.dma_start(emask[:, :], mext).then_inc(mask_in, 16)
                    sample_load()
                sp.wait_ge(x1n_free, n(x1n_free))
                sp.dma_start(x1n, x[t]).then_inc(x1_in, 16)

            def sample_load():
                for g in range(SEQS // GRP):
                    sp.wait_ge(msam_free, n(msam_free))
                    sp.dma_start(msam_sb, msam[g]).then_inc(msam_in, 16)
                    for what in (ktc, vc):
                        for b in range(GRP * g, GRP * g + GRP):
                            sp.wait_ge(e_free, n(e_free))
                            for i in range(PAGES):
                                page = sp.value_load(pt[0:1, b * PAGES + i:b * PAGES + i + 1],
                                                     min_val=0, max_val=ktc.shape[0] - 1)
                                dst = Kb[:, i, :, :].rearrange("p h n -> p (h n)") if what is ktc else Vb[:, i, :]
                                sp.dma_start(dst, what[page]).then_inc(kv_in, 16)

            def y_out(t):
                r = tile_rows(t)
                sp.wait_ge(y_store, n(y_store))
                sp.dma_start(y_all[t][0:r, :], (aT if r == P else e0)[0:r, :]).then_inc(stored, 16)
                sp.wait_ge(stored, n(stored, 16))
                sp.sem_inc(y_stored, 1)

            a_load(0)
            n.settle()
            with sp.Fori(0, LAST - 1) as t:
                a_load(t + 1)
                y_out(t)
                n.settle()
            a_load(LAST)
            y_out(LAST - 1)
            y_out(LAST)

        @block.gpsimd
        def _(pool):
            n = Counter(pool)
            pool.memset(ident[:, :], 0.0).then_inc(pool_own, 1)
            pool.memset(hp[1], 0.0).then_inc(p0_ready, 1)
            pool.wait_ge(pool_own, n(pool_own))
            pool.affine_select(out=ident[:, :], in_=ident[:, :], compare_op=ALU.not_equal, fill=1.0,
                               base=0, pattern=[[-1, P]], channel_multiplier=1).then_inc(pool_own, 1)
            pool.wait_ge(pool_own, n(pool_own))
            pool.memset(fold_id[:, :], 0.0).then_inc(pool_own, 1)
            pool.wait_ge(pool_own, n(pool_own))
            for base in (0, -FOLD):
                pool.affine_select(out=fold_id[:, :], in_=fold_id[:, :], compare_op=ALU.not_equal, fill=1.0,
                                   base=base, pattern=[[-1, ROWS8]], channel_multiplier=1).then_inc(pool_own, 1)
                pool.wait_ge(pool_own, n(pool_own))
            pool.sem_inc(ident_pe, 1)
            pool.sem_inc(ident_act, 1)
            pool.wait_ge(c_pool, n(c_pool, 16))
            n.settle()

            def head(par):
                pool.wait_ge(xT_in[par], n(xT_in[par], 16))
                v = hxT[par].rearrange("p (c n) -> p c n", c=DC)
                pool.tensor_tensor(v, v, hg1.unsqueeze(2).to_broadcast([P, DC, P]), ALU.mult).then_inc(pool_own, 1)
                pool.wait_ge(pool_own, n(pool_own))
                pool.sem_inc(xg_ready, 1)

            with pool.Fori(0, LAST // 2):
                head(0)
                head(1)
                n.settle()
            head(0)
            pool.sem_inc(head_over, 1)
            n.settle()

            def gather(r, steps):
                for k in range(steps):
                    if k == 0:
                        pool.wait_ge(idx_lo, n(idx_lo))
                    if k == PICKS // 2 or steps < PICKS and k == 0:
                        pool.wait_ge(idx_hi, n(idx_hi))
                    pool.wait_ge(slot_free[k % SLOTS], n(slot_free[k % SLOTS]))
                    pool.indirect_dma_start(ring[k % SLOTS][0:r, :], None, wuv,
                                            bass.IndirectOffsetOnAxis(ap=idx_c[0:r, k:k + 1], axis=0)
                                            ).then_inc(landed[k % SLOTS], 16)
                n.settle()

            with pool.Fori(0, LAST):
                gather(P, PICKS)
            gather(ROWSF, PICKS // 2)

        @block.tensor
        def _(pe):
            n = Counter(pe)

            def head(par, first=False, last=False):
                pe.wait_ge(xg_ready, n(xg_ready))
                for q in range(4):
                    pe.wait_ge(z_free, n(z_free))
                    for c in range(DC):
                        if first and q == 0:
                            pe.wait_ge(c_w_in[c], n(c_w_in[c], 16))
                        mm = pe.matmul(zbank[q], hxT[par][:, c * P:(c + 1) * P],
                                       w_in_sb[:, c, q * 512:(q + 1) * 512], start=(c == 0), stop=(c == DC - 1))
                    mm.then_inc(z_ready, 1)
                pe.wait_ge(qk_ready, n(qk_ready))
                pe.wait_ge(qTp_free, n(qTp_free))
                for h in range(HEADS):
                    mm = pe.transpose(qTp[:, h * P:(h + 1) * P], hqk[par][:, h * P:(h + 1) * P], ident[:, :])
                mm.then_inc(qTp_ready, 1)
                pe.wait_ge(kTp_free, n(kTp_free))
                for h in range(HEADS):
                    mm = pe.transpose(kTp[:, h * P:(h + 1) * P], hqk[par][:, 512 + h * P:512 + (h + 1) * P], ident[:, :])
                mm.then_inc(kTp_ready, 1)
                pe.wait_ge(p_ready, n(p_ready))
                pe.wait_ge(mt_in[par], n(mt_in[par], 16))
                for g in range(4):
                    s = slice(g * P, (g + 1) * P)
                    pe.matmul(dTp[:, s], hp[par][:, s], hmt[par][:, s], start=True, stop=False)
                    mm = pe.matmul(dTp[:, s], hp[1 - par][:, s], hmt[par][:, 512 + g * P:512 + (g + 1) * P],
                                   start=False, stop=not last)
                    if last:
                        r = SEQS * STATE
                        mm = pe.matmul(dTp[:, s], hst[0:r, s], hmst[0:r, s], start=False, stop=True)
                mm.then_inc(dTp_ready, 1)
                pe.wait_ge(dT_ready, n(dT_ready))
                pe.wait_ge(py_free, n(py_free))
                for g in range(4):
                    s = slice(g * P, (g + 1) * P)
                    mm = pe.matmul(pyp[:, s], hwp[:, s], hdT[:, s], start=True, stop=True)
                mm.then_inc(py_ready, 1)
                pe.wait_ge(pe_done, n(pe_done))
                pe.sem_inc(in_free, 1)

            pe.wait_ge(ident_pe, n(ident_pe))
            pe.wait_ge(p0_ready, n(p0_ready))
            pe.wait_ge(c_pe, n(c_pe, 64))
            head(0, first=True)
            head(1)
            n.settle()
            with pe.Fori(1, LAST // 2):
                head(0)
                head(1)
                n.settle()
            head(0, last=True)
            pe.sem_inc(head_pe, 1)
            pe.sem_inc(head_over, 1)
            n.settle()

            for j in range(GROUPS):
                if j % 4 == 0:
                    pe.wait_ge(wq_in[j // 4], n(wq_in[j // 4], 16))
                pe.wait_ge(fold_free, n(fold_free))
                bank = S[j % 2]
                for c in range(DC):
                    mm = pe.matmul(bank[:, c * P:(c + 1) * P], wqT_sb[:, j, c * P:(c + 1) * P], skT_sb[:, j, :],
                                   start=True, stop=True)
                mm.then_inc(fold_ready, 1)
            pe.wait_ge(route_w, n(route_w))
            pe.sem_inc(folded, 1)
            pe.wait_ge(wo_ready, n(wo_ready))
            n.settle()

            def scores_of(h, u, last):
                c, m = divmod(u, 2)
                r = slice(QK * c, QK * c + QK)
                if h == 0 and u == 0:
                    pe.wait_ge(qp_in, n(qp_in, 16))
                if u == 0:
                    pe.wait_ge(s_free, n(s_free))
                    if last:
                        pe.wait_ge(t_free, n(t_free))
                mm = pe.matmul(S[c][:, m * 512:(m + 1) * 512], qT[r, h, :], KT3[r, h, m * 512:(m + 1) * 512],
                               start=True, stop=True)
                if last and m == 1:
                    mm = pe.matmul(T[:, c * ROWS8:(c + 1) * ROWS8], qT[r, h, :], KT3[r, h, KEYS:KTW],
                                   start=True, stop=True)
                    if c == 0:
                        mm.then_inc(pe_own, 1)
                        pe.wait_ge(pe_own, n(pe_own))
                if m == 1 and last and c == 1:
                    mm.then_inc(s_ready, 2)
                if m == 1 and not last:
                    mm.then_inc(s_ready, 1)

            def flip(m, last):
                if m == 0:
                    pe.wait_ge(a_ready, n(a_ready))
                pe.wait_ge(t_free, n(t_free))
                for i in range(4):
                    b = 4 * m + i
                    mm = pe.transpose(T[:, i * P:(i + 1) * P], e0[:, b * P:(b + 1) * P], ident[:, :])
                mm.then_inc(t_ready, 1)
                if m == 1 and last:
                    pe.wait_ge(t_free, n(t_free))
                    pe.transpose(T[0:ROWS8, 0:P], ex0, ident[:, :]).then_inc(t_ready, 1)

            def values(h, u, last):
                if u == 0:
                    pe.wait_ge(t_evac, n(t_evac, 3 if last else 2))
                    pe.sem_inc(a_used, 1)
                    if h == 0:
                        pe.wait_ge(o_free, n(o_free))
                for b in (2 * u, 2 * u + 1):
                    mm = pe.matmul(O[:, h * P:(h + 1) * P], aT[:, b * P:(b + 1) * P], V3[:, b, h * P:(h + 1) * P],
                                   start=(b == 0 and (h == 0 or not last)), stop=(b == LAST - 1) and not last,
                                   skip_group_check=True)
                if u == 3 and last:
                    mm = pe.matmul(O[:, h * P:(h + 1) * P], exT[0:ROWS8, :], V3[0:ROWS8, LAST, h * P:(h + 1) * P],
                                   start=False, stop=False, skip_group_check=True)
                    if h == HEADS - 1:
                        mm.then_inc(qz_free, 1)
                elif u == 3 and h == HEADS - 1:
                    mm.then_inc(o_ready, 1)

            def sample_scores(b):
                bl = b % GRP
                if bl == 0:
                    pe.wait_ge(s_free, n(s_free))
                pe.wait_ge(qz_ready, n(qz_ready))
                pe.wait_ge(kv_in, n(kv_in, 32))
                for h in range(HEADS):
                    lo = P + P * h - (bl * 32 + h * 8)
                    w = QZ[:, lo:lo + P]
                    a, z = (bl == 0 and h == 0), (bl == GRP - 1 and h == HEADS - 1)
                    for i in range(PAGES):
                        pe.matmul(S0[:, i * P:(i + 1) * P], w, Kb[:, i, h, :], start=a and i == 0, stop=z, skip_group_check=True)
                    mm = pe.matmul(S1[:, 0:ROWS8], w, KT3[:, h, KEYS:KTW], start=a, stop=z, skip_group_check=True)
                mm.then_inc(qz_free, 1)

            def sample_flip():
                pe.wait_ge(a_ready, n(a_ready))
                pe.wait_ge(t_free, n(t_free))
                pe.transpose(T[:, 0:P], Ps[:, 0:P], ident[:, :])
                pe.transpose(T[:, P:2 * P], Ps[:, P:2 * P], ident[:, :])
                pe.transpose(T[0:ROWS8, 2 * P:3 * P], Ps[:, 2 * P:SW], ident[:, :]).then_inc(t_ready, 1)

            def sample_values(b):
                pe.wait_ge(qz_ready, n(qz_ready))
                pe.wait_ge(kv_in, n(kv_in, 32))
                for h in range(HEADS):
                    z = b == SEQS - 1
                    for i in range(3):
                        lo = P + P * (HEADS * i + h) - (TAIL + NEW * b)
                        if i < PAGES:
                            w, v = AZ[:, lo:lo + P], Vb[:, i, h * P:(h + 1) * P]
                        else:
                            w, v = AZ[0:ROWS8, lo:lo + P], V3[0:ROWS8, LAST, h * P:(h + 1) * P]
                        mm = pe.matmul(O[:, h * P:(h + 1) * P], w, v, start=False, stop=z and i == 2,
                                       skip_group_check=True)
                mm.then_inc(qz_free, 1)

            def flip_att():
                pe.wait_ge(att_ready, n(att_ready))
                pe.wait_ge(t_free, n(t_free))
                for h in range(HEADS):
                    mm = pe.transpose(T[:, h * P:(h + 1) * P], att[:, h * P:(h + 1) * P], ident[:, :])
                mm.then_inc(t_ready, 1)

            def project(u):
                c, m = divmod(u, 2)
                if u == 0:
                    pe.wait_ge(t_evac, n(t_evac))
                    pe.wait_ge(s_free, n(s_free))
                lhs = aT[:, c * P:(c + 1) * P] if c < HEADS else pyT[:, c - HEADS, :]
                mm = pe.matmul(S0[:, m * 512:(m + 1) * 512], lhs, w_out_sb[:, c, m * 512:(m + 1) * 512],
                               start=(c == 0), stop=(c == DC - 1), skip_group_check=True)
                if u == 2 * DC - 1:
                    mm.then_inc(proj_ready, 1)

            def flip_x1(m):
                if m == 0:
                    pe.wait_ge(x1_ready, n(x1_ready))
                pe.wait_ge(t_free, n(t_free))
                for i in range(4):
                    b = 4 * m + i
                    mm = pe.transpose(T[:, i * P:(i + 1) * P], x1n[:, b * P:(b + 1) * P], ident[:, :])
                mm.then_inc(t_ready, 1)

            def route(u):
                q, c = divmod(u, DC)
                if u == 0:
                    pe.wait_ge(t_evac, n(t_evac, 2))
                    pe.wait_ge(s_free, n(s_free))
                mm = pe.matmul(route_bank[q], aT[:, c * P:(c + 1) * P], w_route[:, c, q * 512:(q + 1) * 512],
                               start=(c == 0), stop=(c == DC - 1), skip_group_check=True)
                if c == DC - 1:
                    mm.then_inc(route_ready, 1)

            def a_part(k, last):
                at = PLANS[last]
                for h in range(HEADS):
                    for u in at.head(k, at.scores, h):
                        scores_of(h, u, last)
                    for m in at.head(k, at.flip, h):
                        flip(m, last)
                    for u in at.head(k, at.values, h):
                        values(h, u, last)
                if last:
                    for g in range(SEQS // GRP):
                        s = at.sample0 + at.samplew * g
                        for i in range(GRP):
                            if k == s + 2 * i + 1:
                                sample_scores(GRP * g + i)
                            if k == s + 12 + 2 * i + 1:
                                sample_values(GRP * g + i)
                        if k == s + 10:
                            sample_flip()
                if k == at.flip_att:
                    flip_att()
                for u in at.run(k, at.project, 2 * DC, at.pace):
                    project(u)
                for m in range(2):
                    if k == at.flip_x1[m]:
                        flip_x1(m)
                for u in at.run(k, at.route, 4 * DC, at.pace):
                    route(u)

            def g_step(k, r, steps):
                if k == 0:
                    pe.wait_ge(y_free, n(y_free))
                    pe.wait_ge(h2_ready, n(h2_ready))
                    for m in range(2):
                        mm = pe.matmul(Y[:, m * 512:(m + 1) * 512], ident[:, :], x1n[:, m * 512:(m + 1) * 512],
                                       start=True, stop=False, skip_group_check=True)
                    mm.then_inc(x1n_read, 1)
                pe.wait_ge(diag_ready, n(diag_ready))
                s = k % SLOTS
                w = P if r == P else ROWS8
                for m in range(2):
                    mm = pe.matmul(Y[0:w, m * 512:(m + 1) * 512], diag[0:r, s * P:s * P + w],
                                   ring[s][0:r, D + m * 512:D + (m + 1) * 512],
                                   start=False, stop=(k == steps - 1), skip_group_check=True)
                mm.then_inc(slot_free[s] if k < steps - 1 else y_ready, 1)

            for k in range(PICKS):
                a_part(k, False)
            n.settle()
            with pe.Fori(0, LAST - 1):
                for k in range(PICKS):
                    g_step(k, P, PICKS)
                    a_part(k, False)
                n.settle()
            for k in range(PICKS):
                g_step(k, P, PICKS)
                a_part(k, True)
            for k in range(PICKS // 2):
                g_step(k, ROWSF, PICKS // 2)

        @block.scalar
        def _(act):
            n = Counter(act)
            act.sem_inc(z_free, 4)
            act.sem_inc(qTp_free, 1)
            act.sem_inc(t_free, 1)
            act.sem_inc(o_free, 1)
            act.wait_ge(eps_ready, n(eps_ready))
            n.settle()

            def head(par, t):
                act.wait_ge(x_in[par], n(x_in[par], 16))
                act.activation(hx[par], hx[par], ACT.Square, accum_out=ss1).then_inc(act_own, 1)
                act.wait_ge(act_own, n(act_own))
                act.activation(rs1, ss1, ACT.Sqrt, scale=1.0 / D, bias=eps).then_inc(sq_ready, 1)
                act.wait_ge(r1_ready, n(r1_ready))
                act.wait_ge(qk_free, n(qk_free))
                for q in range(4):
                    act.wait_ge(z_ready, n(z_ready))
                    dst = [hqk[par][:, 0:512], hqk[par][:, 512:1024], V3[:, t, :], hp[par]][q]
                    act.activation(dst, zbank[q], ACT.Copy, scale=rs1).then_inc(act_own, 1)
                    act.wait_ge(act_own, n(act_own))
                    act.sem_inc(z_free, 1)
                    if q == 1:
                        act.sem_inc(qk_raw, 1)
                    if q == 2:
                        act.wait_ge(ss16_ready, n(ss16_ready))
                        act.activation(rs16, ss16, ACT.Sqrt, scale=1.0 / QK, bias=eps).then_inc(rs16_ready, 1)
                act.sem_inc(p_ready, 1)
                act.sem_inc(v_store, 1)
                act.wait_ge(qTp_ready, n(qTp_ready))
                act.activation(hqp[par][:, 0:512], qTp, ACT.Copy).then_inc(act_own, 1)
                act.wait_ge(act_own, n(act_own))
                act.sem_inc(qTp_free, 1)
                act.sem_inc(qp_store, 1)
                act.wait_ge(dTp_ready, n(dTp_ready))
                act.activation(hdT, dTp, ACT.Copy).then_inc(dT_ready, 1)

            with act.Fori(0, LAST // 2) as j:
                head(0, 2 * j)
                head(1, 2 * j + 1)
                n.settle()
            head(0, LAST)
            n.settle()
            act.wait_ge(lam_ready, n(lam_ready))
            act.activation(lamt[:, 2:4], lamt[:, 0:2], ACT.Exp).then_inc(lam_done, 1)
            act.sem_inc(head_over, 1)
            act.wait_ge(ident_act, n(ident_act))
            n.settle()

            def exps(c, last):
                act.wait_ge(nm_ready, n(nm_ready))
                act.activation([e0, e1][c], [e0, e1][c], ACT.Exp, scale=-1.0, bias=nm[:, c:c + 1],
                               accum_out=sums[:, c:c + 1]).then_inc(act_own, 1)
                if last:
                    act.activation([ex0, ex1][c], [ex0, ex1][c], ACT.Exp, scale=-1.0, bias=nm[:, c:c + 1],
                                   accum_out=sums[:, 2 + c:3 + c]).then_inc(act_own, 1)
                act.wait_ge(act_own, n(act_own, 2 if last else 1))
                if c == 1:
                    act.sem_inc(exp_ready, 1)

            def evac(dst, src):
                act.wait_ge(t_ready, n(t_ready))
                act.activation(dst, src, ACT.Copy).then_inc(act_own, 1)
                act.wait_ge(act_own, n(act_own))
                act.sem_inc(t_free, 1)
                act.sem_inc(t_evac, 1)

            def a_part(k, last):
                at = PLANS[last]
                for h in range(HEADS):
                    for c in at.head(k, at.exp, h):
                        exps(c, last)
                    for m in at.head(k, at.flip, h):
                        if h == 0 and m == 0:
                            act.wait_ge(y_stored, n(y_stored))
                        evac(aT[:, m * 512:(m + 1) * 512], T[:, :])
                        if last and m == 1:
                            evac(exT[0:ROWS8, :], T[0:ROWS8, 0:P])
                if last:
                    for g in range(SEQS // GRP):
                        s = at.sample0 + at.samplew * g
                        if k == s + 9:
                            act.wait_ge(nm_ready, n(nm_ready))
                            act.activation(Ps, Ps, ACT.Exp, scale=-1.0, bias=snm, accum_out=ssum).then_inc(exp_ready, 1)
                        if k == s + 10:
                            act.wait_ge(t_ready, n(t_ready))
                            act.activation(PT[:, 0:2, :], T[:, 0:2 * P].rearrange("p (k n) -> p k n", k=2),
                                           ACT.Copy).then_inc(act_own, 1)
                            act.activation(PT[0:ROWS8, 2, :], T[0:ROWS8, 2 * P:3 * P], ACT.Copy).then_inc(act_own, 1)
                            act.wait_ge(act_own, n(act_own, 2))
                            act.sem_inc(t_free, 1)
                            act.sem_inc(pt_ready, 1)
                if k == at.att:
                    act.wait_ge(o_ready, n(o_ready))
                    act.activation(att[:, :], O[:, :], ACT.Copy).then_inc(act_own, 1)
                    act.wait_ge(act_own, n(act_own))
                    act.sem_inc(o_free, 1)
                    act.sem_inc(att_raw, 1)
                if k == at.squares + 1:
                    act.wait_ge(ss4_ready, n(ss4_ready))
                    act.activation(rs4, ss4, ACT.Sqrt, scale=1.0 / P, bias=eps).then_inc(rs4_ready, 1)
                if k == at.flip_att:
                    evac(aT[:, 0:512], T[:, :])
                if k == at.flip_x1[0]:
                    act.wait_ge(x1_sq, n(x1_sq))
                    act.activation(e0, x1n, ACT.Square, accum_out=ss2).then_inc(act_own, 1)
                    act.wait_ge(act_own, n(act_own))
                    act.activation(rs2, ss2, ACT.Sqrt, scale=1.0 / D, bias=eps).then_inc(rs2_ready, 1)
                    evac(aT[:, 0:512], T[:, :])
                if k == at.flip_x1[1]:
                    evac(aT[:, 512:1024], T[:, :])
                for q in range(4):
                    if k == at.take[q]:
                        if q == 0:
                            act.wait_ge(r2_ready, n(r2_ready))
                        act.wait_ge(route_ready, n(route_ready))
                        act.activation(work[:, q * 512:(q + 1) * 512], route_bank[q], ACT.Copy, scale=r2)\
                            .then_inc(act_own, 1)
                        act.wait_ge(act_own, n(act_own))
                        act.sem_inc(sc_ready, 1)
                        if q == 3:
                            act.sem_inc(s_free, 1)
                if k == at.gate + 1:
                    act.wait_ge(gexp_in, n(gexp_in))
                    act.activation(gate_n[:, :], gate_n[:, :], ACT.Exp).then_inc(gexp_out, 1)

            def g_step(k, r):
                s = k % SLOTS
                w = P if r == P else ROWS8
                act.wait_ge(dot_ready, n(dot_ready))
                act.activation(gel[0:r, s:s + 1], dots[0:r, s:s + 1], ACT.Gelu).then_inc(act_own, 1)
                act.wait_ge(act_own, n(act_own))
                act.activation(amp[0:r, s:s + 1], gel[0:r, s:s + 1], ACT.Copy, scale=gate_c[0:r, k:k + 1])\
                    .then_inc(act_own, 1)
                act.wait_ge(act_own, n(act_own))
                act.activation(diag[0:r, s * P:s * P + w], (ident if r == P else fold_id)[0:r, 0:w], ACT.Copy,
                               scale=amp[0:r, s:s + 1]).then_inc(diag_ready, 1)

            for k in range(PICKS):
                a_part(k, False)
            n.settle()
            with act.Fori(0, LAST - 1):
                for k in range(PICKS):
                    g_step(k, P)
                    a_part(k, False)
                n.settle()
            for k in range(PICKS):
                g_step(k, P)
                a_part(k, True)
            for k in range(PICKS // 2):
                g_step(k, ROWSF)

        @block.vector
        def _(dve):
            n = Counter(dve)

            dve.memset(eps, EPS).then_inc(dve_own, 1)
            dve.wait_ge(dve_own, n(dve_own))
            dve.sem_inc(eps_ready, 1)
            dve.sem_inc(in_free, 2)
            dve.sem_inc(qk_free, 2)
            dve.sem_inc(kTp_free, 1)
            dve.sem_inc(py_free, 1)
            dve.sem_inc(fold_free, 2)
            dve.sem_inc(s_free, 1)
            dve.sem_inc(y_free, 1)
            for s in range(SLOTS):
                dve.sem_inc(slot_free[s], 1)
            dve.sem_inc(y_stored, 2)
            dve.sem_inc(x1n_free, 1)
            dve.sem_inc(a_over, 1)
            dve.wait_ge(c_dve, n(c_dve, 9 * 16))
            for i in range(2):
                dve.tensor_tensor_reduce(out=att[:, i * 128:i * 128 + QK], in0=att[:, i * 128:i * 128 + QK],
                                         in1=att[:, i * 128 + QK:(i + 1) * 128], scale=1.0, scalar=0.0,
                                         op0=ALU.mult, op1=ALU.add, accum_out=lamt[:, i:i + 1]).then_inc(dve_own, 1)
                dve.wait_ge(dve_own, n(dve_own))
            dve.sem_inc(lam_ready, 1)
            n.settle()

            def head(par, t):
                dve.wait_ge(sq_ready, n(sq_ready))
                dve.reciprocal(rs1, rs1).then_inc(r1_ready, 1)
                dve.wait_ge(qk_raw, n(qk_raw))
                qk = hqk[par]
                qk3 = qk.rearrange("p (g n) -> p g n", g=16)
                dve.tensor_tensor(hsq, qk, qk, ALU.mult).then_inc(dve_own, 1)
                dve.wait_ge(dve_own, n(dve_own))
                dve.tensor_reduce(ss16, hsq.rearrange("p (g n) -> p g n", g=16), AX.X, ALU.add).then_inc(ss16_ready, 1)
                dve.wait_ge(rs16_ready, n(rs16_ready))
                dve.reciprocal(rs16, rs16).then_inc(dve_own, 1)
                dve.wait_ge(dve_own, n(dve_own))
                dve.tensor_tensor(qk3, qk3, rs16.unsqueeze(2).to_broadcast([P, 16, QK]), ALU.mult)\
                    .then_inc(dve_own, 1)
                dve.wait_ge(dve_own, n(dve_own))
                dve.tensor_tensor(qk, qk, hgqk, ALU.mult).then_inc(dve_own, 1)
                dve.wait_ge(dve_own, n(dve_own))
                dve.wait_ge(cs_in[par], n(cs_in[par], 16))
                a, b = qk3[:, :, 0:HALF], qk3[:, :, HALF:ROPE]
                cos = hcs[par][:, 0:HALF].unsqueeze(1).to_broadcast([P, 16, HALF])
                sin = hcs[par][:, HALF:ROPE].unsqueeze(1).to_broadcast([P, 16, HALF])
                tmp = [hrope[:, i * 128:(i + 1) * 128].rearrange("p (g n) -> p g n", g=16) for i in range(4)]
                for to, u, w in zip(tmp, (a, b, b, a), (cos, sin, cos, sin)):
                    dve.tensor_tensor(to, u, w, ALU.mult).then_inc(dve_own, 1)
                dve.wait_ge(dve_own, n(dve_own, 4))
                dve.tensor_tensor(a, tmp[0], tmp[1], ALU.subtract).then_inc(dve_own, 1)
                dve.tensor_tensor(b, tmp[2], tmp[3], ALU.add).then_inc(dve_own, 1)
                dve.wait_ge(dve_own, n(dve_own, 2))
                dve.sem_inc(qk_ready, 1)
                dve.sem_inc(k_store, 1)
                dve.wait_ge(kTp_ready, n(kTp_ready))
                w = P if not isinstance(t, int) or t < LAST else ROWS8
                dve.tensor_copy(KT3[:, :, bass.ds(t * P, w)],
                                kTp.rearrange("p (h n) -> p h n", h=HEADS)[:, :, 0:w]).then_inc(dve_own, 1)
                dve.wait_ge(dve_own, n(dve_own))
                dve.sem_inc(kTp_free, 1)
                dve.wait_ge(py_ready, n(py_ready))
                for g in range(4):
                    dve.tensor_scalar(hqp[par][:, 512 + g * P:512 + (g + 1) * P], pyp[:, g * P:(g + 1) * P],
                                      bpT[:, g:g + 1], scT[:, g:g + 1], ALU.add, ALU.mult).then_inc(dve_own, 1)
                dve.wait_ge(dve_own, n(dve_own, 4))
                dve.sem_inc(py_free, 1)
                dve.sem_inc(pe_done, 1)
                dve.sem_inc(qp_store, 1)

            with dve.Fori(0, LAST // 2) as j:
                head(0, 2 * j)
                head(1, 2 * j + 1)
                n.settle()
            head(0, LAST)
            dve.wait_ge(head_over, n(head_over, 4))
            for j in range(GROUPS):
                dve.wait_ge(fold_ready, n(fold_ready))
                dve.tensor_tensor(w_route[:, :, j * P:(j + 1) * P],
                                  S[j % 2][:, :].rearrange("p (c n) -> p c n", c=DC),
                                  g2c.unsqueeze(2).to_broadcast([P, DC, P]), ALU.mult).then_inc(dve_own, 1)
                dve.wait_ge(dve_own, n(dve_own))
                dve.sem_inc(fold_free, 1)
            dve.sem_inc(route_w, 1)
            dve.wait_ge(lam_done, n(lam_done))
            dve.tensor_tensor(lamt[:, 0:1], lamt[:, 3:4], lamt[:, 2:3], ALU.subtract).then_inc(dve_own, 1)
            dve.wait_ge(dve_own, n(dve_own))
            dve.tensor_scalar(coef[:, 1:2], lamt[:, 0:1], -LAM_INIT, None, ALU.add).then_inc(dve_own, 1)
            dve.wait_ge(dve_own, n(dve_own))
            dve.memset(coef[:, 0:1], 1.0).then_inc(dve_own, 1)
            dve.tensor_copy(coef[:, 2:3], r01[:, 0:1]).then_inc(dve_own, 1)
            dve.tensor_tensor(coef[:, 3:4], coef[:, 1:2], r01[:, 0:1], ALU.mult).then_inc(dve_own, 1)
            dve.scalar_tensor_tensor(scoef, r01[:, 2:3], coef[:, 1:2], r01[:, 1:2], ALU.mult, ALU.add)\
                .then_inc(dve_own, 1)
            dve.wait_ge(dve_own, n(dve_own, 4))
            dve.wait_ge(wo_in, n(wo_in, 16))
            for c in range(HEADS):
                dve.tensor_scalar(w_out_sb[:, c, :], w_out_sb[:, c, :], subc, 1.0 - LAM_INIT, ALU.mult, ALU.mult)\
                    .then_inc(dve_own, 1)
            dve.wait_ge(dve_own, n(dve_own, HEADS))
            dve.sem_inc(wo_ready, 1)
            n.settle()

            def scale_mask(h, c, last):
                if c == 0:
                    if h == 0:
                        dve.wait_ge(mask_in, n(mask_in, 32 if last else 16))
                    else:
                        dve.wait_ge(a_used, n(a_used))
                dve.wait_ge(s_ready, n(s_ready))
                low = nmx if last else nm
                dve.tensor_tensor_reduce(out=[e0, e1][c], in0=S[c][:, :], in1=mask_sb, scale=-(QK ** -0.5),
                                         scalar=3e38, op0=ALU.add, op1=ALU.min,
                                         accum_out=low[:, c:c + 1]).then_inc(dve_own, 1)
                if last:
                    dve.tensor_tensor_reduce(out=[ex0, ex1][c], in0=T[:, c * ROWS8:(c + 1) * ROWS8], in1=emask[:, :],
                                             scale=-(QK ** -0.5), scalar=3e38, op0=ALU.add, op1=ALU.min,
                                             accum_out=nmx[:, 2 + c:3 + c]).then_inc(dve_own, 1)
                    dve.wait_ge(dve_own, n(dve_own, 2))
                    dve.tensor_tensor(nm[:, c:c + 1], nmx[:, c:c + 1], nmx[:, 2 + c:3 + c], ALU.min).then_inc(dve_own, 1)
                dve.wait_ge(dve_own, n(dve_own))
                dve.sem_inc(nm_ready, 1)
                if c == 1:
                    dve.sem_inc(s_free, 1)
                    if last:
                        dve.sem_inc(t_free, 1)

            def combine(part, last):
                if part == 0:
                    dve.wait_ge(exp_ready, n(exp_ready))
                    if last:
                        dve.tensor_tensor(sums[:, 0:2], sums[:, 0:2], sums[:, 2:4], ALU.add).then_inc(dve_own, 1)
                        dve.wait_ge(dve_own, n(dve_own))
                    dve.reciprocal(rc, sums[:, 0:2]).then_inc(dve_own, 1)
                    dve.wait_ge(dve_own, n(dve_own))
                    dve.tensor_tensor(rc, rc, coef[:, 2:4] if last else coef[:, 0:2], ALU.mult).then_inc(dve_own, 1)
                    dve.wait_ge(dve_own, n(dve_own))
                    dve.tensor_scalar(e1, e1, rc[:, 1:2], None, ALU.mult).then_inc(dve_own, 1)
                    if last:
                        dve.tensor_scalar(ex1, ex1, rc[:, 1:2], None, ALU.mult).then_inc(dve_own, 1)
                    dve.wait_ge(dve_own, n(dve_own, 2 if last else 1))
                else:
                    dve.scalar_tensor_tensor(e0, e0, rc[:, 0:1], e1, ALU.mult, ALU.add).then_inc(dve_own, 1)
                    if last:
                        dve.scalar_tensor_tensor(ex0, ex0, rc[:, 0:1], ex1, ALU.mult, ALU.add).then_inc(dve_own, 1)
                    dve.wait_ge(dve_own, n(dve_own, 2 if last else 1))
                    dve.sem_inc(a_ready, 1)

            def sample(k, g, s):
                for i in range(GRP):
                    b = GRP * g + i
                    if k == s + 2 * i:
                        if i == 0:
                            if g == 0:
                                dve.wait_ge(a_used, n(a_used))
                                dve.wait_ge(qz_free, n(qz_free))
                            dve.memset(QZ, 0.0).then_inc(dve_own, 1)
                            dve.wait_ge(dve_own, n(dve_own))
                            dve.sem_inc(msam_free, 1)
                            dve.sem_inc(e_free, 1)
                        if i > 0:
                            dve.wait_ge(qz_free, n(qz_free))
                            dve.sem_inc(e_free, 1)
                        for c in range(2):
                            r = slice(QK * c, QK * c + QK)
                            dve.tensor_copy(QZ[r, P:].rearrange("p (h n) -> p h n", h=HEADS)[:, :, c * NEW:(c + 1) * NEW],
                                            qT[r, :, TAIL + NEW * b:TAIL + NEW * (b + 1)]).then_inc(dve_own, 1)
                        dve.wait_ge(dve_own, n(dve_own, 2))
                        dve.sem_inc(qz_ready, 1)
                if k == s + 8:
                    dve.wait_ge(qz_free, n(qz_free))
                    dve.wait_ge(msam_in, n(msam_in, 16))
                    dve.tensor_tensor(Ps[:, 0:PAST], S0[:, 0:PAST], msam_sb[:, 0:PAST], ALU.add).then_inc(dve_own, 1)
                    dve.wait_ge(dve_own, n(dve_own))
                    dve.tensor_tensor(Ps[:, PAST:SW], S1[:, 0:ROWS8], msam_sb[:, PAST:SW], ALU.add)\
                        .then_inc(dve_own, 1)
                    dve.wait_ge(dve_own, n(dve_own))
                    dve.sem_inc(s_free, 1)
                    dve.tensor_scalar(Ps, Ps, -(QK ** -0.5), None, ALU.mult).then_inc(dve_own, 1)
                    dve.wait_ge(dve_own, n(dve_own))
                    dve.tensor_reduce(snm, Ps, AX.X, ALU.min).then_inc(dve_own, 1)
                    dve.wait_ge(dve_own, n(dve_own))
                    dve.sem_inc(nm_ready, 1)
                if k == s + 10:
                    dve.wait_ge(exp_ready, n(exp_ready))
                    dve.reciprocal(src, ssum).then_inc(dve_own, 1)
                    dve.wait_ge(dve_own, n(dve_own))
                    dve.tensor_tensor(src, src, scoef, ALU.mult).then_inc(dve_own, 1)
                    dve.wait_ge(dve_own, n(dve_own))
                    dve.tensor_scalar(Ps, Ps, src, None, ALU.mult).then_inc(dve_own, 1)
                    dve.wait_ge(dve_own, n(dve_own))
                    dve.sem_inc(a_ready, 1)
                    dve.memset(AZ, 0.0).then_inc(dve_own, 1)
                    dve.wait_ge(dve_own, n(dve_own))
                for i in range(GRP):
                    b = GRP * g + i
                    if k == s + 12 + 2 * i:
                        if i == 0:
                            dve.wait_ge(pt_ready, n(pt_ready))
                        else:
                            dve.wait_ge(qz_free, n(qz_free))
                        dve.sem_inc(e_free, 1)
                        for kind in range(3):
                            r = slice(0, P if kind < PAGES else ROWS8)
                            src4 = PT[r, kind, i * 32:(i + 1) * 32].rearrange("p (h n) -> p h n", h=HEADS)
                            to = AZ[r, P + P * HEADS * kind:P + P * HEADS * (kind + 1)]\
                                .rearrange("p (h n) -> p h n", h=HEADS)[:, :, 0:NEW]
                            dve.tensor_tensor(to, src4[:, :, 0:NEW], src4[:, :, NEW:2 * NEW], ALU.add)\
                                .then_inc(dve_own, 1)
                        dve.wait_ge(dve_own, n(dve_own, 3))
                        dve.sem_inc(qz_ready, 1)
                if k == s + 19:
                    dve.wait_ge(qz_free, n(qz_free))
                    if g == SEQS // GRP - 1:
                        dve.sem_inc(o_ready, 1)
                        dve.sem_inc(x1n_free, 1)

            def top16(values, indices, source, which, lo):
                m = len(which)
                for g in which:
                    dve.max(values[:, g, lo:lo + 8], source[:, g, :]).then_inc(dve_own, 1)
                dve.wait_ge(dve_own, n(dve_own, m))
                for g in which:
                    dve.max_index(indices[:, g, lo:lo + 8], values[:, g, lo:lo + 8], source[:, g, :])\
                        .then_inc(dve_own, 1)
                dve.wait_ge(dve_own, n(dve_own, m))
                if lo == 0:
                    for g in which:
                        dve.match_replace(source[:, g, :], values[:, g, lo:lo + 8], source[:, g, :], -3e38)\
                            .then_inc(dve_own, 1)
                    dve.wait_ge(dve_own, n(dve_own, m))

            def lookup(pick, pos, half, q):
                hs, ks = slice(2 * q, 2 * q + 2), slice(2 * TOPK * q, 2 * TOPK * (q + 1))
                shape = [P, 2, TOPK, TOPK]
                dve.tensor_tensor(onehot[:, hs], pos[:, ks].rearrange("p (h k) -> p h k", h=2).unsqueeze(3)
                                  .to_broadcast(shape),
                                  iota16[:, :].unsqueeze(1).unsqueeze(1).to_broadcast(shape),
                                  ALU.is_equal).then_inc(dve_own, 1)
                dve.wait_ge(dve_own, n(dve_own))
                keys = sif.rearrange("p (h c) k -> p h c k", c=2)[:, hs, half, :]
                dve.tensor_tensor(onehot[:, hs], onehot[:, hs], keys.unsqueeze(2).to_broadcast(shape), ALU.mult)\
                    .then_inc(dve_own, 1)
                dve.wait_ge(dve_own, n(dve_own))
                dve.tensor_reduce(pick[:, ks], work[:, 512 * q:512 * (q + 1)].rearrange("p (m j) -> p m j", j=TOPK),
                                  AX.X, ALU.add).then_inc(dve_own, 1)
                dve.wait_ge(dve_own, n(dve_own))

            def top_part(q, u):
                h0, g0 = 2 * q, 4 * q
                ks = slice(2 * TOPK * q, 2 * TOPK * (q + 1))
                if u == 0:
                    dve.wait_ge(sc_ready, n(sc_ready))
                if u < 4:
                    g = g0 + u // 2 * 2
                    top16(sv, si, scores, (g, g + 1), 8 * (u % 2))
                if u == 4:
                    dve.tensor_copy(sif[:, g0:g0 + 4, :], si[:, g0:g0 + 4, :]).then_inc(dve_own, 1)
                    sv4 = sv.rearrange("p (h c) k -> p h c k", c=2)[:, h0:h0 + 2]
                    shape = [P, 2, TOPK, TOPK]
                    dve.tensor_tensor(cand[:, h0:h0 + 2].rearrange("p h (a b) -> p h a b", a=TOPK),
                                      sv4[:, :, 0, :].unsqueeze(3).to_broadcast(shape),
                                      sv4[:, :, 1, :].unsqueeze(2).to_broadcast(shape), ALU.add).then_inc(dve_own, 1)
                    dve.wait_ge(dve_own, n(dve_own, 2))
                if u == 5 or u == 6:
                    top16(tv, tpos, cand, (h0 + u - 5,), 0)
                if u == 7:
                    top16(tv, tpos, cand, (h0, h0 + 1), 8)
                if u == 8:
                    tp = qpw[:, 896:1024].bitcast(U32)[:, ks]
                    tmp = idx_n[:, ks].bitcast(U32)
                    for op, by, to in ((ALU.logical_shift_right, 4, posa), (ALU.bitwise_and, TOPK - 1, posb)):
                        dve.tensor_scalar(tmp, tp, by, None, op).then_inc(dve_own, 1)
                        dve.wait_ge(dve_own, n(dve_own))
                        dve.tensor_copy(to[:, ks], tmp).then_inc(dve_own, 1)
                        dve.wait_ge(dve_own, n(dve_own))
                    lookup(pick1, posa, 0, q)
                if u == 9:
                    lookup(pick2, posb, 1, q)
                    dve.scalar_tensor_tensor(pick1[:, ks], pick1[:, ks], float(NK), pick2[:, ks], ALU.mult, ALU.add)\
                        .then_inc(dve_own, 1)
                    dve.wait_ge(dve_own, n(dve_own))
                    dve.tensor_copy(idx_n[:, ks], pick1[:, ks]).then_inc(dve_own, 1)
                    dve.wait_ge(dve_own, n(dve_own))

            def a_part(k, last):
                at = PLANS[last]
                for h in range(HEADS):
                    for c in at.head(k, at.scale, h):
                        scale_mask(h, c, last)
                    for part in at.head(k, at.combine, h):
                        combine(part, last)
                if last:
                    for g in range(SEQS // GRP):
                        sample(k, g, at.sample0 + at.samplew * g)
                if k == at.squares:
                    if not last:
                        dve.wait_ge(a_used, n(a_used))
                    dve.wait_ge(att_raw, n(att_raw))
                    dve.tensor_tensor(e1[:, 0:ATT], att[:, :], att[:, :], ALU.mult).then_inc(dve_own, 1)
                    dve.wait_ge(dve_own, n(dve_own))
                    dve.tensor_reduce(ss4, e1[:, 0:ATT].rearrange("p (h n) -> p h n", h=HEADS), AX.X, ALU.add)\
                        .then_inc(ss4_ready, 1)
                if k == at.norm:
                    dve.wait_ge(rs4_ready, n(rs4_ready))
                    dve.reciprocal(rs4, rs4).then_inc(dve_own, 1)
                    dve.wait_ge(dve_own, n(dve_own))
                    a3 = att[:, :].rearrange("p (h n) -> p h n", h=HEADS)
                    dve.tensor_tensor(a3, a3, rs4.unsqueeze(2).to_broadcast([P, HEADS, P]), ALU.mult)\
                        .then_inc(att_ready, 1)
                if k == at.x1:
                    dve.wait_ge(x1_in, n(x1_in, 16))
                    dve.wait_ge(proj_ready, n(proj_ready))
                    dve.tensor_tensor(x1n, x1n, S0[:, :], ALU.add).then_inc(dve_own, 1)
                    dve.wait_ge(dve_own, n(dve_own))
                    dve.sem_inc(s_free, 1)
                    dve.sem_inc(x1_ready, 1)
                    dve.sem_inc(x1_sq, 1)
                if k == at.r2:
                    dve.wait_ge(rs2_ready, n(rs2_ready))
                    dve.reciprocal(r2, rs2).then_inc(dve_own, 1)
                    dve.wait_ge(dve_own, n(dve_own))
                    dve.sem_inc(r2_ready, 1)
                for u in at.run(k, at.top, 4 * TOPU, at.top_pace):
                    top_part(*divmod(u, TOPU))
                g3 = gate_n[:, :].rearrange("p (h k) -> p h k", h=PH)
                if k == at.gate:
                    dve.tensor_tensor(g3, tv, tv[:, :, 0:1].to_broadcast([P, PH, TOPK]), ALU.subtract)\
                        .then_inc(dve_own, 1)
                    dve.wait_ge(dve_own, n(dve_own))
                    dve.sem_inc(gexp_in, 1)
                if k == at.gate + 2:
                    dve.wait_ge(gexp_out, n(gexp_out))
                    dve.tensor_reduce(gsum, g3, AX.X, ALU.add).then_inc(dve_own, 1)
                    dve.wait_ge(dve_own, n(dve_own))
                    dve.reciprocal(grec, gsum).then_inc(dve_own, 1)
                    dve.wait_ge(dve_own, n(dve_own))
                    dve.tensor_tensor(g3, g3, grec.unsqueeze(2).to_broadcast([P, PH, TOPK]), ALU.mult)\
                        .then_inc(dve_own, 1)
                    dve.wait_ge(dve_own, n(dve_own))
                    dve.sem_inc(a_over, 1)

            def promote_lo():
                dve.tensor_copy(idx_c[:, 0:PICKS // 2], idx_n[:, 0:PICKS // 2]).then_inc(dve_own, 1)
                dve.wait_ge(dve_own, n(dve_own))
                dve.sem_inc(idx_lo, 1)

            def promote(last):
                dve.tensor_copy(idx_c[:, PICKS // 2:], idx_n[:, PICKS // 2:]).then_inc(dve_own, 1)
                dve.tensor_copy(gate_c[:, :], gate_n[:, :]).then_inc(dve_own, 1)
                dve.scalar_tensor_tensor(h2c[:, :], x1n, r2, g2w[:, :], ALU.mult, ALU.mult).then_inc(dve_own, 1)
                dve.wait_ge(dve_own, n(dve_own, 3))
                if last:
                    half = slice(0, PICKS // 2), slice(PICKS // 2, PICKS)
                    dve.tensor_copy(idx_c[FOLD:ROWSF, half[0]], idx_n[0:ROWS8, half[1]]).then_inc(dve_own, 1)
                    dve.tensor_copy(gate_c[FOLD:ROWSF, half[0]], gate_n[0:ROWS8, half[1]]).then_inc(dve_own, 1)
                    dve.tensor_copy(h2c[FOLD:ROWSF, :], h2c[0:ROWS8, :]).then_inc(dve_own, 1)
                    dve.wait_ge(dve_own, n(dve_own, 3))
                dve.sem_inc(idx_hi, 1)
                dve.sem_inc(h2_ready, 1)

            def g_step(t, k, r):
                s = k % SLOTS
                of_tile = len(range(s, PICKS, SLOTS))
                dve.wait_ge(landed[s], t * (16 * of_tile) + 16 * (k // SLOTS + 1))
                dve.tensor_tensor_reduce(out=ring[s][0:r, 0:D], in0=ring[s][0:r, 0:D], in1=h2c[0:r, :], scale=1.0,
                                         scalar=0.0, op0=ALU.mult, op1=ALU.add,
                                         accum_out=dots[0:r, s:s + 1]).then_inc(dot_ready, 1)

            def finish(r, last_slot):
                dve.wait_ge(y_ready, n(y_ready))
                dve.sem_inc(slot_free[last_slot], 1)
                dve.tensor_copy((aT if r == P else e0)[0:r, :], Y[0:r, :]).then_inc(dve_own, 1)
                dve.wait_ge(dve_own, n(dve_own))
                dve.sem_inc(y_free, 1)
                dve.sem_inc(y_store, 1)

            for k in range(PICKS):
                a_part(k, False)
            promote_lo()
            n.settle()
            with dve.Fori(0, LAST - 1) as t:
                promote(False)
                for k in range(PICKS):
                    g_step(t, k, P)
                    if k == 1:
                        dve.wait_ge(x1n_read, n(x1n_read))
                        dve.sem_inc(x1n_free, 1)
                    a_part(k, False)
                    if k == PROMOTE:
                        promote_lo()
                finish(P, (PICKS - 1) % SLOTS)
                n.settle()
            promote(False)
            for k in range(PICKS):
                g_step(LAST - 1, k, P)
                if k == 1:
                    dve.wait_ge(x1n_read, n(x1n_read))
                a_part(k, True)
            finish(P, (PICKS - 1) % SLOTS)
            promote_lo()
            promote(True)
            for k in range(PICKS // 2):
                g_step(LAST, k, ROWSF)
            finish(ROWS8, 0)


def rotary_table():
    pos = np.zeros(TILES * P)
    pos[:META + SEQ] = np.arange(META + SEQ)
    pos[META + SEQ:LAST * P + ROWS8] = PAST + np.arange(SEQS * NEW) % NEW
    inv = (np.float32(500000.0) ** (-np.arange(0, ROPE, 2, dtype=np.float32) / ROPE)).astype(np.float32)
    ang = (pos.astype(np.float32)[:, None] * inv[None, :]).astype(np.float64)
    return np.concatenate([np.cos(ang), np.sin(ang)], 1).astype(np.float32).reshape(TILES, P, ROPE)


def pool_tables():
    cur = np.zeros((TILES, P, 2, 4, P), np.float32)
    old = np.zeros((SEQS, STATE, 4, P), np.float32)
    for g, w in enumerate(WINDOWS):
        for t in range(TILES):
            for p in range(P if t < LAST else TAIL):
                pos = t * P + p
                for q in range(max(0, pos - w + 1), pos + 1):
                    cur[t, q % P, 0 if q // P == t else 1, g, p] += np.float32(1.0) / np.float32(min(pos + 1, w))
                cur[t, p, 0, g, p] -= 1
        for b in range(SEQS):
            for s in range(NEW):
                p = TAIL + NEW * b + s
                for q in range(s - w + 1, s + 1):
                    if q >= 0:
                        cur[LAST, TAIL + NEW * b + q, 0, g, p] += 1.0 / w
                    else:
                        old[b, STATE + q, g, p] += 1.0 / w
                cur[LAST, p, 0, g, p] -= 1
    return cur.reshape(TILES, P, 1024), old.reshape(SEQS * STATE, 512)


def masks(bf16):
    full = np.full((TILES, P, KEYS), NEG, np.float32)
    for t in range(TILES):
        for p in range(P):
            full[t, p, :t * P + p + 1] = 0
    extra = np.full((P, ROWS8), NEG, np.float32)
    for p in range(TAIL):
        extra[p, :p + 1] = 0
    sample = np.full((SEQS // GRP, P, SW), NEG, np.float32)
    sample[:, :, :PAST] = 0
    for g in range(SEQS // GRP):
        for r in range(P):
            b, s = GRP * g + r // 32, r % NEW
            lo = PAST + TAIL + NEW * b
            sample[g, r, lo:lo + s + 1] = 0
    return full.astype(bf16), extra, sample


def kernel(x_prompt, x_sample, cache_k, cache_v, state_pool, page_table, meta_tokens, norm1_g, w_in,
           q_norm_g, k_norm_g, lambda_q1, lambda_k1, lambda_q2, lambda_k2, subln_g, w_pool, b_pool,
           pool_scale, w_out, norm2_g, w_query, sub_keys, w_u, w_v):
    import ml_dtypes
    import concourse.bacc as bacc
    from concourse.bass_utils import run_bass_kernel_spmd

    a = {k: np.asarray(v) for k, v in dict(
        x_prompt=x_prompt, x_sample=x_sample, cache_k=cache_k, cache_v=cache_v, state_pool=state_pool,
        page_table=page_table, meta_tokens=meta_tokens, norm1_g=norm1_g, w_in=w_in, q_norm_g=q_norm_g,
        k_norm_g=k_norm_g, lambda_q1=lambda_q1, lambda_k1=lambda_k1, lambda_q2=lambda_q2,
        lambda_k2=lambda_k2, subln_g=subln_g, w_pool=w_pool, b_pool=b_pool, pool_scale=pool_scale,
        w_out=w_out, norm2_g=norm2_g, w_query=w_query, sub_keys=sub_keys, w_u=w_u, w_v=w_v).items()}

    def wide(row):
        return np.broadcast_to(row.reshape(1, -1), (P, row.size))

    x = np.zeros((TILES * P, D), np.float32)
    x[:META] = a["meta_tokens"]
    x[META:META + SEQ] = a["x_prompt"][0]
    x[META + SEQ:LAST * P + ROWS8] = a["x_sample"].reshape(-1, D)
    x = x.reshape(TILES, P, D)
    mt, mst = pool_tables()
    mask, mext, msam = masks(ml_dtypes.bfloat16)
    rows01 = np.zeros((P, 3), np.float32)
    rows01[:TAIL, 0] = 1
    comp = np.arange(P) // NEW % 2
    rows01[:, 1], rows01[:, 2] = comp == 0, comp == 1
    n_pool = a["cache_k"].shape[1]
    ins = dict(
        x=x,
        xT=x.reshape(TILES, P, DC, P).transpose(0, 3, 2, 1).reshape(TILES, P, D),
        g1T=a["norm1_g"].reshape(DC, P).T,
        w_in=a["w_in"][0].reshape(DC, P, INW),
        gqk=np.concatenate([wide(np.tile(a["q_norm_g"], 8)), wide(np.tile(a["k_norm_g"], 8))], 1),
        cs=rotary_table(), mt=mt, mst=mst,
        state=a["state_pool"][0].reshape(SEQS * STATE, 512),
        w_pool=a["w_pool"][0].transpose(1, 0, 2).reshape(P, 512),
        b_poolT=a["b_pool"][0].T, scaleT=a["pool_scale"].reshape(4, P).T,
        wqT=a["w_query"][0].T.reshape(GROUPS, P, D),
        skT=a["sub_keys"][0].reshape(GROUPS, NK, P).transpose(2, 0, 1),
        g2T=a["norm2_g"].reshape(DC, P).T, g2b=wide(a["norm2_g"]),
        lams=np.concatenate([wide(a[k]) for k in ("lambda_q1", "lambda_k1", "lambda_q2", "lambda_k2")], 1),
        rows01=rows01, w_out=a["w_out"][0], subT=a["subln_g"].reshape(P, 1),
        mask=mask, mext=mext, msam=msam,
        ktc=a["cache_k"][0].transpose(0, 3, 2, 1).reshape(n_pool, P, HEADS * PAGE),
        vc=a["cache_v"][0].reshape(n_pool, PAGE, HEADS * P),
        pages=a["page_table"].reshape(1, -1),
        wuv=np.concatenate([a["w_u"][0], a["w_v"][0]], 1),
        iota=wide(np.arange(TOPK, dtype=np.float32)),
    )
    outs = dict(y_all=(TILES, P, D), k_all=(TILES, P, 512), v_all=(TILES, P, 512), p_last=(ROWS8, 512),
                state_old=(SEQS, STATE - NEW, 512))
    nc = bacc.Bacc("TRN2", target_bir_lowering=False, num_devices=1)
    args, arrays = [], {}
    for name, v in ins.items():
        arrays["in_" + name] = v = np.ascontiguousarray(v)
        args.append(nc.dram_tensor("in_" + name, v.shape, mybir.dt.from_np(v.dtype), kind="ExternalInput").ap())
    for name, shape in outs.items():
        args.append(nc.dram_tensor("out_" + name, shape, F32, kind="ExternalOutput").ap())
    build(nc, *args)
    res = run_bass_kernel_spmd(nc, [arrays], core_ids=[0]).results[0]
    y, k, v = (res["out_" + m].reshape(TILES * P, -1) for m in ("y_all", "k_all", "v_all"))
    p_new = res["out_p_last"]
    n_p, n_all = META + SEQ, LAST * P + ROWS8
    return (y[META:n_p].reshape(1, SEQ, D), y[n_p:n_all].reshape(SEQS, NEW, D),
            k[:n_p].reshape(1, 1, n_p, HEADS, P), v[:n_p].reshape(1, 1, n_p, HEADS, P),
            p_new[TAIL - STATE:TAIL].reshape(1, 1, STATE, 512),
            k[n_p:n_all].reshape(1, SEQS, NEW, HEADS, P), v[n_p:n_all].reshape(1, SEQS, NEW, HEADS, P),
            np.concatenate([res["out_state_old"], p_new[TAIL:].reshape(SEQS, NEW, 512)], 1)[None])
```

```python
import math
from contextlib import ExitStack

import concourse.bass as bass
from concourse import mybir
import numpy as np

F32 = mybir.dt.float32
BF16 = mybir.dt.bfloat16
I32 = mybir.dt.int32
U32 = mybir.dt.uint32
ALU = mybir.AluOpType
ACT = mybir.ActivationFunctionType
AX = mybir.AxisListType

P = 128
D = 1024
DC = D // P
ATT = 512
HEADS = 4
QK = 64
ROPE = QK // 4
HALF = ROPE // 2
INW = 3 * ATT + 512
META = 16
SEQ = 1024
SEQS = 8
NEW = 4
PAST = 256
PAGE = 128
PAGES = PAST // PAGE
TILES = 9
LAST = TILES - 1
TAIL = META + SEQ - LAST * P
ROWS8 = TAIL + SEQS * NEW
KEYS = LAST * P
KTW = KEYS + ROWS8
WINDOWS = (2, 4, 8, 16)
STATE = 15
PH = 8
NK = 128
TOPK = 16
GROUPS = 2 * PH
PICKS = PH * TOPK
NEXP = NK * NK
EPS = 1e-6
NEG = -1e30
LAM_INIT = 0.8 - 0.6 * math.exp(-0.3 * 0)
SLOTS = 5
GRP = 4
SW = PAST + ROWS8

FOLD = 64
ROWSF = FOLD + ROWS8
TOPU = 10

_SHORT = -PICKS % SLOTS
_LONG = (PICKS - _SHORT * (SLOTS - 1)) // SLOTS
SLOT = [s for i in range(_LONG + _SHORT) for s in range(SLOTS - 1 if 10 <= i < 10 + _SHORT else SLOTS)]
USE = [SLOT[:k + 1].count(SLOT[k]) for k in range(PICKS)]
KVBUF = 3
EARLY = 1


class Plan:
    head0, headw = 1, 10
    scores, scale, exp = (0, 1, 2, 3), (4, 5), (6, 6)
    combine, flip, evac, values = (8, 9), (10, 11, 12), (11, 12, 12), (12, 13, 14, 15)
    att = head0 + (HEADS - 1) * headw + values[-1] + 1
    squares, norm, flip_att = att + 1, att + 3, att + 4
    project = flip_att + 1
    x1 = project + 2 * DC
    flip_x1 = (x1 + 1, x1 + 2)
    r2 = x1 + 2
    route = x1 + 3
    take = (route + DC, route + 2 * DC, route + 3 * DC, route + 4 * DC)
    top = take[0] + 1
    gate = top + 4 * TOPU
    sample0, samplew = take[0], 20
    sample_out = sample0 + samplew * SEQS // GRP
    promote = gate + 1
    residual, x1n_free = 16, 24

    @classmethod
    def head(cls, k, at, h):
        return [i for i, a in enumerate(at) if k == cls.head0 + cls.headw * h + a]


class Counter:

    def __init__(self, eng):
        self.eng, self.count = eng, {}

    def __call__(self, sem, more=1):
        self.count[sem] = self.count.get(sem, 0) + more
        return self.count[sem]

    def settle(self):
        for sem, n in self.count.items():
            self.eng.sem_inc(sem, -n)
        self.count = {}


def build(nc, x, xT, g1T, w_in, gqk, cs, mt, mst, state, w_pool, b_poolT, scaleT, wqT, skT, g2T, g2b, lams,
          rows01, w_out, subT, mask, mext, msam, ktc, vc, pages, wuv, iota,
          y_all, k_all, v_all, p_last, state_old):
    with ExitStack() as ctx:
        def sb(name, n, dt=F32):
            return ctx.enter_context(nc.sbuf_tensor(name, [P, n], dt))

        def pb(name, n):
            return ctx.enter_context(nc.psum_tensor(name, [P, n], F32))

        def sem(name):
            return ctx.enter_context(nc.semaphore(name))

        sam_dram = nc.dram_tensor("sam_dram", [P, ATT], F32).ap()
        qp_dram = nc.dram_tensor("qp_dram", [TILES, P, 1024], F32).ap()

        big1 = sb("big1", 16384)
        big2 = sb("big2", 16384)
        KT = sb("KT", HEADS * KTW)
        V = sb("V", TILES * ATT)
        work = sb("work", 4096)
        h2c = sb("h2c", D)
        g2w = sb("g2w", D)
        maskw = sb("maskw", 512)
        qpw = sb("qpw", 1024)
        slot5 = sb("slot5", 2 * D)
        ext = sb("ext", 2 * ROWS8 + P)
        emask = sb("emask", ROWS8)
        ident = sb("ident", P)
        fold_id = sb("fold_id", ROWS8)
        diag = sb("diag", SLOTS * P)
        idx_n = sb("idx_n", PICKS, I32)
        idx_c = sb("idx_c", PICKS, I32)
        gate_n = sb("gate_n", PICKS)
        gate_c = sb("gate_c", PICKS)
        dots = sb("dots", SLOTS)
        gel = sb("gel", SLOTS)
        amp = sb("amp", SLOTS)
        iota16 = sb("iota16", TOPK)
        sm = sb("sm", P)
        pt = sb("pt", SEQS * PAGES, I32)

        w_in_sb = big1[:, :].rearrange("p (q c n) -> p q c n", q=4, c=DC)
        wqT_sb = big1[:, :].rearrange("p (j n) -> p j n", j=GROUPS)
        w_out_sb = big1[:, 0:8192].rearrange("p (c n) -> p c n", c=DC)
        ring = [big1[:, 8192 + 2048 * i:8192 + 2048 * (i + 1)] for i in range(4)] + [slot5[:, :]]
        att = maskw
        w_route = big2[:, :].rearrange("p (c n) -> p c n", c=DC)
        KT3 = KT[:, :].rearrange("p (h n) -> p h n", h=HEADS)
        V3 = V[:, :].rearrange("p (t n) -> p t n", t=TILES)

        def part(lo, n):
            return big2[:, lo:lo + n]
        hxT = [part(0, 1024), part(1024, 1024)]
        hx = [part(2048, 1024), part(3072, 1024)]
        hqk = [part(4096, 1024), part(5120, 1024)]
        hsq = part(6144, 1024)
        hgqk = part(7168, 1024)
        hp = [part(8192, 512), part(8704, 512)]
        hdT = part(9216, 512)
        hqp = [part(9728, 1024), part(10752, 1024)]
        hmt = [part(11776, 1024), part(12800, 1024)]
        hcs = [part(13824, ROPE), part(13840, ROPE)]
        hwp = part(13856, 512)
        hst = part(14368, 512)
        hmst = part(14880, 512)
        hrope = part(15392, 512)
        hg1 = part(15904, DC)

        e0, e1, aT, x1n = (work[:, a:a + 1024] for a in (0, 1024, 2048, 3072))
        scores = work[:, 0:2048].rearrange("p (g n) -> p g n", g=GROUPS)
        cand = work[:, 0:2048].rearrange("p (h n) -> p h n", h=PH)
        onehot = work[:, 0:2048].rearrange("p (h k j) -> p h k j", h=PH, k=TOPK)
        skT_sb = work[:, 0:2048].rearrange("p (j n) -> p j n", j=GROUPS)
        qT = qpw[:, 0:512].rearrange("p (h n) -> p h n", h=HEADS)
        pyT = qpw[:, 512:1024].rearrange("p (g n) -> p g n", g=HEADS)
        sv = qpw[:, 0:256].rearrange("p (g k) -> p g k", g=GROUPS)
        si = qpw[:, 256:512].bitcast(U32).rearrange("p (g k) -> p g k", g=GROUPS)
        sif = qpw[:, 512:768].rearrange("p (g k) -> p g k", g=GROUPS)
        tv = qpw[:, 768:896].rearrange("p (h k) -> p h k", h=PH)
        tpos = qpw[:, 896:1024].bitcast(U32).rearrange("p (h k) -> p h k", h=PH)
        mask_sb = maskw[:, :].bitcast(BF16)
        posa, posb, pick1, pick2 = (maskw[:, a:a + PICKS] for a in (0, 128, 256, 384))
        ex0, ex1, exT = ext[:, 0:ROWS8], ext[:, ROWS8:2 * ROWS8], ext[:, 2 * ROWS8:]
        QZ = diag[:, 0:P * (1 + HEADS)]
        AZ = ring[4][:, 0:P * (1 + 3 * HEADS)]
        PT = ring[4][:, P * (1 + 3 * HEADS):2 * D].rearrange("p (k n) -> p k n", k=3)
        Ps = h2c[:, 0:SW]
        msam_sb = [h2c[:, SW * g:SW * (g + 1)] for g in (1, 2)]
        sam_kv = [ring[3][:, 0:PAGES * 512], ring[3][:, PAGES * 512:], ring[2][:, PAGES * 512:]]
        sam_q = ring[2][:, 0:512].rearrange("p (h n) -> p h n", h=HEADS)
        sam_o = aT[:, 0:ATT]
        add_o = e1[:, ATT:2 * ATT]

        def col(i, n=1):
            return sm[:, i:i + n]
        ss1, rs1, ss16, rs16 = col(0), col(1), col(4, 16), col(20, 16)
        eps = col(36)
        coef = col(38, 4)
        nmx = col(42, 4)
        sums = col(46, 4)
        rc = col(50, 2)
        ss4, rs4 = col(52, 4), col(56, 4)
        ss2, rs2, r2 = col(60), col(61), col(62)
        gsum, grec = col(64, 8), col(72, 8)
        snm, ssum, src, scoef = col(80), col(81), col(82), col(83)
        lamt = col(84, 4)
        bpT, scT, g2c, subc, r01 = col(88, 4), col(92, 4), col(96, 8), col(104), col(106, 3)
        nm = col(110, 2)

        Y = pb("Y", 1024)
        S0 = pb("S0", 1024)
        S1 = pb("S1", 1024)
        T = pb("T", 512)
        O = pb("O", 512)
        S = [S0, S1]
        zbank = [Y[:, 0:512], Y[:, 512:1024], S0[:, 0:512], S0[:, 512:1024]]
        qTp, kTp = S1[:, 0:512], S1[:, 512:1024]
        dTp, pyp = T[:, :], O[:, :]
        sam_s, sam_y = Y[:, 0:SW], Y[:, 512:1024]
        route_bank = [S0[:, 0:512], S0[:, 512:1024], S1[:, 0:512], S1[:, 512:1024]]

        pe_own, act_own, dve_own, pool_own = sem("pe_own"), sem("act_own"), sem("dve_own"), sem("pool_own")
        c_w_in = [sem(f"c_w_in{c}") for c in range(DC)]
        c_dve = sem("c_dve")
        c_pool = sem("c_pool")
        c_pe = sem("c_pe")
        c_sp = sem("c_sp")
        ident_pe, ident_act = sem("ident_pe"), sem("ident_act")
        eps_ready = sem("eps_ready")
        p0_ready = sem("p0_ready")
        x_in = [sem("x_in0"), sem("x_in1")]
        xT_in = [sem("xT_in0"), sem("xT_in1")]
        mt_in = [sem("mt_in0"), sem("mt_in1")]
        cs_in = [sem("cs_in0"), sem("cs_in1")]
        in_free = sem("in_free")
        xg_ready = sem("xg_ready")
        z_ready = sem("z_ready")
        z_free = sem("z_free")
        sq_ready = sem("sq_ready")
        r1_ready = sem("r1_ready")
        qk_raw = sem("qk_raw")
        ss16_ready, rs16_ready = sem("ss16_ready"), sem("rs16_ready")
        qk_ready = sem("qk_ready")
        k_store = sem("k_store")
        v_store = sem("v_store")
        qp_store = sem("qp_store")
        stored = sem("stored")
        qk_free = sem("qk_free")
        p_ready = sem("p_ready")
        qTp_ready, qTp_free = sem("qTp_ready"), sem("qTp_free")
        kTp_ready, kTp_free = sem("kTp_ready"), sem("kTp_free")
        dTp_ready, dT_ready = sem("dTp_ready"), sem("dT_ready")
        py_ready, py_free = sem("py_ready"), sem("py_free")
        w_in_free = sem("w_in_free")
        head_over = sem("head_over")
        wq_in = [sem(f"wq_in{i}") for i in range(4)]
        fold_ready, fold_free = sem("fold_ready"), sem("fold_free")
        folded = sem("folded")
        route_w = sem("route_w")
        wo_in, wo_ready = sem("wo_in"), sem("wo_ready")
        lam_ready, lam_done = sem("lam_ready"), sem("lam_done")
        a_over = sem("a_over")
        x1n_free = sem("x1n_free")
        mask_in = sem("mask_in")
        qp_in = sem("qp_in")
        x1_in = sem("x1_in")
        s_free = sem("s_free")
        s_ready = sem("s_ready")
        nm_ready, exp_ready = sem("nm_ready"), sem("exp_ready")
        a_ready, a_used = sem("a_ready"), sem("a_used")
        t_free, t_ready = sem("t_free"), sem("t_ready")
        t_evac = sem("t_evac")
        o_ready, o_free = sem("o_ready"), sem("o_free")
        att_raw = sem("att_raw")
        ss4_ready, rs4_ready = sem("ss4_ready"), sem("rs4_ready")
        att_ready = sem("att_ready")
        proj_ready = sem("proj_ready")
        x1_ready, x1_sq = sem("x1_ready"), sem("x1_sq")
        rs2_ready, r2_ready = sem("rs2_ready"), sem("r2_ready")
        route_ready, sc_ready = sem("route_ready"), sem("sc_ready")
        gexp_in, gexp_out = sem("gexp_in"), sem("gexp_out")
        kv_free = sem("kv_free")
        kv_in = [sem(f"kv_in{i}") for i in range(KVBUF)]
        sam_in = sem("sam_in")
        sam_min, sam_exp, sam_a = sem("sam_min"), sem("sam_exp"), sem("sam_a")
        sam_store = sem("sam_store")
        add_free, add_in = sem("add_free"), sem("add_in")
        qz_ready, qz_free = sem("qz_ready"), sem("qz_free")
        pt_ready = sem("pt_ready")
        idx_lo, idx_hi = sem("idx_lo"), sem("idx_hi")
        slot_free = [sem(f"slot_free{s}") for s in range(SLOTS)]
        landed = [sem(f"landed{s}") for s in range(SLOTS)]
        dot_ready = sem("dot_ready")
        diag_ready = sem("diag_ready")
        y_ready = sem("y_ready")
        y_free = sem("y_free")
        y_store = sem("y_store")
        y_stored = sem("y_stored")
        x1n_read = sem("x1n_read")
        gate_ready = sem("gate_ready")

        block = ctx.enter_context(nc.Block())

        def tile_rows(t):
            return P if not isinstance(t, int) or t < LAST else ROWS8

        @block.sync
        def _(sp):
            n = Counter(sp)

            def head_load(t, par):
                sp.wait_ge(in_free, n(in_free))
                sp.dma_start(hxT[par], xT[t]).then_inc(xT_in[par], 16)
                sp.dma_start(hx[par], x[t]).then_inc(x_in[par], 16)
                sp.dma_start(hcs[par], cs[t]).then_inc(cs_in[par], 16)
                sp.dma_start(hmt[par], mt[t]).then_inc(mt_in[par], 16)

            def head_store(t, par):
                r = tile_rows(t)
                sp.wait_ge(k_store, n(k_store))
                sp.dma_start(k_all[t][0:r, :], hqk[par][0:r, 512:1024]).then_inc(stored, 16)
                sp.wait_ge(v_store, n(v_store))
                sp.dma_start(v_all[t][0:r, :], V3[0:r, t, :]).then_inc(stored, 16)
                if r < P:
                    sp.dma_start(p_last, hp[par][0:r, :]).then_inc(stored, 16)
                sp.wait_ge(qp_store, n(qp_store, 2))
                sp.dma_start(qp_dram[t], hqp[par]).then_inc(stored, 16)
                sp.wait_ge(stored, n(stored, 64 if r < P else 48))
                sp.sem_inc(qk_free, 1)

            sp.dma_start(hg1, g1T).then_inc(c_pool, 16)
            head_load(0, 0)
            for c in range(DC):
                sp.dma_start(w_in_sb[:, :, c, :], w_in[c].rearrange("p (q n) -> p q n", q=4)).then_inc(c_w_in[c], 16)
                if c == 3:
                    sp.dma_start(hgqk, gqk).then_inc(c_dve, 16)
                    sp.dma_start(bpT, b_poolT).then_inc(c_dve, 16)
                    sp.dma_start(scT, scaleT).then_inc(c_dve, 16)
                    sp.dma_start(g2c, g2T).then_inc(c_dve, 16)
                    sp.dma_start(subc, subT).then_inc(c_dve, 16)
                    sp.dma_start(r01, rows01).then_inc(c_dve, 16)
                    sp.dma_start(emask[:, :], mext).then_inc(c_dve, 16)
                    sp.dma_start(att[:, 0:256], lams).then_inc(c_dve, 16)
                    sp.dma_start(g2w[:, :], g2b).then_inc(c_dve, 16)
                    sp.dma_start(iota16[:, :], iota).then_inc(c_dve, 16)
            sp.dma_start(hwp, w_pool).then_inc(c_pe, 16)
            sp.dma_start(hst[0:SEQS * STATE, :], state).then_inc(c_pe, 16)
            sp.dma_start(hmst[0:SEQS * STATE, :], mst).then_inc(c_pe, 16)
            sp.dma_start(skT_sb, skT).then_inc(c_pe, 16)
            sp.dma_start(pt[0:1, :], pages).then_inc(c_sp, 16)
            sp.dma_start(state_old, state.rearrange("(b j) n -> b j n", b=SEQS)[:, NEW:STATE, :]).then_inc(stored, 16)
            sp.wait_ge(stored, n(stored, 16))
            sp.wait_ge(c_sp, n(c_sp, 16))
            n.settle()
            with sp.Fori(0, LAST // 2) as j:
                head_load(2 * j + 1, 1)
                head_store(2 * j, 0)
                head_load(2 * j + 2, 0)
                head_store(2 * j + 1, 1)
                n.settle()
            for q in range(4):
                sp.wait_ge(w_in_free, n(w_in_free))
                sp.dma_start(wqT_sb[:, 4 * q:4 * q + 4, :], wqT[4 * q:4 * q + 4].rearrange("j p n -> p j n"))\
                    .then_inc(wq_in[q], 16)
            head_store(LAST, 0)
            sp.sem_inc(head_over, 1)

            def a_load(t):
                sp.wait_ge(a_over, n(a_over))
                sp.dma_start(mask_sb, mask[t]).then_inc(mask_in, 16)
                sp.dma_start(qpw[:, :], qp_dram[t]).then_inc(qp_in, 16)

            def x_load(t):
                sp.wait_ge(x1n_free, n(x1n_free))
                sp.dma_start(x1n, x[t]).then_inc(x1_in, 16)

            def sample_load():
                for g in range(SEQS // GRP):
                    sp.dma_start(msam_sb[g], msam[g]).then_inc(sam_in, 16)
                sp.dma_start(sam_q.rearrange("p h n -> p (h n)"), qp_dram[LAST][:, 0:512]).then_inc(sam_in, 16)
                for i in range(2 * SEQS):
                    g, what, b = i // (2 * GRP), (ktc, vc)[i // GRP % 2], i % GRP
                    sp.wait_ge(kv_free, n(kv_free))
                    for j in range(PAGES):
                        at = (GRP * g + b) * PAGES + j
                        page = sp.value_load(pt[0:1, at:at + 1], min_val=0, max_val=ktc.shape[0] - 1)
                        sp.dma_start(sam_kv[i % KVBUF][:, j * 512:(j + 1) * 512], what[page])\
                            .then_inc(kv_in[i % KVBUF], 16)
                sp.wait_ge(sam_store, n(sam_store))
                sp.dma_start(sam_dram, sam_o).then_inc(stored, 16)
                sp.wait_ge(stored, n(stored, 16))
                sp.sem_inc(y_stored, 1)

            def y_out(t):
                r = tile_rows(t)
                sp.wait_ge(y_store, n(y_store))
                sp.dma_start(y_all[t][0:r, :], (aT if r == P else e0)[0:r, :]).then_inc(stored, 16)
                sp.wait_ge(stored, n(stored, 16))
                sp.sem_inc(y_stored, 1)

            a_load(0)
            x_load(0)
            sp.wait_ge(folded, n(folded))
            sp.dma_start(w_out_sb, w_out.rearrange("(c p) n -> p c n", p=P)).then_inc(wo_in, 16)
            sp.wait_ge(folded, n(folded))
            sample_load()
            a_load(1)
            n.settle()
            with sp.Fori(0, LAST - 1) as t:
                x_load(t + 1)
                a_load(t + 2)
                y_out(t)
                n.settle()
            x_load(LAST)
            sp.wait_ge(add_free, n(add_free))
            sp.dma_start(add_o, sam_dram).then_inc(add_in, 16)
            y_out(LAST - 1)
            y_out(LAST)

        @block.gpsimd
        def _(pool):
            n = Counter(pool)
            pool.memset(ident[:, :], 0.0).then_inc(pool_own, 1)
            pool.memset(hp[1], 0.0).then_inc(p0_ready, 1)
            pool.wait_ge(pool_own, n(pool_own))
            pool.affine_select(out=ident[:, :], in_=ident[:, :], compare_op=ALU.not_equal, fill=1.0,
                               base=0, pattern=[[-1, P]], channel_multiplier=1).then_inc(pool_own, 1)
            pool.wait_ge(pool_own, n(pool_own))
            pool.memset(fold_id[:, :], 0.0).then_inc(pool_own, 1)
            pool.wait_ge(pool_own, n(pool_own))
            for base in (0, -FOLD):
                pool.affine_select(out=fold_id[:, :], in_=fold_id[:, :], compare_op=ALU.not_equal, fill=1.0,
                                   base=base, pattern=[[-1, ROWS8]], channel_multiplier=1).then_inc(pool_own, 1)
                pool.wait_ge(pool_own, n(pool_own))
            pool.sem_inc(ident_pe, 1)
            pool.sem_inc(ident_act, 1)
            pool.wait_ge(c_pool, n(c_pool, 16))
            n.settle()

            def head(par):
                pool.wait_ge(xT_in[par], n(xT_in[par], 16))
                v = hxT[par].rearrange("p (c n) -> p c n", c=DC)
                pool.tensor_tensor(v, v, hg1.unsqueeze(2).to_broadcast([P, DC, P]), ALU.mult).then_inc(pool_own, 1)
                pool.wait_ge(pool_own, n(pool_own))
                pool.sem_inc(xg_ready, 1)

            with pool.Fori(0, LAST // 2):
                head(0)
                head(1)
                n.settle()
            head(0)
            pool.sem_inc(head_over, 1)
            n.settle()

            def gather(r, steps):
                for k in range(steps):
                    if k == 0:
                        pool.wait_ge(idx_lo, n(idx_lo))
                    if k == PICKS // 2:
                        pool.wait_ge(idx_hi, n(idx_hi))
                    pool.wait_ge(slot_free[SLOT[k]], n(slot_free[SLOT[k]]))
                    pool.indirect_dma_start(ring[SLOT[k]][0:r, :], None, wuv,
                                            bass.IndirectOffsetOnAxis(ap=idx_c[0:r, k:k + 1], axis=0)
                                            ).then_inc(landed[SLOT[k]], 16)
                n.settle()

            with pool.Fori(0, LAST):
                gather(P, PICKS)
            gather(ROWSF, PICKS // 2)

        @block.tensor
        def _(pe):
            n = Counter(pe)

            def head(par, first=False, last=False):
                pe.wait_ge(xg_ready, n(xg_ready))
                if first:
                    pe.wait_ge(z_free, n(z_free, 4))
                    for c in range(DC):
                        pe.wait_ge(c_w_in[c], n(c_w_in[c], 16))
                        for q in range(4):
                            mm = pe.matmul(zbank[q], hxT[par][:, c * P:(c + 1) * P], w_in_sb[:, q, c, :],
                                           start=(c == 0), stop=(c == DC - 1), skip_group_check=True)
                            if c == DC - 1:
                                mm.then_inc(z_ready, 1)
                else:
                    for q in range(4):
                        pe.wait_ge(z_free, n(z_free))
                        for c in range(DC):
                            mm = pe.matmul(zbank[q], hxT[par][:, c * P:(c + 1) * P], w_in_sb[:, q, c, :],
                                           start=(c == 0), stop=(c == DC - 1))
                        mm.then_inc(z_ready, 1)
                pe.wait_ge(qk_ready, n(qk_ready))
                if first:
                    pe.wait_ge(ident_pe, n(ident_pe))
                pe.wait_ge(qTp_free, n(qTp_free))
                for h in range(HEADS):
                    mm = pe.transpose(qTp[:, h * P:(h + 1) * P], hqk[par][:, h * P:(h + 1) * P], ident[:, :])
                mm.then_inc(qTp_ready, 1)
                pe.wait_ge(kTp_free, n(kTp_free))
                for h in range(HEADS):
                    mm = pe.transpose(kTp[:, h * P:(h + 1) * P], hqk[par][:, 512 + h * P:512 + (h + 1) * P], ident[:, :])
                mm.then_inc(kTp_ready, 1)
                pe.wait_ge(p_ready, n(p_ready))
                pe.wait_ge(mt_in[par], n(mt_in[par], 16))
                if first:
                    pe.wait_ge(p0_ready, n(p0_ready))
                    pe.wait_ge(c_pe, n(c_pe, 64))
                for g in range(4):
                    s = slice(g * P, (g + 1) * P)
                    pe.matmul(dTp[:, s], hp[par][:, s], hmt[par][:, s], start=True, stop=False)
                    mm = pe.matmul(dTp[:, s], hp[1 - par][:, s], hmt[par][:, 512 + g * P:512 + (g + 1) * P],
                                   start=False, stop=not last)
                    if last:
                        r = SEQS * STATE
                        mm = pe.matmul(dTp[:, s], hst[0:r, s], hmst[0:r, s], start=False, stop=True)
                mm.then_inc(dTp_ready, 1)
                pe.wait_ge(dT_ready, n(dT_ready))
                pe.wait_ge(py_free, n(py_free))
                for g in range(4):
                    s = slice(g * P, (g + 1) * P)
                    mm = pe.matmul(pyp[:, s], hwp[:, s], hdT[:, s], start=True, stop=True)
                mm.then_inc(py_ready, 1)

            head(0, first=True)
            head(1)
            n.settle()
            with pe.Fori(1, LAST // 2):
                head(0)
                head(1)
                n.settle()
            head(0, last=True)
            pe.sem_inc(head_over, 1)
            n.settle()

            for j in range(GROUPS):
                if j % 4 == 0:
                    pe.wait_ge(wq_in[j // 4], n(wq_in[j // 4], 16))
                pe.wait_ge(fold_free, n(fold_free))
                bank = S[j % 2]
                for c in range(DC):
                    mm = pe.matmul(bank[:, c * P:(c + 1) * P], wqT_sb[:, j, c * P:(c + 1) * P], skT_sb[:, j, :],
                                   start=True, stop=True)
                mm.then_inc(fold_ready, 1)
            pe.wait_ge(route_w, n(route_w))
            pe.wait_ge(wo_ready, n(wo_ready))
            n.settle()

            def scores_of(h, u, last, first):
                c, m = divmod(u, 2)
                r = slice(QK * c, QK * c + QK)
                if first and m == 1:
                    return
                if h == 0 and u == 0:
                    pe.wait_ge(qp_in, n(qp_in, 16))
                if u == 0:
                    pe.wait_ge(s_free, n(s_free))
                w = P if first else 512
                mm = pe.matmul(S[c][:, m * 512:m * 512 + w], qT[r, h, :], KT3[r, h, m * 512:m * 512 + w],
                               start=True, stop=True)
                if (m == 1 or first) and not last:
                    mm.then_inc(s_ready, 1)
                if u == 3 and last:
                    pe.wait_ge(t_free, n(t_free))
                    for c in range(2):
                        r = slice(QK * c, QK * c + QK)
                        pe.matmul(T[:, c * ROWS8:(c + 1) * ROWS8], qT[r, h, :], KT3[r, h, KEYS:KTW],
                                  start=True, stop=True).then_inc(pe_own, 1)
                        pe.wait_ge(pe_own, n(pe_own))
                    pe.sem_inc(s_ready, 2)

            def flip(m, last, first):
                if first and m == 1:
                    return
                if m == 2:
                    if last:
                        pe.wait_ge(t_free, n(t_free))
                        pe.transpose(T[0:ROWS8, 0:P], ex0, ident[:, :]).then_inc(t_ready, 1)
                    return
                if m == 0:
                    pe.wait_ge(a_ready, n(a_ready))
                pe.wait_ge(t_free, n(t_free))
                for i in range(1 if first else 4):
                    b = 4 * m + i
                    mm = pe.transpose(T[:, i * P:(i + 1) * P], e0[:, b * P:(b + 1) * P], ident[:, :])
                mm.then_inc(t_ready, 1)

            def values(h, u, last, first):
                if u == 0:
                    pe.wait_ge(t_evac, n(t_evac, 3 if last else 1 if first else 2))
                    pe.sem_inc(a_used, 1)
                    if h == 0:
                        pe.wait_ge(o_free, n(o_free))
                for b in (2 * u, 2 * u + 1):
                    if first and b > 0:
                        continue
                    mm = pe.matmul(O[:, h * P:(h + 1) * P], aT[:, b * P:(b + 1) * P], V3[:, b, h * P:(h + 1) * P],
                                   start=(b == 0), stop=first or b == LAST - 1 and not last, skip_group_check=True)
                if u == 3 and last:
                    mm = pe.matmul(O[:, h * P:(h + 1) * P], exT[0:ROWS8, :], V3[0:ROWS8, LAST, h * P:(h + 1) * P],
                                   start=False, stop=True, skip_group_check=True)
                if u == (0 if first else 3) and h == HEADS - 1:
                    mm.then_inc(o_ready, 1)

            def sample_scores(b):
                bl = b % GRP
                i = (b // GRP * 2 * GRP + bl) % KVBUF
                keys = sam_kv[i]
                pe.wait_ge(qz_ready, n(qz_ready))
                pe.wait_ge(kv_in[i], n(kv_in[i], 32))
                for h in range(HEADS):
                    lo = P + P * h - (bl * 32 + h * 8)
                    w = QZ[:, lo:lo + P]
                    a, z = (bl == 0 and h == 0), (bl == GRP - 1 and h == HEADS - 1)
                    for i in range(PAGES):
                        pe.matmul(sam_s[:, i * P:(i + 1) * P], w, keys[:, (i * HEADS + h) * P:(i * HEADS + h + 1) * P],
                                  start=a and i == 0, stop=z, skip_group_check=True)
                    mm = pe.matmul(sam_s[:, PAST:SW], w, KT3[:, h, KEYS:KTW], start=False, stop=z,
                                   skip_group_check=True)
                mm.then_inc(qz_free, 1)

            def sample_flip():
                pe.wait_ge(sam_a, n(sam_a))
                pe.wait_ge(t_free, n(t_free))
                pe.transpose(T[:, 0:P], Ps[:, 0:P], ident[:, :])
                pe.transpose(T[:, P:2 * P], Ps[:, P:2 * P], ident[:, :])
                pe.transpose(T[0:ROWS8, 2 * P:3 * P], Ps[:, 2 * P:SW], ident[:, :]).then_inc(t_ready, 1)

            def sample_values(b):
                i = (b // GRP * 2 * GRP + GRP + b % GRP) % KVBUF
                vals = sam_kv[i]
                pe.wait_ge(qz_ready, n(qz_ready))
                pe.wait_ge(kv_in[i], n(kv_in[i], 32))
                for h in range(HEADS):
                    z = b == SEQS - 1
                    for i in range(PAGES + 1):
                        lo = P + P * (HEADS * i + h) - (TAIL + NEW * b)
                        if i < PAGES:
                            w, v = AZ[:, lo:lo + P], vals[:, i * 512 + h * P:i * 512 + (h + 1) * P]
                        else:
                            w, v = AZ[0:ROWS8, lo:lo + P], V3[0:ROWS8, LAST, h * P:(h + 1) * P]
                        mm = pe.matmul(sam_y[:, h * P:(h + 1) * P], w, v, start=(b == 0 and h == 0 and i == 0),
                                       stop=z and i == PAGES, skip_group_check=True)
                mm.then_inc(qz_free, 1)

            def flip_att():
                pe.wait_ge(att_ready, n(att_ready))
                pe.wait_ge(t_free, n(t_free))
                for h in range(HEADS):
                    mm = pe.transpose(T[:, h * P:(h + 1) * P], att[:, h * P:(h + 1) * P], ident[:, :])
                mm.then_inc(t_ready, 1)

            def project(u):
                c, m = divmod(u, 2)
                if u == 0:
                    pe.wait_ge(t_evac, n(t_evac))
                    pe.wait_ge(s_free, n(s_free))
                lhs = aT[:, c * P:(c + 1) * P] if c < HEADS else pyT[:, c - HEADS, :]
                mm = pe.matmul(S0[:, m * 512:(m + 1) * 512], lhs, w_out_sb[:, c, m * 512:(m + 1) * 512],
                               start=(c == 0), stop=(c == DC - 1), skip_group_check=True)
                if u == 2 * DC - 1:
                    mm.then_inc(proj_ready, 1)

            def flip_x1(m):
                if m == 0:
                    pe.wait_ge(x1_ready, n(x1_ready))
                pe.wait_ge(t_free, n(t_free))
                for i in range(4):
                    b = 4 * m + i
                    mm = pe.transpose(T[:, i * P:(i + 1) * P], x1n[:, b * P:(b + 1) * P], ident[:, :])
                mm.then_inc(t_ready, 1)

            def route(u):
                q, c = divmod(u, DC)
                if u == 0:
                    pe.wait_ge(t_evac, n(t_evac, 2))
                    pe.wait_ge(s_free, n(s_free))
                mm = pe.matmul(route_bank[q], aT[:, c * P:(c + 1) * P], w_route[:, c, q * 512:(q + 1) * 512],
                               start=(c == 0), stop=(c == DC - 1), skip_group_check=True)
                if c == DC - 1:
                    mm.then_inc(route_ready, 1)

            def a_part(k, last=False, first=False):
                at = Plan
                for h in range(HEADS):
                    for u in at.head(k, at.scores, h):
                        scores_of(h, u, last, first)
                    for m in at.head(k, at.flip, h):
                        flip(m, last, first)
                    for u in at.head(k, at.values, h):
                        values(h, u, last, first)
                if first:
                    for g in range(SEQS // GRP):
                        s = at.sample0 + at.samplew * g
                        for i in range(GRP):
                            if k == s + 2 * i + 1:
                                sample_scores(GRP * g + i)
                            if k == s + 12 + 2 * i + 1:
                                sample_values(GRP * g + i)
                        if k == s + 10:
                            sample_flip()
                if k == at.flip_att:
                    flip_att()
                if at.project <= k < at.project + 2 * DC:
                    project(k - at.project)
                for m in range(2):
                    if k == at.flip_x1[m]:
                        flip_x1(m)
                if at.route <= k < at.route + 4 * DC:
                    route(k - at.route)

            def g_step(k, r, steps):
                s = SLOT[k]
                w = P if r == P else ROWS8
                if k == 0:
                    pe.wait_ge(y_free, n(y_free))
                pe.wait_ge(diag_ready, n(diag_ready))
                for m in range(2):
                    mm = pe.matmul(Y[0:w, m * 512:(m + 1) * 512], diag[0:r, s * P:s * P + w],
                                   ring[s][0:r, D + m * 512:D + (m + 1) * 512],
                                   start=(k == 0), stop=(k == steps - 1), skip_group_check=True)
                mm.then_inc(slot_free[s] if k < steps - 1 else y_ready, 1)
                if k == Plan.residual:
                    for m in range(2):
                        mm = pe.matmul(Y[0:w, m * 512:(m + 1) * 512], ident[:, 0:w], x1n[:, m * 512:(m + 1) * 512],
                                       start=False, stop=False, skip_group_check=True)
                    mm.then_inc(x1n_read, 1)

            for k in range(PICKS):
                a_part(k, first=True)
            n.settle()
            with pe.Fori(0, LAST - 1):
                for k in range(PICKS):
                    g_step(k, P, PICKS)
                    a_part(k)
                n.settle()
            for k in range(PICKS):
                g_step(k, P, PICKS)
                a_part(k, last=True)
            for k in range(PICKS // 2):
                g_step(k, ROWSF, PICKS // 2)

        @block.scalar
        def _(act):
            n = Counter(act)
            act.sem_inc(z_free, 4)
            act.sem_inc(qTp_free, 1)
            act.sem_inc(t_free, 1)
            act.sem_inc(o_free, 1)
            act.wait_ge(eps_ready, n(eps_ready))
            n.settle()

            def head(par, t):
                act.wait_ge(x_in[par], n(x_in[par], 16))
                act.activation(hx[par], hx[par], ACT.Square, accum_out=ss1).then_inc(act_own, 1)
                act.wait_ge(act_own, n(act_own))
                act.activation(rs1, ss1, ACT.Sqrt, scale=1.0 / D, bias=eps).then_inc(sq_ready, 1)
                act.wait_ge(r1_ready, n(r1_ready))
                act.wait_ge(qk_free, n(qk_free))
                for q in range(4):
                    act.wait_ge(z_ready, n(z_ready))
                    dst = [hqk[par][:, 0:512], hqk[par][:, 512:1024], V3[:, t, :], hp[par]][q]
                    act.activation(dst, zbank[q], ACT.Copy, scale=rs1).then_inc(act_own, 1)
                    act.wait_ge(act_own, n(act_own))
                    act.sem_inc(z_free, 1)
                    if isinstance(t, int):
                        act.sem_inc(w_in_free, 1)
                    if q == 1:
                        act.sem_inc(qk_raw, 1)
                    if q == 2:
                        act.wait_ge(ss16_ready, n(ss16_ready))
                        act.activation(rs16, ss16, ACT.Sqrt, scale=1.0 / QK, bias=eps).then_inc(rs16_ready, 1)
                act.sem_inc(p_ready, 1)
                act.sem_inc(v_store, 1)
                act.wait_ge(qTp_ready, n(qTp_ready))
                act.activation(hqp[par][:, 0:512], qTp, ACT.Copy).then_inc(act_own, 1)
                act.wait_ge(act_own, n(act_own))
                act.sem_inc(qTp_free, 1)
                act.sem_inc(qp_store, 1)
                act.wait_ge(dTp_ready, n(dTp_ready))
                act.activation(hdT, dTp, ACT.Copy).then_inc(dT_ready, 1)

            with act.Fori(0, LAST // 2) as j:
                head(0, 2 * j)
                head(1, 2 * j + 1)
                n.settle()
            head(0, LAST)
            n.settle()
            act.wait_ge(lam_ready, n(lam_ready))
            act.activation(lamt[:, 2:4], lamt[:, 0:2], ACT.Exp).then_inc(lam_done, 1)
            act.sem_inc(head_over, 1)
            act.wait_ge(ident_act, n(ident_act))
            n.settle()

            def exps(c, last, first):
                act.wait_ge(nm_ready, n(nm_ready))
                e = [e0, e1][c][:, 0:P if first else KEYS]
                act.activation(e, e, ACT.Exp, scale=-1.0, bias=nm[:, c:c + 1],
                               accum_out=sums[:, c:c + 1]).then_inc(act_own, 1)
                if last:
                    act.activation([ex0, ex1][c], [ex0, ex1][c], ACT.Exp, scale=-1.0, bias=nm[:, c:c + 1],
                                   accum_out=sums[:, 2 + c:3 + c]).then_inc(act_own, 1)
                act.wait_ge(act_own, n(act_own, 2 if last else 1))
                if c == 1:
                    act.sem_inc(exp_ready, 1)

            def evac(dst, src):
                act.wait_ge(t_ready, n(t_ready))
                act.activation(dst, src, ACT.Copy).then_inc(act_own, 1)
                act.wait_ge(act_own, n(act_own))
                act.sem_inc(t_free, 1)
                act.sem_inc(t_evac, 1)

            def a_part(k, last=False, first=False):
                at = Plan
                for h in range(HEADS):
                    for c in at.head(k, at.exp, h):
                        exps(c, last, first)
                    for m in at.head(k, at.evac, h):
                        if h == 0 and m == 0:
                            act.wait_ge(y_stored, n(y_stored))
                        if first:
                            if m == 0:
                                evac(aT[:, 0:P], T[:, 0:P])
                        elif m < 2:
                            evac(aT[:, m * 512:(m + 1) * 512], T[:, :])
                        elif last:
                            evac(exT[0:ROWS8, :], T[0:ROWS8, 0:P])
                if first:
                    for g in range(SEQS // GRP):
                        s = at.sample0 + at.samplew * g
                        if k == s + 9:
                            act.wait_ge(sam_min, n(sam_min))
                            act.activation(Ps, Ps, ACT.Exp, scale=-1.0, bias=snm, accum_out=ssum).then_inc(sam_exp, 1)
                        if k == s + 11:
                            act.wait_ge(t_ready, n(t_ready))
                            act.activation(PT[:, 0:2, :], T[:, 0:2 * P].rearrange("p (k n) -> p k n", k=2),
                                           ACT.Copy).then_inc(act_own, 1)
                            act.activation(PT[0:ROWS8, 2, :], T[0:ROWS8, 2 * P:3 * P], ACT.Copy).then_inc(act_own, 1)
                            act.wait_ge(act_own, n(act_own, 2))
                            act.sem_inc(t_free, 1)
                            act.sem_inc(pt_ready, 1)
                if k == at.att:
                    act.wait_ge(o_ready, n(o_ready))
                    act.activation(att[:, :], O[:, :], ACT.Copy).then_inc(act_own, 1)
                    act.wait_ge(act_own, n(act_own))
                    act.sem_inc(o_free, 1)
                    act.sem_inc(att_raw, 1)
                if k == at.squares + 1:
                    act.wait_ge(ss4_ready, n(ss4_ready))
                    act.activation(rs4, ss4, ACT.Sqrt, scale=1.0 / P, bias=eps).then_inc(rs4_ready, 1)
                if k == at.flip_att + 1:
                    evac(aT[:, 0:512], T[:, :])
                if k == at.flip_x1[0]:
                    act.wait_ge(x1_sq, n(x1_sq))
                    act.activation(e0, x1n, ACT.Square, accum_out=ss2).then_inc(act_own, 1)
                    act.wait_ge(act_own, n(act_own))
                    act.activation(rs2, ss2, ACT.Sqrt, scale=1.0 / D, bias=eps).then_inc(rs2_ready, 1)
                for m in range(2):
                    if k == at.flip_x1[m] + 1:
                        evac(aT[:, m * 512:(m + 1) * 512], T[:, :])
                for q in range(4):
                    if k == at.take[q]:
                        if q == 0:
                            act.wait_ge(r2_ready, n(r2_ready))
                        act.wait_ge(route_ready, n(route_ready))
                        act.activation(work[:, q * 512:(q + 1) * 512], route_bank[q], ACT.Copy, scale=r2)\
                            .then_inc(act_own, 1)
                        act.wait_ge(act_own, n(act_own))
                        act.sem_inc(sc_ready, 1)
                        if q == 3:
                            act.sem_inc(s_free, 1)
                if k == at.gate + 1:
                    act.wait_ge(gexp_in, n(gexp_in))
                    act.activation(gate_n[:, :], gate_n[:, :], ACT.Exp).then_inc(gexp_out, 1)

            def g_step(k, r):
                s = SLOT[k]
                w = P if r == P else ROWS8
                act.wait_ge(dot_ready, n(dot_ready))
                act.activation(gel[0:r, s:s + 1], dots[0:r, s:s + 1], ACT.Gelu).then_inc(act_own, 1)
                act.wait_ge(act_own, n(act_own))
                if k == 0:
                    act.wait_ge(gate_ready, n(gate_ready))
                    act.activation(gate_c[:, :], gate_n[:, :], ACT.Copy).then_inc(act_own, 1)
                    act.wait_ge(act_own, n(act_own))
                    if r < P:
                        act.activation(gate_c[FOLD:ROWSF, 0:PICKS // 2], gate_n[0:ROWS8, PICKS // 2:], ACT.Copy)\
                            .then_inc(act_own, 1)
                        act.wait_ge(act_own, n(act_own))
                act.activation(amp[0:r, s:s + 1], gel[0:r, s:s + 1], ACT.Copy, scale=gate_c[0:r, k:k + 1])\
                    .then_inc(act_own, 1)
                act.wait_ge(act_own, n(act_own))
                act.activation(diag[0:r, s * P:s * P + w], (ident if r == P else fold_id)[0:r, 0:w], ACT.Copy,
                               scale=amp[0:r, s:s + 1]).then_inc(diag_ready, 1)

            for k in range(PICKS):
                a_part(k, first=True)
            n.settle()
            with act.Fori(0, LAST - 1):
                for k in range(PICKS):
                    g_step(k, P)
                    a_part(k)
                n.settle()
            for k in range(PICKS):
                g_step(k, P)
                a_part(k, last=True)
            for k in range(PICKS // 2):
                g_step(k, ROWSF)

        @block.vector
        def _(dve):
            n = Counter(dve)

            dve.memset(eps, EPS).then_inc(dve_own, 1)
            dve.wait_ge(dve_own, n(dve_own))
            dve.sem_inc(eps_ready, 1)
            dve.sem_inc(in_free, 2)
            dve.sem_inc(qk_free, 2)
            dve.sem_inc(kTp_free, 1)
            dve.sem_inc(py_free, 1)
            dve.sem_inc(s_free, 1)
            dve.sem_inc(kv_free, KVBUF)
            dve.sem_inc(y_stored, 1)
            dve.sem_inc(slot_free[0], 1)
            dve.sem_inc(slot_free[1], 1)
            dve.sem_inc(x1n_free, 1)
            dve.wait_ge(c_dve, n(c_dve, 10 * 16))
            for i in range(2):
                dve.tensor_tensor_reduce(out=att[:, i * 128:i * 128 + QK], in0=att[:, i * 128:i * 128 + QK],
                                         in1=att[:, i * 128 + QK:(i + 1) * 128], scale=1.0, scalar=0.0,
                                         op0=ALU.mult, op1=ALU.add, accum_out=lamt[:, i:i + 1]).then_inc(dve_own, 1)
                dve.wait_ge(dve_own, n(dve_own))
            dve.sem_inc(lam_ready, 1)
            dve.sem_inc(a_over, 1)
            n.settle()

            def head(par, t):
                dve.wait_ge(sq_ready, n(sq_ready))
                dve.reciprocal(rs1, rs1).then_inc(r1_ready, 1)
                dve.wait_ge(qk_raw, n(qk_raw))
                qk = hqk[par]
                qk3 = qk.rearrange("p (g n) -> p g n", g=16)
                dve.tensor_tensor(hsq, qk, qk, ALU.mult).then_inc(dve_own, 1)
                dve.wait_ge(dve_own, n(dve_own))
                dve.tensor_reduce(ss16, hsq.rearrange("p (g n) -> p g n", g=16), AX.X, ALU.add).then_inc(ss16_ready, 1)
                dve.wait_ge(rs16_ready, n(rs16_ready))
                dve.reciprocal(rs16, rs16).then_inc(dve_own, 1)
                dve.wait_ge(dve_own, n(dve_own))
                dve.tensor_tensor(qk3, qk3, rs16.unsqueeze(2).to_broadcast([P, 16, QK]), ALU.mult)\
                    .then_inc(dve_own, 1)
                dve.wait_ge(dve_own, n(dve_own))
                dve.tensor_tensor(qk, qk, hgqk, ALU.mult).then_inc(dve_own, 1)
                dve.wait_ge(dve_own, n(dve_own))
                dve.wait_ge(cs_in[par], n(cs_in[par], 16))
                a, b = qk3[:, :, 0:HALF], qk3[:, :, HALF:ROPE]
                cos = hcs[par][:, 0:HALF].unsqueeze(1).to_broadcast([P, 16, HALF])
                sin = hcs[par][:, HALF:ROPE].unsqueeze(1).to_broadcast([P, 16, HALF])
                tmp = [hrope[:, i * 128:(i + 1) * 128].rearrange("p (g n) -> p g n", g=16) for i in range(4)]
                for to, u, w in zip(tmp, (a, b, b, a), (cos, sin, cos, sin)):
                    dve.tensor_tensor(to, u, w, ALU.mult).then_inc(dve_own, 1)
                dve.wait_ge(dve_own, n(dve_own, 4))
                dve.tensor_tensor(a, tmp[0], tmp[1], ALU.subtract).then_inc(dve_own, 1)
                dve.tensor_tensor(b, tmp[2], tmp[3], ALU.add).then_inc(dve_own, 1)
                dve.wait_ge(dve_own, n(dve_own, 2))
                dve.sem_inc(qk_ready, 1)
                dve.sem_inc(k_store, 1)
                dve.wait_ge(kTp_ready, n(kTp_ready))
                w = P if not isinstance(t, int) or t < LAST else ROWS8
                dve.tensor_copy(KT3[:, :, bass.ds(t * P, w)],
                                kTp.rearrange("p (h n) -> p h n", h=HEADS)[:, :, 0:w]).then_inc(dve_own, 1)
                dve.wait_ge(dve_own, n(dve_own))
                dve.sem_inc(kTp_free, 1)
                dve.wait_ge(py_ready, n(py_ready))
                for g in range(4):
                    dve.tensor_scalar(hqp[par][:, 512 + g * P:512 + (g + 1) * P], pyp[:, g * P:(g + 1) * P],
                                      bpT[:, g:g + 1], scT[:, g:g + 1], ALU.add, ALU.mult).then_inc(dve_own, 1)
                dve.wait_ge(dve_own, n(dve_own, 4))
                dve.sem_inc(py_free, 1)
                dve.sem_inc(in_free, 1)
                dve.sem_inc(qp_store, 1)

            with dve.Fori(0, LAST // 2) as j:
                head(0, 2 * j)
                head(1, 2 * j + 1)
                n.settle()
            head(0, LAST)
            dve.wait_ge(head_over, n(head_over, 4))
            dve.sem_inc(fold_free, 2)
            for j in range(GROUPS):
                dve.wait_ge(fold_ready, n(fold_ready))
                dve.tensor_tensor(w_route[:, :, j * P:(j + 1) * P],
                                  S[j % 2][:, :].rearrange("p (c n) -> p c n", c=DC),
                                  g2c.unsqueeze(2).to_broadcast([P, DC, P]), ALU.mult).then_inc(dve_own, 1)
                dve.wait_ge(dve_own, n(dve_own))
                dve.sem_inc(fold_free, 1)
                if j % (GROUPS // 2) == GROUPS // 2 - 1:
                    dve.sem_inc(folded, 1)
            dve.sem_inc(route_w, 1)
            dve.wait_ge(lam_done, n(lam_done))
            dve.tensor_tensor(lamt[:, 0:1], lamt[:, 3:4], lamt[:, 2:3], ALU.subtract).then_inc(dve_own, 1)
            dve.wait_ge(dve_own, n(dve_own))
            dve.tensor_scalar(coef[:, 1:2], lamt[:, 0:1], -LAM_INIT, None, ALU.add).then_inc(dve_own, 1)
            dve.wait_ge(dve_own, n(dve_own))
            dve.memset(coef[:, 0:1], 1.0).then_inc(dve_own, 1)
            dve.tensor_copy(coef[:, 2:3], r01[:, 0:1]).then_inc(dve_own, 1)
            dve.tensor_tensor(coef[:, 3:4], coef[:, 1:2], r01[:, 0:1], ALU.mult).then_inc(dve_own, 1)
            dve.scalar_tensor_tensor(scoef, r01[:, 2:3], coef[:, 1:2], r01[:, 1:2], ALU.mult, ALU.add)\
                .then_inc(dve_own, 1)
            dve.wait_ge(dve_own, n(dve_own, 4))
            dve.wait_ge(wo_in, n(wo_in, 16))
            for c in range(HEADS):
                dve.tensor_scalar(w_out_sb[:, c, :], w_out_sb[:, c, :], subc, 1.0 - LAM_INIT, ALU.mult, ALU.mult)\
                    .then_inc(dve_own, 1)
            dve.wait_ge(dve_own, n(dve_own, HEADS))
            dve.sem_inc(wo_ready, 1)
            n.settle()

            def scale_mask(h, c, last, first):
                if c == 0:
                    if h == 0:
                        dve.wait_ge(mask_in, n(mask_in, 16))
                    else:
                        dve.wait_ge(a_used, n(a_used))
                dve.wait_ge(s_ready, n(s_ready))
                low = nmx if last else nm
                w = slice(0, P if first else KEYS)
                dve.tensor_tensor_reduce(out=[e0, e1][c][:, w], in0=S[c][:, w], in1=mask_sb[:, w], scale=-(QK ** -0.5),
                                         scalar=3e38, op0=ALU.add, op1=ALU.min,
                                         accum_out=low[:, c:c + 1]).then_inc(dve_own, 1)
                if last:
                    dve.tensor_tensor_reduce(out=[ex0, ex1][c], in0=T[:, c * ROWS8:(c + 1) * ROWS8], in1=emask[:, :],
                                             scale=-(QK ** -0.5), scalar=3e38, op0=ALU.add, op1=ALU.min,
                                             accum_out=nmx[:, 2 + c:3 + c]).then_inc(dve_own, 1)
                    dve.wait_ge(dve_own, n(dve_own, 2))
                    dve.tensor_tensor(nm[:, c:c + 1], nmx[:, c:c + 1], nmx[:, 2 + c:3 + c], ALU.min).then_inc(dve_own, 1)
                dve.wait_ge(dve_own, n(dve_own))
                dve.sem_inc(nm_ready, 1)
                if c == 1:
                    dve.sem_inc(s_free, 1)
                    if last:
                        dve.sem_inc(t_free, 1)

            def combine(part, last, first):
                w = slice(0, P if first else KEYS)
                if part == 0:
                    dve.wait_ge(exp_ready, n(exp_ready))
                    if last:
                        dve.tensor_tensor(sums[:, 0:2], sums[:, 0:2], sums[:, 2:4], ALU.add).then_inc(dve_own, 1)
                        dve.wait_ge(dve_own, n(dve_own))
                    dve.reciprocal(rc, sums[:, 0:2]).then_inc(dve_own, 1)
                    dve.wait_ge(dve_own, n(dve_own))
                    dve.tensor_tensor(rc, rc, coef[:, 2:4] if last else coef[:, 0:2], ALU.mult).then_inc(dve_own, 1)
                    dve.wait_ge(dve_own, n(dve_own))
                    dve.tensor_scalar(e1[:, w], e1[:, w], rc[:, 1:2], None, ALU.mult).then_inc(dve_own, 1)
                    if last:
                        dve.tensor_scalar(ex1, ex1, rc[:, 1:2], None, ALU.mult).then_inc(dve_own, 1)
                    dve.wait_ge(dve_own, n(dve_own, 2 if last else 1))
                else:
                    dve.scalar_tensor_tensor(e0[:, w], e0[:, w], rc[:, 0:1], e1[:, w], ALU.mult, ALU.add).then_inc(dve_own, 1)
                    if last:
                        dve.scalar_tensor_tensor(ex0, ex0, rc[:, 0:1], ex1, ALU.mult, ALU.add).then_inc(dve_own, 1)
                    dve.wait_ge(dve_own, n(dve_own, 2 if last else 1))
                    dve.sem_inc(a_ready, 1)

            def sample(k, g, s):
                for i in range(GRP):
                    b = GRP * g + i
                    if k == s + 2 * i:
                        if b == 0:
                            dve.wait_ge(sam_in, n(sam_in, 16 * (SEQS // GRP + 1)))
                            dve.memset(QZ, 0.0).then_inc(dve_own, 1)
                            dve.memset(AZ, 0.0).then_inc(dve_own, 1)
                            dve.wait_ge(dve_own, n(dve_own, 2))
                        if i > 0:
                            dve.wait_ge(qz_free, n(qz_free))
                            dve.sem_inc(kv_free, 1)
                        for c in range(2):
                            r = slice(QK * c, QK * c + QK)
                            dve.tensor_copy(QZ[r, P:].rearrange("p (h n) -> p h n", h=HEADS)[:, :, c * NEW:(c + 1) * NEW],
                                            sam_q[r, :, TAIL + NEW * b:TAIL + NEW * (b + 1)]).then_inc(dve_own, 1)
                        dve.wait_ge(dve_own, n(dve_own, 2))
                        dve.sem_inc(qz_ready, 1)
                if k == s + 8:
                    dve.wait_ge(qz_free, n(qz_free))
                    dve.sem_inc(kv_free, 1)
                    dve.tensor_tensor_reduce(out=Ps, in0=sam_s, in1=msam_sb[g], scale=-(QK ** -0.5), scalar=3e38,
                                             op0=ALU.add, op1=ALU.min, accum_out=snm).then_inc(dve_own, 1)
                    dve.wait_ge(dve_own, n(dve_own))
                    dve.sem_inc(sam_min, 1)
                if k == s + 10:
                    dve.wait_ge(sam_exp, n(sam_exp))
                    dve.reciprocal(src, ssum).then_inc(dve_own, 1)
                    dve.wait_ge(dve_own, n(dve_own))
                    dve.tensor_tensor(src, src, scoef, ALU.mult).then_inc(dve_own, 1)
                    dve.wait_ge(dve_own, n(dve_own))
                    dve.tensor_scalar(Ps, Ps, src, None, ALU.mult).then_inc(sam_a, 1)
                for i in range(GRP):
                    b = GRP * g + i
                    if k == s + 12 + 2 * i:
                        if i == 0:
                            dve.wait_ge(pt_ready, n(pt_ready))
                        else:
                            dve.wait_ge(qz_free, n(qz_free))
                            dve.sem_inc(kv_free, 1)
                        for kind in range(PAGES + 1):
                            r = slice(0, P if kind < PAGES else ROWS8)
                            src4 = PT[r, kind, i * 32:(i + 1) * 32].rearrange("p (h n) -> p h n", h=HEADS)
                            to = AZ[r, P + P * HEADS * kind:P + P * HEADS * (kind + 1)]\
                                .rearrange("p (h n) -> p h n", h=HEADS)[:, :, 0:NEW]
                            dve.tensor_tensor(to, src4[:, :, 0:NEW], src4[:, :, NEW:2 * NEW], ALU.add)\
                                .then_inc(dve_own, 1)
                        dve.wait_ge(dve_own, n(dve_own, PAGES + 1))
                        dve.sem_inc(qz_ready, 1)
                if k == s + 19:
                    dve.wait_ge(qz_free, n(qz_free))
                    dve.sem_inc(kv_free, 1)

            def sample_out():
                dve.tensor_copy(sam_o, sam_y).then_inc(dve_own, 1)
                dve.wait_ge(dve_own, n(dve_own))
                dve.sem_inc(sam_store, 1)
                dve.sem_inc(y_free, 1)
                for s in range(2, SLOTS):
                    dve.sem_inc(slot_free[s], 1)

            def top16(values, indices, source, which, lo):
                m = len(which)
                for g in which:
                    dve.max(values[:, g, lo:lo + 8], source[:, g, :]).then_inc(dve_own, 1)
                dve.wait_ge(dve_own, n(dve_own, m))
                for g in which:
                    dve.max_index(indices[:, g, lo:lo + 8], values[:, g, lo:lo + 8], source[:, g, :])\
                        .then_inc(dve_own, 1)
                dve.wait_ge(dve_own, n(dve_own, m))
                if lo == 0:
                    for g in which:
                        dve.match_replace(source[:, g, :], values[:, g, lo:lo + 8], source[:, g, :], -3e38)\
                            .then_inc(dve_own, 1)
                    dve.wait_ge(dve_own, n(dve_own, m))

            def lookup(pick, pos, half, q):
                hs, ks = slice(2 * q, 2 * q + 2), slice(2 * TOPK * q, 2 * TOPK * (q + 1))
                shape = [P, 2, TOPK, TOPK]
                dve.tensor_tensor(onehot[:, hs], pos[:, ks].rearrange("p (h k) -> p h k", h=2).unsqueeze(3)
                                  .to_broadcast(shape),
                                  iota16[:, :].unsqueeze(1).unsqueeze(1).to_broadcast(shape),
                                  ALU.is_equal).then_inc(dve_own, 1)
                dve.wait_ge(dve_own, n(dve_own))
                keys = sif.rearrange("p (h c) k -> p h c k", c=2)[:, hs, half, :]
                dve.tensor_tensor(onehot[:, hs], onehot[:, hs], keys.unsqueeze(2).to_broadcast(shape), ALU.mult)\
                    .then_inc(dve_own, 1)
                dve.wait_ge(dve_own, n(dve_own))
                dve.tensor_reduce(pick[:, ks], work[:, 512 * q:512 * (q + 1)].rearrange("p (m j) -> p m j", j=TOPK),
                                  AX.X, ALU.add).then_inc(dve_own, 1)
                dve.wait_ge(dve_own, n(dve_own))

            def top_part(q, u):
                h0, g0 = 2 * q, 4 * q
                ks = slice(2 * TOPK * q, 2 * TOPK * (q + 1))
                if u == 0:
                    dve.wait_ge(sc_ready, n(sc_ready))
                if u < 4:
                    g = g0 + u // 2 * 2
                    top16(sv, si, scores, (g, g + 1), 8 * (u % 2))
                if u == 4:
                    dve.tensor_copy(sif[:, g0:g0 + 4, :], si[:, g0:g0 + 4, :]).then_inc(dve_own, 1)
                    sv4 = sv.rearrange("p (h c) k -> p h c k", c=2)[:, h0:h0 + 2]
                    shape = [P, 2, TOPK, TOPK]
                    dve.tensor_tensor(cand[:, h0:h0 + 2].rearrange("p h (a b) -> p h a b", a=TOPK),
                                      sv4[:, :, 0, :].unsqueeze(3).to_broadcast(shape),
                                      sv4[:, :, 1, :].unsqueeze(2).to_broadcast(shape), ALU.add).then_inc(dve_own, 1)
                    dve.wait_ge(dve_own, n(dve_own, 2))
                if u == 5 or u == 6:
                    top16(tv, tpos, cand, (h0 + u - 5,), 0)
                if u == 7:
                    top16(tv, tpos, cand, (h0, h0 + 1), 8)
                if u == 8:
                    tp = qpw[:, 896:1024].bitcast(U32)[:, ks]
                    tmp = idx_n[:, ks].bitcast(U32)
                    for op, by, to in ((ALU.logical_shift_right, 4, posa), (ALU.bitwise_and, TOPK - 1, posb)):
                        dve.tensor_scalar(tmp, tp, by, None, op).then_inc(dve_own, 1)
                        dve.wait_ge(dve_own, n(dve_own))
                        dve.tensor_copy(to[:, ks], tmp).then_inc(dve_own, 1)
                        dve.wait_ge(dve_own, n(dve_own))
                    lookup(pick1, posa, 0, q)
                if u == 9:
                    lookup(pick2, posb, 1, q)
                    dve.scalar_tensor_tensor(pick1[:, ks], pick1[:, ks], float(NK), pick2[:, ks], ALU.mult, ALU.add)\
                        .then_inc(dve_own, 1)
                    dve.wait_ge(dve_own, n(dve_own))
                    dve.tensor_copy(idx_n[:, ks], pick1[:, ks]).then_inc(dve_own, 1)
                    dve.wait_ge(dve_own, n(dve_own))

            def a_part(k, last=False, first=False):
                at = Plan
                for h in range(HEADS):
                    for c in at.head(k, at.scale, h):
                        scale_mask(h, c, last, first)
                    for part in at.head(k, at.combine, h):
                        combine(part, last, first)
                        if last and h == HEADS - 1 and part == 1:
                            dve.sem_inc(add_free, 1)
                if first:
                    for g in range(SEQS // GRP):
                        sample(k, g, at.sample0 + at.samplew * g)
                    if k == at.sample_out:
                        sample_out()
                if k == at.squares:
                    dve.wait_ge(a_used, n(a_used))
                    dve.wait_ge(att_raw, n(att_raw))
                    if last:
                        dve.wait_ge(add_in, n(add_in, 16))
                        dve.tensor_tensor(att[:, :], att[:, :], add_o, ALU.add).then_inc(dve_own, 1)
                        dve.wait_ge(dve_own, n(dve_own))
                    dve.tensor_tensor(e1[:, 0:ATT], att[:, :], att[:, :], ALU.mult).then_inc(dve_own, 1)
                    dve.wait_ge(dve_own, n(dve_own))
                    dve.tensor_reduce(ss4, e1[:, 0:ATT].rearrange("p (h n) -> p h n", h=HEADS), AX.X, ALU.add)\
                        .then_inc(ss4_ready, 1)
                if k == at.norm:
                    dve.wait_ge(rs4_ready, n(rs4_ready))
                    dve.reciprocal(rs4, rs4).then_inc(dve_own, 1)
                    dve.wait_ge(dve_own, n(dve_own))
                    a3 = att[:, :].rearrange("p (h n) -> p h n", h=HEADS)
                    dve.tensor_tensor(a3, a3, rs4.unsqueeze(2).to_broadcast([P, HEADS, P]), ALU.mult)\
                        .then_inc(att_ready, 1)
                if k == at.x1:
                    dve.wait_ge(x1_in, n(x1_in, 16))
                    dve.wait_ge(proj_ready, n(proj_ready))
                    dve.tensor_tensor(x1n, x1n, S0[:, :], ALU.add).then_inc(dve_own, 1)
                    dve.wait_ge(dve_own, n(dve_own))
                    dve.sem_inc(s_free, 1)
                    dve.sem_inc(x1_ready, 1)
                    dve.sem_inc(x1_sq, 1)
                if k == at.r2:
                    dve.wait_ge(rs2_ready, n(rs2_ready))
                    dve.reciprocal(r2, rs2).then_inc(dve_own, 1)
                    dve.wait_ge(dve_own, n(dve_own))
                    dve.sem_inc(r2_ready, 1)
                if at.top <= k < at.top + 4 * TOPU:
                    top_part(*divmod(k - at.top, TOPU))
                g3 = gate_n[:, :].rearrange("p (h k) -> p h k", h=PH)
                if k == at.gate:
                    dve.tensor_tensor(g3, tv, tv[:, :, 0:1].to_broadcast([P, PH, TOPK]), ALU.subtract)\
                        .then_inc(dve_own, 1)
                    dve.wait_ge(dve_own, n(dve_own))
                    dve.sem_inc(gexp_in, 1)
                if k == at.gate + 2:
                    dve.wait_ge(gexp_out, n(gexp_out))
                    dve.tensor_reduce(gsum, g3, AX.X, ALU.add).then_inc(dve_own, 1)
                    dve.wait_ge(dve_own, n(dve_own))
                    dve.reciprocal(grec, gsum).then_inc(dve_own, 1)
                    dve.wait_ge(dve_own, n(dve_own))
                    dve.tensor_tensor(g3, g3, grec.unsqueeze(2).to_broadcast([P, PH, TOPK]), ALU.mult)\
                        .then_inc(dve_own, 1)
                    dve.wait_ge(dve_own, n(dve_own))
                    dve.sem_inc(a_over, 1)

            def promote_lo(last=False):
                half = slice(0, PICKS // 2)
                dve.tensor_copy(idx_c[:, half], idx_n[:, half]).then_inc(dve_own, 1)
                dve.wait_ge(dve_own, n(dve_own))
                if last:
                    dve.tensor_copy(idx_c[FOLD:ROWSF, half], idx_n[0:ROWS8, PICKS // 2:]).then_inc(dve_own, 1)
                    dve.wait_ge(dve_own, n(dve_own))
                dve.sem_inc(idx_lo, 1)

            def promote(last=False):
                if not last:
                    dve.tensor_copy(idx_c[:, PICKS // 2:], idx_n[:, PICKS // 2:]).then_inc(dve_own, 1)
                    dve.wait_ge(dve_own, n(dve_own))
                    dve.sem_inc(idx_hi, 1)
                dve.scalar_tensor_tensor(h2c[:, :], x1n, r2, g2w[:, :], ALU.mult, ALU.mult).then_inc(dve_own, 1)
                dve.wait_ge(dve_own, n(dve_own))
                if last:
                    dve.tensor_copy(h2c[FOLD:ROWSF, :], h2c[0:ROWS8, :]).then_inc(dve_own, 1)
                    dve.wait_ge(dve_own, n(dve_own))
                dve.sem_inc(gate_ready, 1)

            def g_step(t, k, r):
                s = SLOT[k]
                dve.wait_ge(landed[s], t * (16 * SLOT.count(s)) + 16 * USE[k])
                dot = dve.tensor_tensor_reduce(out=ring[s][0:r, 0:D], in0=ring[s][0:r, 0:D], in1=h2c[0:r, :],
                                               scale=1.0, scalar=0.0, op0=ALU.mult, op1=ALU.add,
                                               accum_out=dots[0:r, s:s + 1])
                if k < PICKS - 1:
                    dot.then_inc(dot_ready, 1)
                else:
                    dot.then_inc(dve_own, 1)
                    dve.wait_ge(dve_own, n(dve_own))
                    dve.sem_inc(dot_ready, 1)

            def finish(r, last_slot):
                dve.wait_ge(y_ready, n(y_ready))
                dve.sem_inc(slot_free[last_slot], 1)
                dve.tensor_copy((aT if r == P else e0)[0:r, :], Y[0:r, :]).then_inc(dve_own, 1)
                dve.wait_ge(dve_own, n(dve_own))
                dve.sem_inc(y_free, 1)
                dve.sem_inc(y_store, 1)

            def g_rest(t, last):
                for k in range(EARLY, PICKS):
                    g_step(t, k, P)
                    if k == Plan.x1n_free:
                        dve.wait_ge(x1n_read, n(x1n_read))
                        dve.sem_inc(x1n_free, 1)
                    a_part(k, last)
                    if k == Plan.promote:
                        promote_lo(last)

            def turn(t, last):
                promote(last)
                for k in range(EARLY):
                    g_step(t, k, ROWSF if last else P)
                finish(P, SLOT[PICKS - 1])

            for k in range(PICKS):
                a_part(k, first=True)
                if k == Plan.gate:
                    promote_lo()
            promote()
            for k in range(EARLY):
                g_step(0, k, P)
            n.settle()
            with dve.Fori(0, LAST - 1) as t:
                g_rest(t, False)
                turn(t + 1, False)
                n.settle()
            g_rest(LAST - 1, True)
            turn(LAST, True)
            for k in range(EARLY, PICKS // 2):
                g_step(LAST, k, ROWSF)
            finish(ROWS8, SLOT[PICKS // 2 - 1])


def rotary_table():
    pos = np.zeros(TILES * P)
    pos[:META + SEQ] = np.arange(META + SEQ)
    pos[META + SEQ:LAST * P + ROWS8] = PAST + np.arange(SEQS * NEW) % NEW
    inv = (np.float32(500000.0) ** (-np.arange(0, ROPE, 2, dtype=np.float32) / ROPE)).astype(np.float32)
    ang = (pos.astype(np.float32)[:, None] * inv[None, :]).astype(np.float64)
    return np.concatenate([np.cos(ang), np.sin(ang)], 1).astype(np.float32).reshape(TILES, P, ROPE)


def pool_tables():
    cur = np.zeros((TILES, P, 2, 4, P), np.float32)
    old = np.zeros((SEQS, STATE, 4, P), np.float32)
    for g, w in enumerate(WINDOWS):
        for t in range(TILES):
            for p in range(P if t < LAST else TAIL):
                pos = t * P + p
                for q in range(max(0, pos - w + 1), pos + 1):
                    cur[t, q % P, 0 if q // P == t else 1, g, p] += np.float32(1.0) / np.float32(min(pos + 1, w))
                cur[t, p, 0, g, p] -= 1
        for b in range(SEQS):
            for s in range(NEW):
                p = TAIL + NEW * b + s
                for q in range(s - w + 1, s + 1):
                    if q >= 0:
                        cur[LAST, TAIL + NEW * b + q, 0, g, p] += 1.0 / w
                    else:
                        old[b, STATE + q, g, p] += 1.0 / w
                cur[LAST, p, 0, g, p] -= 1
    return cur.reshape(TILES, P, 1024), old.reshape(SEQS * STATE, 512)


def masks(bf16):
    full = np.full((TILES, P, KEYS), NEG, np.float32)
    for t in range(TILES):
        for p in range(P):
            full[t, p, :t * P + p + 1] = 0
    extra = np.full((P, ROWS8), NEG, np.float32)
    for p in range(TAIL):
        extra[p, :p + 1] = 0
    sample = np.full((SEQS // GRP, P, SW), NEG, np.float32)
    sample[:, :, :PAST] = 0
    for g in range(SEQS // GRP):
        for r in range(P):
            b, s = GRP * g + r // 32, r % NEW
            lo = PAST + TAIL + NEW * b
            sample[g, r, lo:lo + s + 1] = 0
    return full.astype(bf16), extra, sample


def kernel(x_prompt, x_sample, cache_k, cache_v, state_pool, page_table, meta_tokens, norm1_g, w_in,
           q_norm_g, k_norm_g, lambda_q1, lambda_k1, lambda_q2, lambda_k2, subln_g, w_pool, b_pool,
           pool_scale, w_out, norm2_g, w_query, sub_keys, w_u, w_v):
    import ml_dtypes
    import concourse.bacc as bacc
    from concourse.bass_utils import run_bass_kernel_spmd

    a = {k: np.asarray(v) for k, v in dict(
        x_prompt=x_prompt, x_sample=x_sample, cache_k=cache_k, cache_v=cache_v, state_pool=state_pool,
        page_table=page_table, meta_tokens=meta_tokens, norm1_g=norm1_g, w_in=w_in, q_norm_g=q_norm_g,
        k_norm_g=k_norm_g, lambda_q1=lambda_q1, lambda_k1=lambda_k1, lambda_q2=lambda_q2,
        lambda_k2=lambda_k2, subln_g=subln_g, w_pool=w_pool, b_pool=b_pool, pool_scale=pool_scale,
        w_out=w_out, norm2_g=norm2_g, w_query=w_query, sub_keys=sub_keys, w_u=w_u, w_v=w_v).items()}

    def wide(row):
        return np.broadcast_to(row.reshape(1, -1), (P, row.size))

    x = np.zeros((TILES * P, D), np.float32)
    x[:META] = a["meta_tokens"]
    x[META:META + SEQ] = a["x_prompt"][0]
    x[META + SEQ:LAST * P + ROWS8] = a["x_sample"].reshape(-1, D)
    x = x.reshape(TILES, P, D)
    mt, mst = pool_tables()
    mask, mext, msam = masks(ml_dtypes.bfloat16)
    rows01 = np.zeros((P, 3), np.float32)
    rows01[:TAIL, 0] = 1
    comp = np.arange(P) // NEW % 2
    rows01[:, 1], rows01[:, 2] = comp == 0, comp == 1
    n_pool = a["cache_k"].shape[1]
    ins = dict(
        x=x,
        xT=x.reshape(TILES, P, DC, P).transpose(0, 3, 2, 1).reshape(TILES, P, D),
        g1T=a["norm1_g"].reshape(DC, P).T,
        w_in=a["w_in"][0].reshape(DC, P, INW),
        gqk=np.concatenate([wide(np.tile(a["q_norm_g"], 8)), wide(np.tile(a["k_norm_g"], 8))], 1),
        cs=rotary_table(), mt=mt, mst=mst,
        state=a["state_pool"][0].reshape(SEQS * STATE, 512),
        w_pool=a["w_pool"][0].transpose(1, 0, 2).reshape(P, 512),
        b_poolT=a["b_pool"][0].T, scaleT=a["pool_scale"].reshape(4, P).T,
        wqT=a["w_query"][0].T.reshape(GROUPS, P, D),
        skT=a["sub_keys"][0].reshape(GROUPS, NK, P).transpose(2, 0, 1),
        g2T=a["norm2_g"].reshape(DC, P).T, g2b=wide(a["norm2_g"]),
        lams=np.concatenate([wide(a[k]) for k in ("lambda_q1", "lambda_k1", "lambda_q2", "lambda_k2")], 1),
        rows01=rows01, w_out=a["w_out"][0], subT=a["subln_g"].reshape(P, 1),
        mask=mask, mext=mext, msam=msam,
        ktc=a["cache_k"][0].transpose(0, 3, 2, 1).reshape(n_pool, P, HEADS * PAGE),
        vc=a["cache_v"][0].reshape(n_pool, PAGE, HEADS * P),
        pages=a["page_table"].reshape(1, -1),
        wuv=np.concatenate([a["w_u"][0], a["w_v"][0]], 1),
        iota=wide(np.arange(TOPK, dtype=np.float32)),
    )
    outs = dict(y_all=(TILES, P, D), k_all=(TILES, P, 512), v_all=(TILES, P, 512), p_last=(ROWS8, 512),
                state_old=(SEQS, STATE - NEW, 512))
    nc = bacc.Bacc("TRN2", target_bir_lowering=False, num_devices=1)
    args, arrays = [], {}
    for name, v in ins.items():
        arrays["in_" + name] = v = np.ascontiguousarray(v)
        args.append(nc.dram_tensor("in_" + name, v.shape, mybir.dt.from_np(v.dtype), kind="ExternalInput").ap())
    for name, shape in outs.items():
        args.append(nc.dram_tensor("out_" + name, shape, F32, kind="ExternalOutput").ap())
    build(nc, *args)
    res = run_bass_kernel_spmd(nc, [arrays], core_ids=[0]).results[0]
    y, k, v = (res["out_" + m].reshape(TILES * P, -1) for m in ("y_all", "k_all", "v_all"))
    p_new = res["out_p_last"]
    n_p, n_all = META + SEQ, LAST * P + ROWS8
    return (y[META:n_p].reshape(1, SEQ, D), y[n_p:n_all].reshape(SEQS, NEW, D),
            k[:n_p].reshape(1, 1, n_p, HEADS, P), v[:n_p].reshape(1, 1, n_p, HEADS, P),
            p_new[TAIL - STATE:TAIL].reshape(1, 1, STATE, 512),
            k[n_p:n_all].reshape(1, SEQS, NEW, HEADS, P), v[n_p:n_all].reshape(1, SEQS, NEW, HEADS, P),
            np.concatenate([res["out_state_old"], p_new[TAIL:].reshape(SEQS, NEW, 512)], 1)[None])
```
